# Optimizing a Trainium2 kernel written in Bass

```python
import jax
import jax.numpy as jnp
from jax import lax
import numpy as np
import math
import jax, jax.numpy as jnp

D_MODEL = 1024
BATCH = 1
SEQ = 512
DEPTH = 2

CHUNK = 64
Q_BLOCK = 128
N_HEADS = 4
HEAD_DIM = 128
BRANCH_W = N_HEADS * HEAD_DIM
RET_DK = HEAD_DIM
RET_DV = HEAD_DIM
GLA_DK = HEAD_DIM // 2
GLA_DV = HEAD_DIM
GLA_LOWRANK = 16
GLA_TAU = 16.0
FOX_D = HEAD_DIM
N_BRANCH = 3
D_FF = 2816
CONV_W = 3
ROPE_BASE = 10000.0
EPS = 1e-6

IN_SPLITS = (
    N_HEADS * RET_DK, N_HEADS * RET_DK, N_HEADS * RET_DV, N_HEADS * RET_DV,
    N_HEADS * GLA_DK, N_HEADS * GLA_DK, N_HEADS * GLA_DV, GLA_LOWRANK, N_HEADS * GLA_DV,
    N_HEADS * FOX_D, N_HEADS * FOX_D, N_HEADS * FOX_D, N_HEADS,
)
IN_W = sum(IN_SPLITS)


F32 = jnp.float32

def rms_norm(x, g):
    xf = x.astype(F32)
    y = xf * lax.rsqrt(jnp.mean(xf * xf, axis=-1, keepdims=True) + EPS)
    return (y * g).astype(x.dtype)

def head_group_norm(x, g):
    xf = x.astype(F32)
    mu = jnp.mean(xf, axis=-1, keepdims=True)
    xc = xf - mu
    return xc * lax.rsqrt(jnp.mean(xc * xc, axis=-1, keepdims=True) + EPS) * g

def modulate(h, shift, scale):
    return h * (1.0 + scale[:, None, :]) + shift[:, None, :]

def rotary(x, pos):
    half = x.shape[-1] // 2
    inv_freq = ROPE_BASE ** (-jnp.arange(half, dtype=F32) / half)
    ang = pos[:, None] * inv_freq[None, :]
    cos = jnp.cos(ang)[None, :, None, :]
    sin = jnp.sin(ang)[None, :, None, :]
    x1, x2 = x[..., :half], x[..., half:]
    return jnp.concatenate([x1 * cos - x2 * sin, x1 * sin + x2 * cos], axis=-1)

def retention(q, k, v):
    b, s, h, dk = q.shape
    dv = v.shape[-1]
    n = s // CHUNK
    pos = jnp.arange(s, dtype=F32)
    q = rotary(q.astype(F32), pos)
    k = rotary(k.astype(F32), pos) * dk ** -0.5
    v = v.astype(F32)
    log_g = jnp.log1p(-jnp.exp2(-5.0 - jnp.arange(h, dtype=F32)))
    idx = jnp.arange(CHUNK, dtype=F32)
    d_intra = jnp.exp(jnp.abs(idx[:, None] - idx[None, :])[None] * log_g[:, None, None])
    qc = q.reshape(b, n, CHUNK, h, dk)
    kc = k.reshape(b, n, CHUNK, h, dk)
    vc = v.reshape(b, n, CHUNK, h, dv)
    scores = jnp.einsum('bnihd,bnjhd->bnhij', qc, kc) * d_intra
    o_intra = jnp.einsum('bnhij,bnjhe->bnihe', scores, vc)
    k_w = jnp.exp((CHUNK - 1.0 - idx)[:, None] * log_g[None, :])
    kv = jnp.einsum('bnjhd,bnjhe->nbhde', kc * k_w[:, :, None], vc)
    g_chunk = jnp.exp(CHUNK * log_g)[None, :, None, None]

    def step(r, kv_n):
        return g_chunk * r + kv_n, r

    _, r_prev = lax.scan(step, jnp.zeros((b, h, dk, dv), F32), kv)
    q_w = jnp.exp((idx + 1.0)[:, None] * log_g[None, :])
    o_cross = jnp.einsum('bnihd,nbhde->bnihe', qc * q_w[:, :, None], r_prev)
    return (o_intra + o_cross).reshape(b, s, h, dv)

def gla(q, k, v, log_a):
    b, s, h, dk = q.shape
    dv = v.shape[-1]
    n = s // CHUNK
    qc = (q.astype(F32) * dk ** -0.5).reshape(b, n, CHUNK, h, dk)
    kc = k.astype(F32).reshape(b, n, CHUNK, h, dk)
    vc = v.astype(F32).reshape(b, n, CHUNK, h, dv)
    la = log_a.astype(F32).reshape(b, n, CHUNK, h, dk)
    b_cum = jnp.cumsum(la, axis=2)
    b_end = b_cum[:, :, -1:]
    kv = jnp.einsum('bnjhd,bnjhe->nbhde', kc * jnp.exp(b_end - b_cum), vc)
    a = jnp.exp(b_end[:, :, 0]).transpose(1, 0, 2, 3)

    def step(st, inp):
        a_n, kv_n = inp
        st = a_n[..., None] * st + kv_n
        return st, st

    _, s_all = lax.scan(step, jnp.zeros((b, h, dk, dv), F32), (a, kv))
    o = jnp.einsum('bnihd,nbhde->bnihe', qc, s_all)
    return o.reshape(b, s, h, dv)

def forgetting_attention(q, k, v, f_logit):
    b, s, h, d = q.shape
    log_f = jax.nn.log_sigmoid(f_logit.astype(F32))
    cum = jnp.cumsum(log_f, axis=1).transpose(0, 2, 1)
    outs = []
    for blk in range(s // Q_BLOCK):
        q0 = blk * Q_BLOCK
        q1 = q0 + Q_BLOCK
        logits = jnp.einsum('bihd,bjhd->bhij', q[:, q0:q1], k[:, :q1]).astype(F32) * d ** -0.5
        logits = logits + cum[:, :, q0:q1, None] - cum[:, :, None, :q1]
        mask = jnp.arange(q0, q1)[:, None] >= jnp.arange(q1)[None, :]
        p = jax.nn.softmax(jnp.where(mask, logits, -jnp.inf), axis=-1).astype(v.dtype)
        outs.append(jnp.einsum('bhij,bjhe->bihe', p, v[:, :q1]))
    return jnp.concatenate(outs, axis=1)

def causal_dwconv(u, w, bias):
    s = u.shape[1]
    up = jnp.pad(u, ((0, 0), (CONV_W - 1, 0), (0, 0)))
    out = bias
    for j in range(CONV_W):
        out = out + w[j] * up[:, j:j + s]
    return out

def hybrid_layer(x, c_act, norm1_g, norm2_g, w_ada, b_ada, w_in, w_gla_a2, b_gla_a, b_fox_f,
                 ret_norm_g, gla_norm_g, q_norm_g, k_norm_g, w_br, w_mg, b_mg, w_o,
                 w_up, w_conv, b_conv, w_down):
    b, s = x.shape[0], x.shape[1]
    mod = c_act @ w_ada + b_ada
    shift1, scale1, gate1, shift2, scale2, gate2 = jnp.split(mod, 6, axis=-1)

    h = modulate(rms_norm(x, norm1_g), shift1, scale1)
    split_points = np.cumsum(IN_SPLITS)[:-1].tolist()
    (rq, rk, rv, rg, gq, gk, gv, glr, gg, fq, fk, fv, ff) = jnp.split(h @ w_in, split_points, axis=-1)

    def heads(t, d):
        return t.reshape(b, s, N_HEADS, d)

    ret = retention(heads(rq, RET_DK), heads(rk, RET_DK), heads(rv, RET_DV))
    ret = head_group_norm(ret, ret_norm_g.reshape(N_HEADS, RET_DV)).reshape(b, s, BRANCH_W)
    ret = jax.nn.silu(rg) * ret

    log_a = jax.nn.log_sigmoid((glr @ w_gla_a2 + b_gla_a).astype(F32)) / GLA_TAU
    gla_o = gla(heads(gq, GLA_DK), heads(gk, GLA_DK), heads(gv, GLA_DV), heads(log_a, GLA_DK))
    gla_o = rms_norm(gla_o, gla_norm_g).reshape(b, s, BRANCH_W)
    gla_o = jax.nn.silu(gg) * gla_o

    fox_o = forgetting_attention(rms_norm(heads(fq, FOX_D), q_norm_g),
                                 rms_norm(heads(fk, FOX_D), k_norm_g),
                                 heads(fv, FOX_D), ff + b_fox_f).reshape(b, s, BRANCH_W)

    branches = jnp.stack([ret, gla_o, fox_o], axis=2).astype(h.dtype)
    y_br = jnp.einsum('bsnw,nwd->bsnd', branches, w_br)
    gates = jax.nn.sigmoid(h @ w_mg + b_mg).reshape(b, s, N_BRANCH, D_MODEL)
    mixed = jnp.sum(gates * y_br, axis=2) @ w_o
    x = x + (gate1[:, None, :] * mixed).astype(x.dtype)

    h2 = modulate(rms_norm(x, norm2_g), shift2, scale2)
    u, g = jnp.split(h2 @ w_up, 2, axis=-1)
    u = causal_dwconv(u, w_conv, b_conv)
    y = (jax.nn.silu(u) * g) @ w_down
    x = x + (gate2[:, None, :] * y).astype(x.dtype)
    return x

def first_inputs(seed: int = 0) -> dict:
    key = jax.random.key(seed)
    ks = jax.random.split(key, 24)

    def nrm(k, shape, scale):
        return jax.random.normal(k, shape, F32) * scale

    L, D = DEPTH, D_MODEL
    return {
        'x': nrm(ks[0], (BATCH, SEQ, D), 1.0),
        'c': nrm(ks[1], (BATCH, D), 1.0),
        'norm1_g': 1.0 + nrm(ks[2], (L, D), 0.02),
        'norm2_g': 1.0 + nrm(ks[3], (L, D), 0.02),
        'w_ada': nrm(ks[4], (L, D, 6 * D), 0.5 * D ** -0.5),
        'b_ada': nrm(ks[5], (L, 6 * D), 0.02),
        'w_in': nrm(ks[6], (L, D, IN_W), D ** -0.5),
        'w_gla_a2': nrm(ks[7], (L, GLA_LOWRANK, N_HEADS * GLA_DK), GLA_LOWRANK ** -0.5),
        'b_gla_a': nrm(ks[8], (L, N_HEADS * GLA_DK), 0.1),
        'b_fox_f': 1.0 + nrm(ks[9], (L, N_HEADS), 0.1),
        'ret_norm_g': 1.0 + nrm(ks[10], (L, N_HEADS * RET_DV), 0.02),
        'gla_norm_g': 1.0 + nrm(ks[11], (L, GLA_DV), 0.02),
        'q_norm_g': 1.0 + nrm(ks[12], (L, FOX_D), 0.02),
        'k_norm_g': 1.0 + nrm(ks[13], (L, FOX_D), 0.02),
        'w_br': nrm(ks[14], (L, N_BRANCH, BRANCH_W, D), BRANCH_W ** -0.5),
        'w_mg': nrm(ks[15], (L, D, N_BRANCH * D), D ** -0.5),
        'b_mg': nrm(ks[16], (L, N_BRANCH * D), 0.02),
        'w_o': nrm(ks[17], (L, D, D), D ** -0.5),
        'w_up': nrm(ks[18], (L, D, 2 * D_FF), D ** -0.5),
        'w_conv': nrm(ks[19], (L, CONV_W, D_FF), CONV_W ** -0.5),
        'b_conv': nrm(ks[20], (L, D_FF), 0.02),
        'w_down': nrm(ks[21], (L, D_FF, D), D_FF ** -0.5),
    }

def first_block(x, c, norm1_g, norm2_g, w_ada, b_ada, w_in, w_gla_a2, b_gla_a, b_fox_f,
              ret_norm_g, gla_norm_g, q_norm_g, k_norm_g, w_br, w_mg, b_mg, w_o,
              w_up, w_conv, b_conv, w_down):
    c_act = jax.nn.silu(c)
    for l in range(DEPTH):
        x = hybrid_layer(x, c_act, norm1_g[l], norm2_g[l], w_ada[l], b_ada[l], w_in[l],
                         w_gla_a2[l], b_gla_a[l], b_fox_f[l], ret_norm_g[l], gla_norm_g[l],
                         q_norm_g[l], k_norm_g[l], w_br[l], w_mg[l], b_mg[l], w_o[l],
                         w_up[l], w_conv[l], b_conv[l], w_down[l])
    return x


N_MIXERS = 2
POOL_WINDOWS = (2, 4, 8, 16)
N_POOL_GROUPS = len(POOL_WINDOWS)
POOL_GROUP_DIM = D_MODEL // N_POOL_GROUPS
HEAD_DIM_2 = 64
N_HEADS_2 = D_MODEL // HEAD_DIM_2
D_ATTN = N_HEADS_2 * HEAD_DIM_2
ATTN_PATTERNS = ((128, 1), (512, 4), (2048, 16))
N_ATTN_GROUPS = len(ATTN_PATTERNS)
HEAD_GROUPS = tuple(N_HEADS_2 // N_ATTN_GROUPS + (1 if g < N_HEADS_2 % N_ATTN_GROUPS else 0) for g in range(N_ATTN_GROUPS))
ROPE_THETA = 10000.0
D_FF_2 = -(-8 * D_MODEL // (3 * 256)) * 256
N_POOL_LAYERS = (DEPTH + 1) // 2
N_ATTN_LAYERS = DEPTH // 2
NEG_INF = -1e30


def rmsnorm(x, g):
    xf = x.astype(jnp.float32)
    y = xf * lax.rsqrt(jnp.mean(xf * xf, axis=-1, keepdims=True) + EPS)
    return (y * g.astype(jnp.float32)).astype(x.dtype)

def rope(t):
    S, hd = t.shape[1], t.shape[-1]
    inv_freq = 1.0 / (ROPE_THETA ** (jnp.arange(0, hd, 2, dtype=jnp.float32) / hd))
    ang = jnp.arange(S, dtype=jnp.float32)[:, None] * inv_freq[None, :]
    ang = jnp.concatenate([ang, ang], axis=-1)[None, :, None, :]
    tf = t.astype(jnp.float32)
    t1, t2 = tf[..., : hd // 2], tf[..., hd // 2 :]
    rot = jnp.concatenate([-t2, t1], axis=-1)
    return (tf * jnp.cos(ang) + rot * jnp.sin(ang)).astype(t.dtype)

def pool_mixer(h, w_in, w_group, scale, w_out):
    B, S, _ = h.shape
    u = jnp.einsum('bsd,de->bse', h, w_in).reshape(B, S, N_POOL_GROUPS, POOL_GROUP_DIM)
    cs = jnp.cumsum(u.astype(jnp.float32), axis=1)
    pos = jnp.arange(S)
    outs = []
    for g, w in enumerate(POOL_WINDOWS):
        c = cs[:, :, g]
        lag = jnp.pad(c, ((0, 0), (w, 0), (0, 0)))[:, :S]
        cnt = jnp.minimum(pos + 1, w).astype(jnp.float32)[None, :, None]
        outs.append((c - lag) / cnt - u[:, :, g].astype(jnp.float32))
    p = jnp.stack(outs, axis=2).astype(h.dtype)
    z = jnp.einsum('bsgc,gce->bsge', p, w_group).reshape(B, S, D_MODEL) * scale
    return jnp.einsum('bsd,de->bse', z, w_out)

def dilated_window_attention(q, k, v, window, dilation):
    B, S, H, hd = q.shape
    w = window // dilation
    L = S // dilation
    nb = -(-L // w)
    Lp = nb * w

    def to_blocks(t):
        t = t.reshape(B, L, dilation, H, hd)
        t = jnp.pad(t, ((0, 0), (0, Lp - L), (0, 0), (0, 0), (0, 0)))
        return t.reshape(B, nb, w, dilation, H, hd)

    qb, kb, vb = to_blocks(q), to_blocks(k), to_blocks(v)

    def with_prev(t):
        prev = jnp.concatenate([jnp.zeros_like(t[:, :1]), t[:, :-1]], axis=1)
        return jnp.concatenate([prev, t], axis=2)

    kc, vc = with_prev(kb), with_prev(vb)
    s = jnp.einsum('bnqrhd,bnkrhd->bnrhqk', qb, kc).astype(jnp.float32)
    qi = jnp.arange(w)[:, None]
    kj = jnp.arange(2 * w)[None, :]
    dist = w + qi - kj
    key_idx = jnp.arange(nb)[:, None, None] * w - w + kj[None]
    mask = (dist >= 0)[None] & (dist <= w)[None] & (key_idx >= 0)
    s = jnp.where(mask[None, :, None, None], s, NEG_INF)
    m = jnp.max(s, axis=-1, keepdims=True)
    e = jnp.exp(s - m)
    den = jnp.sum(e, axis=-1, keepdims=True)
    p = (e / den).astype(v.dtype)
    o = jnp.einsum('bnrhqk,bnkrhd->bnqrhd', p, vc)
    lse = (m + jnp.log(den))[..., 0]
    lse = jnp.transpose(lse, (0, 1, 4, 2, 3))
    o = o.reshape(B, Lp, dilation, H, hd)[:, :L].reshape(B, S, H, hd)
    lse = lse.reshape(B, Lp, dilation, H)[:, :L].reshape(B, S, H)
    return o, lse

def attn_mixer(h, w_qkv, w_out):
    B, S, _ = h.shape
    qkv = jnp.einsum('bsd,de->bse', h, w_qkv).reshape(B, S, 3, N_HEADS_2, HEAD_DIM_2)
    q = rope(qkv[:, :, 0]) * jnp.asarray(HEAD_DIM_2 ** -0.5, dtype=h.dtype)
    k = rope(qkv[:, :, 1])
    v = qkv[:, :, 2]
    outs, lses = [], []
    start = 0
    for (window, dilation), n_g in zip(ATTN_PATTERNS, HEAD_GROUPS):
        sl = slice(start, start + n_g)
        o_g, lse_g = dilated_window_attention(q[:, :, sl], k[:, :, sl], v[:, :, sl], window, dilation)
        outs.append(o_g)
        lses.append(jax.nn.logsumexp(lse_g, axis=-1) - math.log(n_g))
        start += n_g
    alpha = jax.nn.softmax(jnp.stack(lses, axis=-1), axis=-1)
    merged = jnp.concatenate(
        [o_g * (N_ATTN_GROUPS * alpha[:, :, g]).astype(o_g.dtype)[:, :, None, None] for g, o_g in enumerate(outs)],
        axis=2,
    ).reshape(B, S, D_ATTN)
    return jnp.einsum('bse,ed->bsd', merged, w_out)

def swiglu(h, w_gate, w_up, w_down):
    g = jnp.einsum('bsd,df->bsf', h, w_gate)
    u = jnp.einsum('bsd,df->bsf', h, w_up)
    return jnp.einsum('bsf,fd->bsd', jax.nn.silu(g) * u, w_down)

def second_inputs(seed: int = 0) -> dict:
    key = jax.random.key(seed)
    ks = jax.random.split(key, 14)
    f32 = jnp.float32
    nrm = lambda k, shape, fan_in: jax.random.normal(k, shape, f32) * (fan_in ** -0.5)
    return {
        "x": jax.random.normal(ks[0], (BATCH, SEQ, D_MODEL), f32),
        "norm_mix": 1.0 + 0.05 * jax.random.normal(ks[1], (DEPTH, D_MODEL), f32),
        "norm_ffn": 1.0 + 0.05 * jax.random.normal(ks[2], (DEPTH, D_MODEL), f32),
        "norm_final": 1.0 + 0.05 * jax.random.normal(ks[3], (D_MODEL,), f32),
        "pool_w_in": nrm(ks[4], (N_POOL_LAYERS, D_MODEL, D_MODEL), D_MODEL),
        "pool_w_group": nrm(ks[5], (N_POOL_LAYERS, N_POOL_GROUPS, POOL_GROUP_DIM, POOL_GROUP_DIM), POOL_GROUP_DIM),
        "pool_scale": 1.0 + 0.1 * jax.random.normal(ks[6], (N_POOL_LAYERS, D_MODEL), f32),
        "pool_w_out": nrm(ks[7], (N_POOL_LAYERS, D_MODEL, D_MODEL), D_MODEL),
        "attn_w_qkv": nrm(ks[8], (N_ATTN_LAYERS, D_MODEL, 3 * D_ATTN), D_MODEL),
        "attn_w_out": nrm(ks[9], (N_ATTN_LAYERS, D_ATTN, D_MODEL), D_ATTN),
        "ffn_w_gate": nrm(ks[10], (DEPTH, D_MODEL, D_FF_2), D_MODEL),
        "ffn_w_up": nrm(ks[11], (DEPTH, D_MODEL, D_FF_2), D_MODEL),
        "ffn_w_down": nrm(ks[12], (DEPTH, D_FF_2, D_MODEL), D_FF_2),
    }

def second_block(x, norm_mix, norm_ffn, norm_final, pool_w_in, pool_w_group, pool_scale, pool_w_out,
              attn_w_qkv, attn_w_out, ffn_w_gate, ffn_w_up, ffn_w_down):
    for i in range(DEPTH):
        h = rmsnorm(x, norm_mix[i])
        j = i // N_MIXERS
        if i % N_MIXERS == 0:
            y = pool_mixer(h, pool_w_in[j], pool_w_group[j], pool_scale[j], pool_w_out[j])
        else:
            y = attn_mixer(h, attn_w_qkv[j], attn_w_out[j])
        x = x + y
        h = rmsnorm(x, norm_ffn[i])
        x = x + swiglu(h, ffn_w_gate[i], ffn_w_up[i], ffn_w_down[i])
    return rmsnorm(x, norm_final)


def setup_inputs(seed=0):
    out = dict(first_inputs(seed))
    for name, value in second_inputs(seed + 1).items():
        if name != "x":
            out[name + "_2"] = value
    return out


def reference(
    x, c, norm1_g, norm2_g, w_ada, b_ada, w_in, w_gla_a2, b_gla_a, b_fox_f, ret_norm_g,
    gla_norm_g, q_norm_g, k_norm_g, w_br, w_mg, b_mg, w_o, w_up, w_conv, b_conv, w_down,
    norm_mix_2, norm_ffn_2, norm_final_2, pool_w_in_2, pool_w_group_2, pool_scale_2,
    pool_w_out_2, attn_w_qkv_2, attn_w_out_2, ffn_w_gate_2, ffn_w_up_2, ffn_w_down_2,
):
    x = first_block(
        x, c, norm1_g, norm2_g, w_ada, b_ada, w_in, w_gla_a2, b_gla_a, b_fox_f, ret_norm_g,
        gla_norm_g, q_norm_g, k_norm_g, w_br, w_mg, b_mg, w_o, w_up, w_conv, b_conv, w_down,
    )
    return second_block(
        x, norm_mix_2, norm_ffn_2, norm_final_2, pool_w_in_2, pool_w_group_2, pool_scale_2,
        pool_w_out_2, attn_w_qkv_2, attn_w_out_2, ffn_w_gate_2, ffn_w_up_2, ffn_w_down_2,
    )


_drawn_inputs = setup_inputs


def setup_inputs(seed=0):
    import zlib

    import numpy as np

    out = dict(_drawn_inputs(seed))
    spreads = {}
    factors = {'norm1_g': 4.917,
     'norm2_g': 5.738,
     'b_gla_a': 6.53,
     'b_fox_f': 6.911,
     'ret_norm_g': 8.0,
     'gla_norm_g': 8.0,
     'q_norm_g': 8.0,
     'k_norm_g': 8.0,
     'b_mg': 8.0,
     'b_conv': 8.0,
     'norm_mix_2': 8.0,
     'norm_ffn_2': 8.0,
     'pool_scale_2': 8.0,
     'attn_w_qkv_2': 3.392,
     'attn_w_out_2': 3.322}
    for name, (base, spread) in spreads.items():
        noise = np.random.default_rng([zlib.crc32(name.encode()), seed]).standard_normal(out[name].shape)
        drawn = base * np.exp(spread * noise) if base else spread * noise
        out[name] = jnp.asarray(drawn.astype(out[name].dtype))
    for name, factor in factors.items():
        out[name] = (out[name] * factor).astype(out[name].dtype)
    return out
```

```python
from contextlib import ExitStack

import concourse.bass as bass
import numpy as np
from concourse import mybir

F32 = mybir.dt.float32
F32R = mybir.dt.float32r
ALU = mybir.AluOpType
ACT = mybir.ActivationFunctionType
AXX = mybir.AxisListType.X

S = 512
D = 1024
KD = D // 128
FF = 2816
KF = FF // 128
DEPTH = 2
EPS = 1e-6
NSLOT = 6
AHEAD = 3
NEG = -1e30
COL_A = [("b_ada", 48), ("b_mg", 24), ("norm1_g", 8), ("norm2_g", 8), ("ret_norm_g", 4), ("gla_norm_g", 1),
         ("q_norm_g", 1), ("k_norm_g", 1), ("b_conv", 22)]


def tables():
    i = np.arange(128)
    out = {}
    out["ident"] = np.eye(128)
    out["center"] = np.eye(128) - 1.0 / 128
    out["causal"] = np.where(i[:, None] >= i[None, :], 0.0, NEG)
    out["tail"] = ((i[:, None] // 64 == i[None, :] // 64) & (i[:, None] > i[None, :])) * 1.0
    out["chunk"] = (i[:, None] // 64 == np.arange(2)[None, :]) * 1.0
    kj = np.arange(256)
    dist = 128 + i[:, None] - kj[None, :]
    out["window"] = np.where((dist >= 0) & (dist <= 128), 0.0, NEG)
    out["dil"] = np.where((i[:, None] >= i[None, :]) & ((i[:, None] - i[None, :]) % 4 == 0), 0.0, NEG)
    out["sel"] = np.concatenate([np.zeros((96, 512)), np.repeat(np.eye(4), 128, axis=1), np.zeros((28, 512))])
    t = np.arange(S, dtype=np.float64)
    f = 10000.0 ** (-np.arange(64) / 64.0)
    ang = f[:, None] * t[None, :]
    out["cos1"] = np.concatenate([np.cos(ang), np.cos(ang)])
    out["sin1"] = np.concatenate([np.sin(ang), -np.sin(ang)])
    f = 10000.0 ** (-np.arange(32) / 32.0)
    ang = f[:, None] * t[None, :]
    out["cos2"] = np.concatenate([np.cos(ang)] * 4)
    out["sin2"] = np.concatenate([np.sin(ang), -np.sin(ang)] * 2)
    lg = np.log1p(-np.exp2(-5.0 - np.arange(4)))
    q = np.arange(S)[None, :]
    j = i[:, None]
    live = (q // 64) >= (j // 64)
    dec = [np.where(live, np.exp(np.abs(q - j) * g), 0.0) * 128 ** -0.5 for g in lg]
    out["decay"] = np.concatenate(dec, axis=1)
    cnt = [np.broadcast_to(1.0 / np.minimum(np.arange(16) + 1, w), (128, 16)) for w in (2, 4, 8, 16)]
    out["cnt"] = np.concatenate(cnt, axis=1)
    return {k: np.ascontiguousarray(v, dtype=np.float32) for k, v in out.items()}


BUSY = "busy"


class Lane:

    def __init__(self, sem):
        self.sem, self.queue, self.count, self.seen = sem, [], 0, {}

    def wait(self, *toks):
        for tok in toks:
            if tok is None:
                continue
            if isinstance(tok, list):
                self.wait(*tok)
                continue
            sem, value = tok
            if self.seen.get(id(sem), 0) < value:
                self.seen[id(sem)] = value
                self.queue.append(lambda e, s=sem, v=value: e.wait_ge(s, v))

    def go(self, fn, *toks):
        self.wait(*toks)
        self.queue.append(fn)

    def __call__(self, fn, *toks):
        self.wait(*toks)
        self.count += 1
        self.queue.append(lambda e, s=self.sem: fn(e).then_inc(s, 1))
        return (self.sem, self.count)

    def emit(self, e):
        for f in self.queue:
            f(e)


class Flow:

    def __init__(self, lane, sem):
        self.lane, self.sem, self.count = lane, sem, 0

    def __call__(self, out, in_, *toks):
        self.lane.wait((self.sem, self.count) if self.count else None, *toks)
        self.count += 16
        self.lane.queue.append(lambda e, s=self.sem: e.dma_start(out, in_).then_inc(s, 16))
        return (self.sem, self.count)


def bc(col, n):
    return col.to_broadcast([col.shape[0], n])


def drain(gen):
    for _ in gen:
        pass


def weave(main, fill, per=1):
    for _ in main:
        for _ in range(per):
            next(fill, None)
    drain(fill)


class Program:
    def __init__(self, nc, I, out, sems, mem, plan):
        self.nc, self.I, self.out, self.mem, self.plan = nc, I, out, mem, plan
        (s_pe, s_ve, s_ac, s_po, s_ring, s_misc, s_out) = sems
        self.pe, self.ve, self.ac, self.po = Lane(s_pe), Lane(s_ve), Lane(s_ac), Lane(s_po)
        self.sp = Lane(None)
        self.ring_flow = [Flow(self.sp, s) for s in s_ring]
        self.misc = [Flow(self.sp, s) for s in s_misc]
        self.mi = 0
        self.out_flow = [Flow(self.sp, s) for s in s_out]
        self.descs = []
        self.n_dma = 0
        self.n_split = 0
        self.dma_tok, self.split_tok, self.done_tok = {}, {}, {}
        self.free = {b: None for b in mem["bank"]}
        self.big_order = ["b0", "b1", "b2"]
        self.big_i = 0
        self.HT = [None] * KD
        self.t = mem["t"]

    def load(self, out, in_, *toks):
        f = self.misc[self.mi % len(self.misc)]
        self.mi += 1
        return f(out, in_, *toks)

    def need(self, desc, pair=False):
        n = len(self.descs)
        if pair and n % NSLOT == NSLOT - 1:
            self.descs.append(None)
            n += 1
        self.descs.append(desc)
        self.pump(n)
        return n

    def pump(self, n):
        plan = self.plan if self.plan is not None else self.descs
        def freed(m):
            m -= NSLOT
            if m >= 0 and plan[m] is None:
                m -= NSLOT
            return (True, None) if m < 0 else (m in self.done_tok, self.done_tok.get(m))

        while self.n_dma < len(plan) and self.n_dma <= n + NSLOT - 1:
            m = self.n_dma
            known, free = freed(m)
            if not known:
                break
            if plan[m] is not None:
                s = m % NSLOT
                for sub, (dst, src) in enumerate(plan[m][1]):
                    f = self.ring_flow[s if sub == 0 else NSLOT + sub - 1]
                    tok = f(dst(self.mem["raw"][:, s, :]), src, free)
                    self.dma_tok.setdefault(m, []).append(tok)
            self.n_dma += 1
        while self.n_split < self.n_dma and self.n_split <= n + AHEAD:
            m = self.n_split
            if plan[m] is not None and plan[m][0]:
                s = m % NSLOT
                w = plan[m][2]
                raw, hi, lo = (self.mem[x][:, s, 0:w] for x in ("raw", "hi", "lo"))
                th = self.ac(lambda e, o=hi, i=raw: e.activation(o, i, ACT.Copy), self.dma_tok[m], freed(m)[1])
                self.split_tok[m] = self.po(
                    lambda e, o=lo, i=raw, h=hi: e.tensor_tensor(o, i, h.bitcast(F32), ALU.subtract), th)
            elif plan[m] is not None:
                self.split_tok[m] = self.dma_tok[m]
            self.n_split += 1
        assert n in self.split_tok

    def weight(self, ap, r0, kt, c0, w, pair=False):
        src = ap[r0:r0 + kt * 128, c0:c0 + w].rearrange("(k p) c -> p k c", p=128)
        return self.need((True, [(lambda r, kt=kt, w=w: r[:, 0:kt * w].rearrange("p (k c) -> p k c", k=kt), src)],
                          kt * w), pair)

    def views(self, n, kt, w):
        s = n % NSLOT
        return tuple(self.mem[x][:, s, 0:kt * w].rearrange("p (k c) -> p k c", k=kt) for x in ("hi", "lo"))

    def pair_views(self, n):
        s = n % NSLOT
        return tuple(self.mem[x][:, s:s + 2, :].rearrange("p h (k c) -> p h k c", k=8) for x in ("hi", "lo"))

    def bank(self):
        b = self.big_order[self.big_i % len(self.big_order)]
        self.big_i += 1
        before, self.free[b] = self.free[b], BUSY
        assert before is not BUSY
        return b, before

    def dot(self, out, terms, start=True, stop=True, toks=()):
        tok = None
        total = len(terms)
        for k, (wh, wl, xh, xl, t) in enumerate(terms):
            self.pe.wait(t, list(toks) if k == 0 else None)
            for a, (w, x) in enumerate(((wh, xh), (wh, xl), (wl, xh))):
                first = start and k == 0 and a == 0
                last = stop and k == total - 1 and a == 2
                f = lambda e, w=w, x=x, fi=first, la=last: e.matmul(out, w, x, start=fi, stop=la)
                if k == total - 1 and a == 2:
                    tok = self.pe(f)
                else:
                    self.pe.go(f)
            if k % 4 == 3 and k != total - 1:
                yield None
        self.last = tok
        yield None
        return tok

    def project(self, ap, c0, then):
        n = self.weight(ap, 0, 8, c0, 128)
        hi, lo = self.views(n, 8, 128)
        yield from self.tile_of(n, hi, lo, then)

    def tile_of(self, n, hi, lo, then):
        b, fr = self.bank()
        out = self.mem["bank"][b]
        HH, HL = self.t["HH"], self.t["HL"]
        terms = [(hi[:, k, :], lo[:, k, :], HH[:, k, :], HL[:, k, :], self.HT[k]) for k in range(8)]
        tok = yield from self.dot(out[:, :], terms, toks=(self.split_tok[n], fr))
        self.done_tok[n] = tok
        self.free[b] = then(out, tok)

    def project_rows(self, ap, c0, then, rows=None):
        na = self.weight(ap, 0, 8, c0, 128, pair=True)
        nb = self.weight(ap, 0, 8, c0 + 128, 128)
        assert nb == na + 1 and na % NSLOT != NSLOT - 1
        hi, lo = self.pair_views(na)
        HH, HL = self.t["HH"], self.t["HL"]
        for u in range(2):
            b, fr = self.bank()
            out = self.mem["bank"][b]
            for t in (2 * u, 2 * u + 1):
                pick = slice(t * 128, t * 128 + 128) if rows is None else rows(t)
                terms = [(HH[:, k, pick], HL[:, k, pick], hi[:, :, k, :], lo[:, :, k, :], self.HT[k])
                         for k in range(8)]
                o = out[:, (t % 2) * 256:(t % 2) * 256 + 256]
                tok = yield from self.dot(o, terms, toks=(self.split_tok[na], self.split_tok[nb], fr))
            self.free[b] = then(out, tok, u)
        self.done_tok[na] = self.done_tok[nb] = tok

    def project_rows_half(self, ap, c0, then, rows=None):
        n = self.weight(ap, 0, 8, c0, 128)
        hi, lo = self.views(n, 8, 128)
        HH, HL = self.t["HH"], self.t["HL"]
        b, fr = self.bank()
        out = self.mem["bank"][b]
        for t in range(4):
            pick = slice(t * 128, t * 128 + 128) if rows is None else rows(t)
            terms = [(HH[:, k, pick], HL[:, k, pick], hi[:, k, :], lo[:, k, :], self.HT[k]) for k in range(8)]
            tok = yield from self.dot(out[:, t * 128:t * 128 + 128], terms, toks=(self.split_tok[n], fr))
        self.done_tok[n] = tok
        self.free[b] = then(out, tok)

    def colsq(self, sq, st, col, tok, start=True, stop=True, check=False):
        ones = self.t["ones"]
        for t in range(4):
            f = lambda e, t=t: e.matmul(st[:, col + t:col + t + 1], sq[:, t * 128:t * 128 + 128], ones[:, 0:1],
                                        start=start if not check else (start and t == 0), stop=stop,
                                        skip_group_check=check)
            if t == 3:
                return self.pe(f, tok)
            self.pe.go(f, tok)

    def rstd(self, st, col, n, width, tok, out):
        a = self.ac(lambda e: e.activation(out, st[:, col:col + n], ACT.Sqrt, bias=self.t["eps"][:, 0:1],
                                           scale=1.0 / width), tok)
        return self.ve(lambda e: e.reciprocal(out, out), a), a

    def spread(self, cols, bank, tok):
        out = self.mem["bank"][bank]
        ident = self.t["ident"]
        self.pe.wait(tok, self.free[bank])
        for t in range(4):
            f = lambda e, t=t: e.matmul(out[:, t * 128:t * 128 + 128], bc(cols[:, t:t + 1], 128), ident[:, :],
                                        start=True, stop=True)
            if t == 3:
                return self.pe(f)
            self.pe.go(f)

    def x_update(self, d, bank, tok, gate):
        X, SQ = self.t["X"], self.t["SQ"]
        out = self.mem["bank"][bank]
        if gate is None:
            a = self.ve(lambda e: e.tensor_tensor(X[:, d, :], out[:, :], X[:, d, :], ALU.add), tok)
        else:
            a = self.ve(lambda e: e.scalar_tensor_tensor(out=X[:, d, :], in0=out[:, :], scalar=gate, in1=X[:, d, :],
                                                         op0=ALU.mult, op1=ALU.add), tok)
        self.free[bank] = a
        self.square(d, a)

    def square(self, d, tok):
        X, SQ = self.t["X"], self.t["SQ"]
        self.sq_tok = self.ac(lambda e: e.activation(SQ[:, d % 2, :], X[:, d, :], ACT.Square), tok,
                              self.sq_used[d % 2])

    def x_sums(self, d):
        st = self.mem["bank"]["t1"]
        self.sq_used[d % 2] = self.colsq(self.t["SQ"][:, d % 2, :], st, 0, [self.sq_tok, self.free["t1"]], start=(d == 0), stop=(d == KD - 1),
                                         check=True)

    def x_norm(self, A, B, at):
        X, HH, HL, NT, RS = (self.t[k] for k in ("X", "HH", "HL", "NT", "RS"))
        r, a = self.rstd(self.mem["bank"]["t1"], 0, 4, D, self.sq_used[(KD - 1) % 2], RS[:, 0:4])
        self.free["t1"] = a
        sp = self.spread(RS, "t0", r)
        row = self.mem["bank"]["t0"]
        used = self.h_used
        for k in range(KD):
            b = k % 3
            v = self.ve(lambda e, k=k, b=b: e.scalar_tensor_tensor(out=NT[:, b, :], in0=X[:, k, :], scalar=A[:, k:k + 1],
                                                                   in1=row[:, :], op0=ALU.mult, op1=ALU.mult),
                        sp, at, self.nt_used[b])
            if B is None:
                h = self.ac(lambda e, k=k, b=b: e.activation(HH[:, k, :], NT[:, b, :], ACT.Copy), v, used)
                l = self.ve(lambda e, k=k, b=b: e.tensor_tensor(HL[:, k, :], NT[:, b, :], HH[:, k, :].bitcast(F32),
                                                                ALU.subtract), h, used)
            else:
                h = self.ac(lambda e, k=k, b=b: e.activation(HH[:, k, :], NT[:, b, :], ACT.Identity,
                                                             bias=B[:, k:k + 1]), v, used, at)
                l = self.ve(lambda e, k=k, b=b: e.scalar_tensor_tensor(out=HL[:, k, :], in0=NT[:, b, :],
                                                                       scalar=B[:, k:k + 1],
                                                                       in1=HH[:, k, :].bitcast(F32), op0=ALU.add,
                                                                       op1=ALU.subtract), h, used)
            self.HT[k] = l
            self.nt_used[b] = l
        self.free["t0"] = v

    def ada(self, l, q):
        w = self.I["w_ada"][l]
        AA, MOD, CA, ones, PAR = (self.t[k] for k in ("AA", "MOD", "CA", "ones", "PAR"))
        v = None
        for g in range(4):
            src = w[g * 256:(g + 1) * 256, q * 512:(q + 1) * 512].rearrange("(k p) c -> p k c", p=128)
            n = self.need((False, [(lambda r: r.rearrange("p (k c) -> p k c", k=2), src)], 1024))
            raw = self.mem["raw"][:, n % NSLOT, :]
            for k in range(2):
                kk = 2 * g + k
                if kk == 0:
                    v = self.ve(lambda e, r=raw: e.tensor_scalar(AA[:, :], r[:, 0:512], CA[:, 0:1], None, ALU.mult),
                                self.split_tok[n], self.ca_tok, self.aa_used)
                else:
                    v = self.ve(lambda e, r=raw, k=k, kk=kk: e.scalar_tensor_tensor(
                        out=AA[:, :], in0=r[:, k * 512:k * 512 + 512], scalar=CA[:, kk:kk + 1], in1=AA[:, :],
                        op0=ALU.mult, op1=ALU.add), self.split_tok[n], v)
            self.done_tok[n] = v
            yield None
        yield None
        b, fr = self.bank()
        out = self.mem["bank"][b]
        self.pe.wait(v, fr)
        for j in range(4):
            f = lambda e, j=j: e.matmul(out[:, j:j + 1], AA[:, j * 128:j * 128 + 128], ones[:, 0:1], start=True,
                                        stop=True)
            p = self.pe(f)
        self.aa_used = p
        c = self.pcol(l, "b_ada")
        self.free[b] = self.mod_tok = self.ve(
            lambda e: e.tensor_tensor(MOD[:, l, 4 * q:4 * q + 4], out[:, 0:4], PAR[:, c + 4 * q:c + 4 * q + 4],
                                      ALU.add), p, self.par_tok)
        yield None

    def pcol(self, l, name):
        c = l * 256
        for key, n in COL_A:
            if key == name:
                return c
            c += n
        assert name == "w_conv"
        return l * 256 + 128

    def rope_pieces(self, out, dst, tmp, cos, sin, half, scale, tok, tt, used):
        a = self.ve(lambda e: e.scalar_tensor_tensor(out=dst, in0=out[:, :], scalar=scale, in1=cos, op0=ALU.mult,
                                                     op1=ALU.mult), tok, tt, used)
        for p in range(0, 128, 2 * half):
            for d, s in ((p, p + half), (p + half, p)):
                b = self.ve(lambda e, d=d, s=s: e.scalar_tensor_tensor(
                    out=tmp[d:d + half, :], in0=out[s:s + half, :], scalar=scale, in1=sin[s:s + half, :],
                    op0=ALU.mult, op1=ALU.mult), used)
        return b, self.ve(lambda e: e.tensor_tensor(dst, dst, tmp, ALU.add), a, b)

    def ret_attention(self):
        q, k, v, O, dec = (self.t[x] for x in ("rq", "rk", "rv", "RO", "decay"))
        PT, OS, SQ, RS, PAR = (self.t[x] for x in ("retP", "retO", "retS", "RS", "PAR"))
        bank, free, pe, ve, ac = self.mem["bank"], self.free, self.pe, self.ve, self.ac
        steps = [(h, j) for h in range(4) for j in range(4)]
        st = {}
        used = [None, None]

        def score(n):
            h, j = steps[n]
            b = f"s{n % 2}"
            w = S - 128 * j
            p = pe(lambda e: e.matmul(bank[b][:, 0:w], k[:, h, j * 128:j * 128 + 128], q[:, h, j * 128:S], start=True,
                                      stop=True), self.rk_tok[h], self.rq_tok[h], free[b])
            free[b] = st[n] = ve(lambda e: e.tensor_tensor(PT[:, n % 2, 0:w], bank[b][:, 0:w],
                                                           dec[:, h * S:h * S + w], ALU.mult), p, used[n % 2],
                                 self.dec_tok)

        def value(n):
            h, j = steps[n]
            w = S - 128 * j
            f = lambda e: e.matmul(bank["o"][:, j * 128:S], v[:, j, h * 128:h * 128 + 128], PT[:, n % 2, 0:w],
                                   start=(j == 0), stop=(j == 3))
            used[n % 2] = pe(f, st[n], self.rv_tok, free["o"] if j == 0 else None)
            if j == 3:
                free["o"] = st["o", h] = ac(lambda e: e.activation(OS[:, h % 2, :], bank["o"][:, :], ACT.Copy),
                                            used[n % 2], st.get(("xc", h - 2)))

        def center(h):
            st["xc", h] = pe(lambda e: e.matmul(bank["t0"][:, :], self.t["center"][:, :], OS[:, h % 2, :], start=True,
                                                stop=True), st["o", h], free["t0"])
            a = ac(lambda e: e.activation(SQ[:, h % 2, :], bank["t0"][:, :], ACT.Square), st["xc", h],
                   st.get(("sq", h - 2)))
            free["t0"] = ve(lambda e: e.tensor_copy(O[:, h, :], bank["t0"][:, :]), a)
            st["s", h] = a

        def sums(h):
            st["sq", h] = self.colsq(SQ[:, h % 2, :], bank["t1"], 4 * h, [st["s", h], free["t1"]])

        for n in range(len(steps) + 4):
            if n < len(steps):
                score(n)
            if 1 <= n <= len(steps):
                value(n - 1)
            if n >= 6 and (n - 6) % 4 == 0 and (n - 6) // 4 < 4:
                center((n - 6) // 4)
            if n >= 7 and (n - 7) % 4 == 0 and (n - 7) // 4 < 4:
                sums((n - 7) // 4)
            yield None
        center(3)
        yield None
        sums(3)
        yield None
        r, a = self.rstd(bank["t1"], 0, 16, 128, st["sq", 3], RS[:, 0:16])
        free["t1"] = a
        yield None
        c = self.pcol(self.l, "ret_norm_g")
        self.ro_tok = [None] * 4
        for h in range(4):
            s = self.spread(RS[:, 4 * h:4 * h + 4], "t0", r)
            free["t0"] = self.ro_tok[h] = ve(lambda e, h=h: e.scalar_tensor_tensor(
                out=O[:, h, :], in0=O[:, h, :], scalar=PAR[:, c + h:c + h + 1], in1=bank["t0"][:, :], op0=ALU.mult,
                op1=ALU.mult), s)
            yield None

    def fox_inputs(self, w):
        bank, pe, ve, ac = self.mem["bank"], self.pe, self.ve, self.ac
        q, k, v, SQ, RS2 = (self.t[x] for x in ("fq", "fk", "fv", "foxS", "RS2"))
        GLR, FFR, FFT, bf = (self.t[x] for x in ("GLR", "FFR", "FFT", "BF"))
        st = bank["b2"]
        sq_used = [None, None]
        prev = []
        l = self.l

        srcs = []
        for (d0, c0, n) in ((0, 3072, 96), (96, 5136, 4), (100, 3168, 28)):
            src = w[:, c0:c0 + n].rearrange("(k p) c -> p k c", p=128)
            srcs.append((lambda r, d0=d0, n=n: r.rearrange("p (k c) -> p k c", k=8)[:, :, d0:d0 + n], src))
        n = self.need((True, srcs, 1024))
        hi, lo = self.views(n, 8, 128)

        def small(out, tok):
            m = self.po(lambda e: e.memset(GLR[0:32, :], 1.0), self.glr_used, self.HT)
            m = self.po(lambda e: e.memset(FFR[:, :], 0.0), self.ffr_used)
            m = self.po(lambda e: e.memset(FFT[:, :], 0.0))
            g = ve(lambda e: e.tensor_copy(GLR[0:16, :], out[0:16, :]), tok, m)
            self.glr_tok = g
            z = slice(96, 100)
            f = ve(lambda e: e.tensor_scalar(FFR[z, :], out[z, :], bf[z, l:l + 1], None, ALU.add), g,
                   self.par_tok, self.ffr_used)
            a = ac(lambda e: e.activation(FFT[z, :], FFR[z, :], ACT.Abs), f)
            a = ac(lambda e: e.activation(FFT[z, :], FFT[z, :], ACT.Exp, scale=-1.0), a)
            a = ac(lambda e: e.activation(FFT[z, :], FFT[z, :], ACT.Ln, bias=self.t["one"][z, 0:1]), a)
            b = ve(lambda e: e.scalar_tensor_tensor(out=FFT[z, :], in0=FFR[z, :], scalar=0.0, in1=FFT[z, :],
                                                    op0=ALU.min, op1=ALU.subtract), a)
            b = ve(lambda e: e.tensor_tensor_scan(FFR[z, :], bc(self.t["one"][z, 0:1], S), FFT[z, :], 0.0,
                                                  ALU.mult, ALU.add), b)
            self.cum_tok = ve(lambda e: e.tensor_scalar(FFT[z, :], FFR[z, :], -1.0, None, ALU.mult), b)
            return f

        yield from self.tile_of(n, hi, lo, small)

        for i, (dst, c0) in enumerate([(q, 3600 + 128 * h) for h in range(4)] + [(k, 4112 + 128 * h) for h in range(4)]):
            h = i % 4

            def take(out, tok, i=i, h=h, dst=dst):
                a = ac(lambda e: e.activation(SQ[:, i % 2, :], out[:, :], ACT.Square), tok, sq_used[i % 2])
                b = ve(lambda e: e.tensor_copy(dst[:, h, :], out[:, :]), a)
                prev.append((i, a, b))
                return b

            yield from self.project(w, c0, take)
            if i >= 1:
                j, a, b = prev[i - 1]
                sq_used[j % 2] = self.colsq(SQ[:, j % 2, :], st, 4 * j, [a, self.free["b2"]])
        self.fv_tok = []
        for c in range(2):
            def keep(out, tok, u, c=c):
                t = ac(lambda e: e.activation(v[:, 2 * u:2 * u + 2, c * 256:c * 256 + 256],
                                              out[:, :].rearrange("p (t c) -> p t c", t=2), ACT.Copy), tok)
                self.fv_tok.append(t)
                return t
            yield from self.project_rows(w, 4624 + 256 * c, keep)
            if c == 0:
                j, a, b = prev[7]
                p = self.colsq(SQ[:, j % 2, :], st, 4 * j, a)
                r, a = self.rstd(st, 0, 32, 128, p, RS2[:, 0:32])
                self.free["b2"] = a
                self.foxr = r
        yield None

    def fox_norm(self):
        bank, ve = self.mem["bank"], self.ve
        RS2, PAR, GQ = (self.t[x] for x in ("RS2", "PAR", "GQ"))
        cq, ck = self.pcol(self.l, "q_norm_g"), self.pcol(self.l, "k_norm_g")
        g = ve(lambda e: e.tensor_scalar(GQ[:, 0:1], PAR[:, cq:cq + 1], 128 ** -0.5, None, ALU.mult), self.par_tok)
        self.fq_tok, self.fk_tok = [None] * 4, [None] * 4
        for h in range(4):
            for i, dst, toks, col in ((h, self.t["fq"], self.fq_tok, GQ[:, 0:1]),
                                      (4 + h, self.t["fk"], self.fk_tok, PAR[:, ck:ck + 1])):
                b = "t0"
                s = self.spread(RS2[:, 4 * i:4 * i + 4], b, self.foxr)
                toks[h] = self.free[b] = ve(lambda e, dst=dst, col=col, b=b, h=h: e.scalar_tensor_tensor(
                    out=dst[:, h, :], in0=dst[:, h, :], scalar=col, in1=bank[b][:, :], op0=ALU.mult, op1=ALU.mult),
                    s, g)
            yield None

    def fox_attention(self):
        q, k, v, EH, EL = (self.t[x] for x in ("fq", "fk", "fv", "EfH", "EfL"))
        P, PT, DG, M, R = (self.t[x] for x in ("foxP", "foxT", "foxD", "foxM", "foxR"))
        cum, ncum, sel = self.t["FFR"], self.t["FFT"], self.t["sel"]
        bank, free, pe, ve, ac = self.mem["bank"], self.free, self.pe, self.ve, self.ac
        z = slice(96, 100)
        steps = [(h, i) for h in range(4) for i in range(4)]
        st = {}
        self.ef_tok = [None] * 4

        def score(n):
            h, i = steps[n]
            b = f"s{n % 2}"
            w = 128 * (i + 1)
            o = bank[b]
            r = slice(i * 128, w)
            pe.go(lambda e: e.matmul(o[:, 0:w], sel[:, h * 128:h * 128 + 128], ncum[:, 0:w], start=True, stop=False),
                  self.cum_tok, free[b])
            pe.go(lambda e: e.matmul(o[:, 0:w], cum[:, r], bc(sel[:, h * 128:h * 128 + 1], w), start=False,
                                     stop=False))
            pe.go(lambda e: e.matmul(o[:, i * 128:w], self.t["ident"][:, :], self.t["causal"][:, :], start=False,
                                     stop=False))
            p = pe(lambda e: e.matmul(o[:, 0:w], q[:, h, r], k[:, h, 0:w], start=False, stop=True), self.fq_tok[h], self.fk_tok[h])
            m = ve(lambda e: e.tensor_reduce(M[:, n:n + 1], o[:, 0:w], AXX, ALU.max), p)
            m = ve(lambda e: e.tensor_scalar(M[:, n:n + 1], M[:, n:n + 1], -1.0, None, ALU.mult), m)
            x = ac(lambda e: e.activation(P[:, n % 2, 0:w], o[:, 0:w], ACT.Exp, bias=M[:, n:n + 1],
                                          accum_out=R[:, n:n + 1]), m, st.get(("t", n - 2)))
            free[b] = x
            x = ve(lambda e: e.reciprocal(R[:, n:n + 1], R[:, n:n + 1]), x)
            st["s", n] = ve(lambda e: e.tensor_scalar(DG[:, n % 2, :], self.t["ident"][:, :], R[:, n:n + 1], None,
                                                      ALU.mult), x, st.get(("t", n - 2)))

        def turn(n):
            h, i = steps[n]
            b = f"t{n % 2}"
            pe.wait(st["s", n], free[b])
            for j in range(i + 1):
                f = lambda e, j=j: e.matmul(bank[b][:, j * 128:j * 128 + 128], P[:, n % 2, j * 128:j * 128 + 128],
                                            DG[:, n % 2, :], start=True, stop=True)
                p = pe(f) if j == i else pe.go(f)
            st["t", n] = p
            w = 128 * (i + 1)
            free[b] = st["p", n] = ac(lambda e: e.activation(PT[:, n % 2, 0:w], bank[b][:, 0:w], ACT.Copy), p,
                                      st.get(("v", n - 2)))

        def value(n):
            h, i = steps[n]
            pe.wait(st["p", n], self.fv_tok, free["o"] if i == 0 else None)
            for j in range(i + 1):
                f = lambda e, j=j: e.matmul(bank["o"][:, i * 128:i * 128 + 128], v[:, j, h * 128:h * 128 + 128],
                                            PT[:, n % 2, j * 128:j * 128 + 128], start=(j == 0), stop=(j == i))
                p = pe(f) if j == i else pe.go(f)
            st["v", n] = p
            if i == 3:
                a = ac(lambda e: e.activation(EH[:, h, :], bank["o"][:, :], ACT.Copy), p)
                free["o"] = self.ef_tok[h] = ve(lambda e: e.tensor_tensor(
                    EL[:, h, :], bank["o"][:, :], EH[:, h, :].bitcast(F32), ALU.subtract), a)

        N = len(steps)
        for n in range(N + 2):
            if n < N:
                score(n)
            if 1 <= n <= N:
                turn(n - 1)
            if n >= 2:
                value(n - 2)
            yield None
        self.ffr_used = [st["s", N - 1], st["t", N - 1]]

    def gla_inputs(self, w):
        gk, gv, gq = (self.t[x] for x in ("gk", "gv", "gq"))
        self.gk_tok, self.gv_tok, self.gq_tok = [], [], [None, None]

        def keep_k(out, tok, u):
            t = self.ac(lambda e: e.activation(gk[:, 2 * u:2 * u + 2, :], out[:, :].rearrange("p (t c) -> p t c", t=2),
                                               ACT.Copy), tok)
            self.gk_tok.append(t)
            return t

        yield from self.project_rows(w, 2304, keep_k)
        for c in range(2):
            def keep_v(out, tok, u, c=c):
                t = self.ac(lambda e: e.activation(gv[:, 2 * u:2 * u + 2, c * 256:c * 256 + 256],
                                                   out[:, :].rearrange("p (t c) -> p t c", t=2), ACT.Copy), tok)
                self.gv_tok.append(t)
                return t
            yield from self.project_rows(w, 2560 + 256 * c, keep_v)
        for c in range(2):
            def keep_q(out, tok, c=c):
                self.gq_tok[c] = self.ac(lambda e: e.activation(gq[:, c, :], out[:, :], ACT.Copy, scale=64 ** -0.5),
                                         tok)
                return self.gq_tok[c]
            yield from self.project(w, 2048 + 128 * c, keep_q)

    def gla_attention(self):
        gk, gv, gq, GO = (self.t[x] for x in ("gk", "gv", "gq", "GO"))
        LA, TA, ED, AD, SA, SQ, RS, GLR, WA, PAR = (self.t[x] for x in (
            "LA", "TA", "ED", "AD", "SA", "glaS", "RS", "GLR", "WA", "PAR"))
        bank, free, pe, ve, ac = self.mem["bank"], self.free, self.pe, self.ve, self.ac
        st = {}
        for u in range(2):
            o = bank[f"s{u}"]
            pe.wait(self.glr_tok, self.wa_tok, free[f"s{u}"])
            for t in (2 * u, 2 * u + 1):
                f = lambda e, t=t, o=o: e.matmul(o[:, (t % 2) * 256:(t % 2) * 256 + 256],
                                                 GLR[0:17, t * 128:t * 128 + 128], WA[0:17, 0:256], start=True, stop=True)
                st["z", u] = pe(f)
        self.glr_used = st["z", 1]
        yield None
        for u in range(2):
            st["a", u] = ac(lambda e, u=u: e.activation(TA[:, u, :], bank[f"s{u}"][:, :], ACT.Abs), st["z", u])
        for u in range(2):
            st["a", u] = ac(lambda e, u=u: e.activation(TA[:, u, :], TA[:, u, :], ACT.Exp, scale=-1.0), st["a", u])
        for u in range(2):
            st["a", u] = ac(lambda e, u=u: e.activation(TA[:, u, :], TA[:, u, :], ACT.Ln,
                                                        bias=self.t["one"][:, 0:1]), st["a", u])
            free[f"s{u}"] = st["l", u] = ve(lambda e, u=u: e.scalar_tensor_tensor(
                out=LA[:, u, :], in0=bank[f"s{u}"][:, :], scalar=0.0, in1=TA[:, u, :], op0=ALU.min,
                op1=ALU.subtract), st["a", u])
        yield None
        yield None
        for u in range(2):
            pe.wait(st["l", u], free[f"t{u}"])
            for t in range(2):
                f = lambda e, t=t, u=u: e.matmul(bank[f"t{u}"][:, t * 256:t * 256 + 256], self.t["tail"][:, :],
                                                 LA[:, u, t * 256:t * 256 + 256], start=True, stop=True)
                p = pe(f)
            free[f"t{u}"] = a = ac(lambda e, u=u: e.activation(ED[:, u, :], bank[f"t{u}"][:, :], ACT.Exp,
                                                               scale=1.0 / 16), p)
            st["k", u] = ve(lambda e, u=u: e.tensor_tensor(ED[:, u, :], ED[:, u, :],
                                                           gk[:, 2 * u:2 * u + 2, :].rearrange("p t c -> p (t c)"),
                                                           ALU.mult), a, self.gk_tok)
        pe.wait(free["s0"])
        for f2 in range(2):
            for t in range(4):
                f = lambda e, f2=f2, t=t: e.matmul(
                    bank["s0"][:, f2 * 8 + 2 * t:f2 * 8 + 2 * t + 2],
                    LA[:, t // 2, (t % 2) * 256 + f2 * 128:(t % 2) * 256 + f2 * 128 + 128],
                    self.t["chunk"][:, :], start=True, stop=True)
                p = pe(f)
        free["s0"] = st["ad"] = ac(lambda e: e.activation(AD[:, 0:16], bank["s0"][:, 0:16], ACT.Exp, scale=1.0 / 16), p)
        yield None
        yield None
        for p2 in range(2):
            pe.wait(st["k", 0], st["k", 1], self.gv_tok, free["t0"], free["t1"])
            for n in range(8):
                for hh in range(2):
                    c0, t = 64 * (n % 2), n // 2
                    h = 2 * p2 + hh
                    f = lambda e, c0=c0, t=t, h=h, hh=hh, n=n: e.matmul(
                        bank[f"t{n % 2}"][64 * hh:64 * hh + 64, (n // 2) * 128:(n // 2) * 128 + 128],
                        ED[c0:c0 + 64, t // 2, (t % 2) * 256 + h * 64:(t % 2) * 256 + h * 64 + 64],
                        gv[c0:c0 + 64, t, h * 128:h * 128 + 128], start=True, stop=True)
                    p = pe(f)
            for n in range(8):
                kv = bank[f"t{n % 2}"][:, (n // 2) * 128:(n // 2) * 128 + 128]
                if n == 0:
                    s = ve(lambda e, kv=kv, p2=p2: e.tensor_copy(SA[:, p2, 0, :], kv), p)
                else:
                    s = ve(lambda e, kv=kv, n=n, p2=p2: e.scalar_tensor_tensor(
                        out=SA[:, p2, n, :], in0=SA[:, p2, n - 1, :], scalar=AD[:, p2 * 8 + n:p2 * 8 + n + 1],
                        in1=kv, op0=ALU.mult, op1=ALU.add), s, p, st["ad"])
            free["t0"] = free["t1"] = s
            yield None
            st["S", p2] = s
        yield None
        for p2 in range(2):
            for hh in range(2):
                h = 2 * p2 + hh
                b = f"s{hh}"
                pe.wait(st["S", p2], self.gq_tok[p2], free[b])
                for n in range(8):
                    f = lambda e, n=n, b=b, p2=p2, hh=hh: e.matmul(
                        bank[b][:, n * 64:n * 64 + 64], SA[64 * hh:64 * hh + 64, p2, n, :],
                        gq[64 * hh:64 * hh + 64, p2, n * 64:n * 64 + 64], start=True, stop=True)
                    p = pe(f)
                a = ac(lambda e, b=b, hh=hh: e.activation(SQ[:, hh, :], bank[b][:, :], ACT.Square), p,
                       st.get(("sq", h - 2)))
                free[b] = ve(lambda e, b=b, h=h: e.tensor_copy(GO[:, h, :], bank[b][:, :]), a)
                st["s", h] = a
                yield None
                if h >= 1:
                    st["sq", h - 1] = self.colsq(SQ[:, (h - 1) % 2, :], bank["t1"], 4 * (h - 1),
                                                 [st["s", h - 1], free["t1"]])
        st["sq", 3] = self.colsq(SQ[:, 1, :], bank["t1"], 12, st["s", 3])
        r, a = self.rstd(bank["t1"], 0, 16, 128, st["sq", 3], RS[:, 0:16])
        free["t1"] = a
        yield None
        c = self.pcol(self.l, "gla_norm_g")
        self.go_tok = [None] * 4
        for h in range(4):
            s = self.spread(RS[:, 4 * h:4 * h + 4], "t0", r)
            free["t0"] = self.go_tok[h] = ve(lambda e, h=h: e.scalar_tensor_tensor(
                out=GO[:, h, :], in0=GO[:, h, :], scalar=PAR[:, c:c + 1], in1=bank["t0"][:, :], op0=ALU.mult,
                op1=ALU.mult), s)
            yield None

    def gated(self, w, c0, O, toks, EH, EL):
        G = self.t["GT"]
        ve, ac = self.ve, self.ac
        out_tok = [None] * 4
        for h in range(4):
            def take(out, tok, h=h):
                b = self.gt_i % 2
                self.gt_i += 1
                a = ac(lambda e: e.activation(G[:, b, :], out[:, :], ACT.Silu), tok, self.gt_used[b])
                m = ve(lambda e: e.tensor_tensor(G[:, b, :], G[:, b, :], O[:, h, :], ALU.mult), a, toks()[h])
                x = ac(lambda e: e.activation(EH[:, h, :], G[:, b, :], ACT.Copy), m)
                self.gt_used[b] = out_tok[h] = ve(lambda e: e.tensor_tensor(
                    EL[:, h, :], G[:, b, :], EH[:, h, :].bitcast(F32), ALU.subtract), x)
                return a
            yield from self.project(w, c0 + 128 * h, take)
        self.gated_tok = out_tok

    def mixing(self, l):
        wmg, wbr = self.I["w_mg"][l], self.I["w_br"][l]
        E = [(self.t[f"E{x}H"], self.t[f"E{x}L"], tk) for x, tk in (("r", self.er_tok), ("g", self.eg_tok),
                                                                    ("f", self.ef_tok))]
        MH, ML, SG, MX, PAR = (self.t[x] for x in ("MH", "ML", "SG", "MX", "PAR"))
        ve, ac = self.ve, self.ac
        c = self.pcol(l, "b_mg")
        self.mix_tok = [None] * 8
        sg_used = [None] * 2
        sg_tok = [None] * 2
        mx_tok = [None] * 2
        for dp in range(4):
            for n in range(3):
                for u in range(2):
                    d = 2 * dp + u

                    def gate(out, tok, u=u, d=d, n=n):
                        j = c + 8 * n + d
                        sg_tok[u] = ac(lambda e: e.activation(SG[:, u, :], out[:, :], ACT.Sigmoid,
                                                              bias=PAR[:, j:j + 1]), tok, sg_used[u])
                        return sg_tok[u]

                    yield from self.project(wmg, n * 1024 + d * 128, gate)
                m = self.weight(wbr[n], 0, 4, dp * 256, 256)
                hi, lo = self.views(m, 4, 256)
                H_, L_, tk = E[n]
                for u in range(2):
                    d = 2 * dp + u
                    b, fr = self.bank()
                    out = self.mem["bank"][b]
                    terms = [(hi[:, k, u * 128:u * 128 + 128], lo[:, k, u * 128:u * 128 + 128], H_[:, k, :], L_[:, k, :], tk[k])
                             for k in range(4)]
                    tok = yield from self.dot(out[:, :], terms, toks=(self.split_tok[m], fr))
                    if n == 0:
                        v = ve(lambda e, u=u, out=out: e.tensor_tensor(MX[:, u, :], out[:, :], SG[:, u, :], ALU.mult),
                               tok, sg_tok[u], mx_tok[u])
                        self.free[b] = sg_used[u] = v
                    else:
                        v = ve(lambda e, u=u, out=out: e.tensor_tensor(SG[:, u, :], out[:, :], SG[:, u, :], ALU.mult),
                               tok, sg_tok[u])
                        self.free[b] = v
                        v = ve(lambda e, u=u: e.tensor_tensor(MX[:, u, :], MX[:, u, :], SG[:, u, :], ALU.add), v,
                               mx_tok[u])
                        sg_used[u] = v
                    mx_tok[u] = v
                self.done_tok[m] = tok
            for u in range(2):
                d = 2 * dp + u
                a = ac(lambda e, u=u, d=d: e.activation(MH[:, d, :], MX[:, u, :], ACT.Copy), mx_tok[u])
                mx_tok[u] = self.mix_tok[d] = ve(lambda e, u=u, d=d: e.tensor_tensor(
                    ML[:, d, :], MX[:, u, :], MH[:, d, :].bitcast(F32), ALU.subtract), a)

    def out_proj(self, ap, kt, AH, AL, toks, gate):
        for d in range(8):
            b, fr = self.bank()
            out = self.mem["bank"][b]
            for k0 in range(0, kt, 8):
                kn = min(8, kt - k0)
                n = self.weight(ap, k0 * 128, kn, d * 128, 128)
                hi, lo = self.views(n, kn, 128)
                terms = [(hi[:, k, :], lo[:, k, :], AH[:, k0 + k, :], AL[:, k0 + k, :], toks[k0 + k]) for k in range(kn)]
                tok = yield from self.dot(out[:, :], terms, start=(k0 == 0), stop=(k0 + kn == kt),
                                          toks=(self.split_tok[n], fr))
                self.done_tok[n] = tok
            if d:
                self.x_sums(d - 1)
            self.x_update(d, b, tok, None if gate is None else gate[:, d:d + 1])
        yield None

    def ffn_up(self, wu, cu, wg, cg, conv):
        AH, AL, CB, PAR = (self.t[x] for x in ("FH", "FL", "CB", "PAR"))
        ve, ac = self.ve, self.ac
        self.ff_tok = [None] * KF
        used = [None, None]
        for f in range(KF):
            i = f % 2
            hold = {}

            def up(out, tok, f=f, i=i):
                if conv is None:
                    hold["s"] = ac(lambda e: e.activation(CB[:, i, :], out[:, :], ACT.Silu), tok, used[i])
                    return hold["s"]
                wc, bcol = conv
                a = ac(lambda e: e.activation(CB[:, i, :], out[:, :], ACT.Identity, scale=wc(2, f), bias=bcol(f)), tok,
                       used[i], self.par_tok)
                v = ve(lambda e: e.scalar_tensor_tensor(out=CB[:, i, 1:S], in0=out[:, 0:S - 1], scalar=wc(1, f),
                                                        in1=CB[:, i, 1:S], op0=ALU.mult, op1=ALU.add), a)
                v = ve(lambda e: e.scalar_tensor_tensor(out=CB[:, i, 2:S], in0=out[:, 0:S - 2], scalar=wc(0, f),
                                                        in1=CB[:, i, 2:S], op0=ALU.mult, op1=ALU.add), v)
                hold["s"] = ac(lambda e: e.activation(CB[:, i, :], CB[:, i, :], ACT.Silu), v)
                return v

            yield from self.project(wu, cu + f * 128, up)

            def gate(out, tok, f=f, i=i):
                v = ve(lambda e: e.tensor_tensor(CB[:, i, :], CB[:, i, :], out[:, :], ALU.mult), tok, hold["s"])
                a = ac(lambda e: e.activation(AH[:, f, :], CB[:, i, :], ACT.Copy), v)
                used[i] = self.ff_tok[f] = ve(lambda e: e.tensor_tensor(
                    AL[:, f, :], CB[:, i, :], AH[:, f, :].bitcast(F32), ALU.subtract), a)
                return v

            yield from self.project(wg, cg + f * 128, gate)

    def pool_mixer(self):
        I, t = self.I, self.t
        bank, free, pe, ve, ac = self.mem["bank"], self.free, self.pe, self.ve, self.ac
        U, W1, W2, PH, PL, ZH, ZL, CT, PAR = (t[x] for x in ("U", "W1", "W2", "PH", "PL", "ZH", "ZL", "CT", "PAR"))
        p_tok = [None] * 8
        for g in range(4):
            for c in range(2):
                d = 2 * g + c
                i = d % 2

                def take(out, tok, g=g, d=d, i=i):
                    u = ac(lambda e: e.activation(U[:, i, :], out[:, :], ACT.Copy), tok,
                           p_tok[d - 2] if d >= 2 else None)
                    src, v = U[:, i, :], u
                    for s in range(g + 1):
                        k = 1 << s
                        dst = (W1 if s % 2 == 0 else W2)[:, i, :]
                        a = ve(lambda e, dst=dst, src=src, k=k: e.tensor_copy(dst[:, 0:k], src[:, 0:k]), v)
                        v = ve(lambda e, dst=dst, src=src, k=k: e.tensor_tensor(dst[:, k:S], src[:, k:S],
                                                                                src[:, 0:S - k], ALU.add), v)
                        v = [a, v]
                        src = dst
                    w = 2 << g
                    oth = (W1 if g % 2 == 1 else W2)[:, i, :]
                    a = ve(lambda e: e.tensor_tensor(oth[:, 0:16], src[:, 0:16], CT[:, g * 16:g * 16 + 16], ALU.mult), v)
                    b = ve(lambda e: e.tensor_scalar(oth[:, 16:S], src[:, 16:S], 1.0 / w, None, ALU.mult))
                    b = ve(lambda e: e.tensor_tensor(oth[:, :], oth[:, :], U[:, i, :], ALU.subtract), a, b)
                    h = ac(lambda e: e.activation(PH[:, d, :], oth[:, :], ACT.Copy), b)
                    p_tok[d] = ve(lambda e: e.tensor_tensor(PL[:, d, :], oth[:, :], PH[:, d, :].bitcast(F32),
                                                            ALU.subtract), h)
                    return u

                yield from self.project(I["pool_w_in_2"][0], d * 128, take)
        z_tok = [None] * 8
        c0 = 512 + 40
        for g in range(4):
            n = self.weight(I["pool_w_group_2"][0, g], 0, 2, 0, 256)
            hi, lo = self.views(n, 2, 256)
            for c in range(2):
                d = 2 * g + c
                b, fr = self.bank()
                out = bank[b]
                terms = [(hi[:, k, c * 128:c * 128 + 128], lo[:, k, c * 128:c * 128 + 128], PH[:, 2 * g + k, :],
                          PL[:, 2 * g + k, :], p_tok[2 * g + k]) for k in range(2)]
                tok = yield from self.dot(out[:, :], terms, toks=(self.split_tok[n], fr))
                sc = PAR[:, c0 + d:c0 + d + 1]
                h = ac(lambda e, out=out, sc=sc, d=d: e.activation(ZH[:, d, :], out[:, :], ACT.Copy, scale=sc), tok)
                free[b] = z_tok[d] = ve(lambda e, out=out, sc=sc, d=d: e.scalar_tensor_tensor(
                    out=ZL[:, d, :], in0=out[:, :], scalar=sc, in1=ZH[:, d, :].bitcast(F32), op0=ALU.mult,
                    op1=ALU.subtract), h)
            self.done_tok[n] = tok
        yield from self.out_proj(I["pool_w_out_2"][0], 8, ZH, ZL, z_tok, None)

    def attn_inputs(self):
        w = self.I["attn_w_qkv_2"][0]
        t = self.t
        self.aq_tok, self.ak_tok, self.av_tok = [None] * 8, [None] * 8, [None] * 8
        used = [None, None]
        i = 0
        strided = lambda r: slice(r, S, 4)
        for p in range(8):
            for dst, c0, sc, toks in ((t["aq"], 0, 64 ** -0.5, self.aq_tok), (t["ak"], 1024, 1.0, self.ak_tok)):
                def take(out, tok, i=i, dst=dst, sc=sc, toks=toks, p=p):
                    b, toks[p] = self.rope_pieces(out, dst[:, p, :], t["aT"][:, i % 2, :], t["cos2"][:, :],
                                                  t["sin2"][:, :], 32, sc, tok, self.tab_tok, used[i % 2])
                    used[i % 2] = toks[p]
                    return b
                i += 1
                yield from self.project(w, c0 + 128 * p, take)

            def keep(out, tok, p=p):
                self.av_tok[p] = self.ac(lambda e: e.activation(
                    t["av"][:, :, p * 128:p * 128 + 128], out[:, :].rearrange("p (t c) -> p t c", t=4), ACT.Copy), tok)
                return self.av_tok[p]

            yield from self.project_rows_half(w, 2048 + 128 * p, keep, None if p < 3 else strided)

    def attn_heads(self):
        t = self.t
        q, k, v, MO = (t[x] for x in ("aq", "ak", "av", "MO"))
        SB, P, PT, DG, M, NM, DEN, R = (t[x] for x in ("aS", "aP", "aPT", "aD", "aM", "aNM", "aDEN", "aR"))
        bank, free, pe, ve, ac = self.mem["bank"], self.free, self.pe, self.ve, self.ac
        steps = [(h, n) for h in range(16) for n in range(4)]
        st = {}
        self.mo_tok = [None] * 8

        def group(h):
            return 0 if h < 6 else 1 if h < 11 else 2

        def cols(h, n):
            if group(h) == 0:
                lo = max(0, n - 1)
                msk = t["window"][:, :] if n else t["window"][:, 128:256]
                return slice(n * 128, n * 128 + 128), slice(lo * 128, n * 128 + 128), list(range(lo, n + 1)), msk
            msk = t["causal"] if group(h) == 1 else t["dil"]
            return slice(n, S, 4), slice(n, S, 4), [n], msk[:, :]

        def score(m):
            h, n = steps[m]
            p, r = h // 2, slice(64 * (h % 2), 64 * (h % 2) + 64)
            b = f"s{m % 2}"
            i = m % 4
            qs, ks, tiles, msk = cols(h, n)
            w = 128 * len(tiles)
            pt = pe(lambda e: e.matmul(bank[b][:, 0:w], q[r, p, qs], k[r, p, ks], start=True, stop=True),
                    self.aq_tok[p], self.ak_tok[p], free[b])
            a = ve(lambda e: e.tensor_tensor_reduce(SB[:, i, 0:w], bank[b][:, 0:w], msk, 1.0, -3e38, ALU.add, ALU.max,
                                                    M[:, m:m + 1]), pt, st.get(("x", m - 4)))
            free[b] = a
            a = ve(lambda e: e.tensor_scalar(NM[:, m:m + 1], M[:, m:m + 1], -1.0, None, ALU.mult), a)
            x = ac(lambda e: e.activation(P[:, i, 0:w], SB[:, i, 0:w], ACT.Exp, bias=NM[:, m:m + 1],
                                          accum_out=DEN[:, m:m + 1]), a, st.get(("t", m - 4)))
            st["x", m] = x
            d = ve(lambda e: e.reciprocal(R[:, m:m + 1], DEN[:, m:m + 1]), x)
            st["s", m] = ve(lambda e: e.tensor_scalar(DG[:, i, :], t["ident"][:, :], R[:, m:m + 1], None, ALU.mult), d,
                            st.get(("t", m - 4)))
            self.lse_in = st["s", m]

        def turn(m):
            h, n = steps[m]
            b = f"t{m % 2}"
            i = m % 4
            nt = len(cols(h, n)[2])
            pe.wait(st["s", m], free[b])
            for j in range(nt):
                f = lambda e, j=j: e.matmul(bank[b][:, j * 128:j * 128 + 128], P[:, i, j * 128:j * 128 + 128],
                                            DG[:, i, :], start=True, stop=True)
                p = pe(f) if j == nt - 1 else pe.go(f)
            st["t", m] = p
            free[b] = st["p", m] = ac(lambda e: e.activation(PT[:, i, 0:128 * nt], bank[b][:, 0:128 * nt], ACT.Copy), p,
                                      st.get(("v", m - 4)))

        def value(m):
            h, n = steps[m]
            p, r = h // 2, slice(64 * (h % 2), 64 * (h % 2) + 64)
            i = m % 4
            ob = "o" if p % 2 == 0 else "b0"
            tiles = cols(h, n)[2]
            pe.wait(st["p", m], self.av_tok[p], free[ob] if n == 0 and h % 2 == 0 else None)
            for j, kt in enumerate(tiles):
                f = lambda e, j=j, kt=kt: e.matmul(bank[ob][r, n * 128:n * 128 + 128], v[:, kt, h * 64:h * 64 + 64],
                                                   PT[:, i, j * 128:j * 128 + 128], start=(j == 0),
                                                   stop=(j == len(tiles) - 1))
                pt = pe(f) if j == len(tiles) - 1 else pe.go(f)
            st["v", m] = pt
            if n == 3 and h % 2 == 1:
                src = bank[ob][:, :]
                if group(h) == 0:
                    f = lambda e: e.activation(MO[:, p, :], src, ACT.Copy)
                else:
                    f = lambda e: e.activation(MO[:, p, :].rearrange("p (l r) -> p r l", r=4),
                                               src.rearrange("p (r l) -> p r l", r=4), ACT.Copy)
                free[ob] = self.mo_tok[p] = ac(f, pt)

        N = len(steps)
        for m in range(N + 4):
            if m < N:
                score(m)
            if 2 <= m < N + 2:
                turn(m - 2)
            if m >= 4:
                value(m - 4)
            yield None

    def attn_merge(self):
        t = self.t
        bank, free, pe, ve, ac = self.mem["bank"], self.free, self.pe, self.ve, self.ac
        M, DEN, L, GM, LT, AL, TM, MO = (t[x] for x in ("aM", "aDEN", "aL", "aG", "aLT", "ALP", "aTM", "MO"))
        a = ac(lambda e: e.activation(L[:, 0:64], DEN[:, 0:64], ACT.Ln), self.lse_in)
        l = ve(lambda e: e.tensor_tensor(L[:, 0:64], L[:, 0:64], M[:, 0:64], ALU.add), a)
        heads = ((0, 6), (6, 11), (11, 16))
        tok = []
        for g, (h0, h1) in enumerate(heads):
            nh = h1 - h0
            x = L[:, 4 * h0:4 * h1].rearrange("p (h n) -> p n h", n=4)
            m = ve(lambda e, g=g, x=x: e.tensor_reduce(GM[:, g, :], x, AXX, ALU.max), l)
            for h in range(h0, h1):
                s = ve(lambda e, h=h, g=g: e.tensor_tensor(LT[:, 4 * h:4 * h + 4], L[:, 4 * h:4 * h + 4], GM[:, g, :],
                                                           ALU.subtract), m, l)
            tok.append((m, s))
        a = ac(lambda e: e.activation(LT[:, 0:64], LT[:, 0:64], ACT.Exp), tok[2][1])
        for g, (h0, h1) in enumerate(heads):
            x = LT[:, 4 * h0:4 * h1].rearrange("p (h n) -> p n h", n=4)
            s = ve(lambda e, g=g, x=x: e.tensor_reduce(GM[:, 3 + g, :], x, AXX, ALU.add), a)
        a = ac(lambda e: e.activation(GM[:, 6:9, :], GM[:, 3:6, :], ACT.Ln, scale=1.0), s)
        for g, (h0, h1) in enumerate(heads):
            s = ve(lambda e, g=g, n=h1 - h0: e.scalar_tensor_tensor(
                out=GM[:, 6 + g, :], in0=GM[:, g, :], scalar=-float(np.log(n)), in1=GM[:, 6 + g, :], op0=ALU.add,
                op1=ALU.add), a)
        for g in range(3):
            b = ("s0", "s1", "t0")[g]
            p = self.spread(GM[:, 6 + g, :], b, s)
            src = bank[b][:, :]
            if g == 0:
                f = lambda e, src=src: e.tensor_copy(AL[:, 0, :], src)
            else:
                f = lambda e, src=src, g=g: e.tensor_copy(AL[:, g, :].rearrange("p (l r) -> p r l", r=4),
                                                          src.rearrange("p (r l) -> p r l", r=4))
            free[b] = c = ve(f, p)
        m = ve(lambda e: e.tensor_tensor(TM[:, 0, :], AL[:, 0, :], AL[:, 1, :], ALU.max), c)
        m = ve(lambda e: e.tensor_tensor(TM[:, 0, :], TM[:, 0, :], AL[:, 2, :], ALU.max), m)
        for g in range(3):
            m2 = ve(lambda e, g=g: e.tensor_tensor(AL[:, g, :], AL[:, g, :], TM[:, 0, :], ALU.subtract), m)
        E3 = t["aE"]
        for g in range(3):
            x = ac(lambda e, g=g: e.activation(E3[:, g, :], AL[:, g, :], ACT.Exp), m2)
        s = ve(lambda e: e.tensor_tensor(TM[:, 0, :], E3[:, 0, :], E3[:, 1, :], ALU.add), x)
        s = ve(lambda e: e.tensor_tensor(TM[:, 0, :], TM[:, 0, :], E3[:, 2, :], ALU.add), s)
        a = ac(lambda e: e.activation(TM[:, 1, :], TM[:, 0, :], ACT.Ln), s)
        for g in range(3):
            s = ve(lambda e, g=g: e.tensor_tensor(AL[:, g, :], AL[:, g, :], TM[:, 1, :], ALU.subtract), a)
        for g in range(3):
            a = ac(lambda e, g=g: e.activation(AL[:, g, :], AL[:, g, :], ACT.Exp), s)
        G = (0, 0, 0, 1, 1, None, 2, 2)
        YH, YL = t["YH"], t["YL"]
        self.y_tok = [None] * 8
        for p in range(8):
            parts = [(slice(0, 128), G[p])] if G[p] is not None else [(slice(0, 64), 1), (slice(64, 128), 2)]
            for r, g in parts:
                v = ve(lambda e, r=r, g=g, p=p: e.scalar_tensor_tensor(
                    out=MO[r, p, :], in0=MO[r, p, :], scalar=3.0, in1=AL[r, g, :], op0=ALU.mult, op1=ALU.mult), a,
                    self.mo_tok[p])
            h = ac(lambda e, p=p: e.activation(YH[:, p, :], MO[:, p, :], ACT.Copy), v)
            self.y_tok[p] = ve(lambda e, p=p: e.tensor_tensor(YL[:, p, :], MO[:, p, :], YH[:, p, :].bitcast(F32),
                                                              ALU.subtract), h)

    def finish(self):
        t = self.t
        bank, free, pe, ve, ac = self.mem["bank"], self.free, self.pe, self.ve, self.ac
        X, RS, OT, PAR = (t[x] for x in ("X", "RS", "OT", "PAR"))
        c0 = 512 + 32
        r, a = self.rstd(bank["t1"], 0, 4, D, self.sq_used[(KD - 1) % 2], RS[:, 0:4])
        x = []
        sp = self.spread(RS, "t0", r)
        for k in range(KD):
            x.append(ve(lambda e, k=k: e.scalar_tensor_tensor(
                out=X[:, k, :], in0=X[:, k, :], scalar=PAR[:, c0 + k:c0 + k + 1], in1=bank["t0"][:, :],
                op0=ALU.mult, op1=ALU.mult), sp))
        outs = []
        i = 0
        for tt in range(4):
            for u in range(2):
                b = ("s0", "s1", "o", "b0", "b1", "b2")[i % 6]
                pe.wait(free[b])
                for k in range(4 * u, 4 * u + 4):
                    f = lambda e, k=k, b=b, tt=tt: e.transpose(bank[b][:, (k % 4) * 128:(k % 4) * 128 + 128],
                                                               X[:, k, tt * 128:tt * 128 + 128], t["ident"][:, :])
                    p = pe(f, x[k])
                if i % 2:
                    g = lambda e, b=b, tt=tt, u=u: e.activation(OT[:, tt, u * 512:u * 512 + 512], bank[b][:, :], ACT.Copy)
                    free[b] = ac(g, p)
                else:
                    g = lambda e, b=b, tt=tt, u=u: e.tensor_copy(OT[:, tt, u * 512:u * 512 + 512], bank[b][:, :])
                    free[b] = ve(g, p)
                outs.append(free[b])
                i += 1
            outs.append(self.out_flow[tt](self.out[0, tt * 128:tt * 128 + 128, :], OT[:, tt, :], outs[-2:]))
        self.sp.wait(*[o for o in outs if o[0] in [f.sem for f in self.out_flow]])

    def run(self):
        I, t = self.I, self.t
        pe, ve, ac, po = self.pe, self.ve, self.ac, self.po
        bank, free = self.mem["bank"], self.free
        self.sq_used, self.nt_used, self.h_used = [None] * 2, [None] * 3, None
        self.gt_i, self.gt_used = 0, [None, None]
        self.glr_used = self.ffr_used = self.aa_used = None
        T = self.mem["tables"]

        one = po(lambda e: e.memset(t["ones"][:, :], 1.0))
        one = po(lambda e: e.memset(t["eps"][:, :], EPS))
        for lane in (pe, ve, ac):
            lane.wait(one)
        XS = t["XS"]
        x_in = [self.load(XS[:, tt, :], I["x"][0, tt * 128:tt * 128 + 128, :]) for tt in range(4)]
        idt = self.load(t["ident"][:, :], T["ident"])
        PST = t["PST"]
        par = []
        for l in range(DEPTH):
            r = 0
            for name, n in COL_A:
                src = I[name][l].rearrange("(r c) -> r c", c=128)
                par.append(self.load(PST[r:r + n, 2 * l, :], src))
                r += n
            src = I["w_conv"][l].rearrange("j (r c) -> (j r) c", c=128)
            par.append(self.load(PST[0:66, 2 * l + 1, :], src))
        r = 0
        for name, n in (("norm_mix_2", 16), ("norm_ffn_2", 16), ("norm_final_2", 8), ("pool_scale_2", 8), ("c", 8)):
            ap = I[name]
            src = ap.rearrange("(r c) -> r c", c=128) if len(ap.shape) == 1 else ap.rearrange("l (r c) -> (l r) c", c=128)
            par.append(self.load(PST[r:r + n, 4, :], src))
            r += n
        for l in range(DEPTH):
            par.append(self.load(t["BF"][96:100, l:l + 1], I["b_fox_f"][l].rearrange("(h o) -> h o", o=1)))
        con = [self.load(t[k][:, :], T[k]) for k in ("center", "causal", "tail", "chunk", "window", "dil", "sel")]
        con.append(self.load(t["CT"][:, :], T["cnt"]))
        self.con_tok = con
        i = 0
        for k in range(KD):
            b = ("s0", "s1", "o", "t0")[k % 4]
            pe.wait(free[b], idt)
            for tt in range(4):
                p = pe(lambda e, k=k, tt=tt, b=b: e.transpose(bank[b][:, tt * 128:tt * 128 + 128],
                                                              XS[:, tt, k * 128:k * 128 + 128], t["ident"][:, :]), x_in[tt])
            free[b] = ve(lambda e, k=k, b=b: e.tensor_copy(t["X"][:, k, :], bank[b][:, :]), p)
            self.square(k, free[b])
            self.x_sums(k)
        rows = (117, 66, 117, 66, 56)
        for j, n in enumerate(rows):
            b = ("s0", "s1")[j % 2]
            p = pe(lambda e, j=j, n=n, b=b: e.transpose(bank[b][:, 0:n], PST[0:n, j, :], t["ident"][0:n, 0:n]), free[b], par)
            free[b] = self.par_tok = ve(lambda e, j=j, n=n, b=b: e.tensor_copy(t["PAR"][:, j * 128:j * 128 + n],
                                                                               bank[b][:, 0:n]), p)
        self.ca_tok = ac(lambda e: e.activation(t["CA"][:, :], t["PAR"][:, 512 + 48:512 + 56], ACT.Silu), self.par_tok)
        for lane in (pe, ve):
            lane.wait(con, idt)

        def mods(l, which):
            c = self.pcol(l, "norm1_g" if which == 0 else "norm2_g")
            A = t["NA"][:, 2 * l + which, :]
            MOD = t["MOD"]
            s = 24 * which
            return ve(lambda e: e.scalar_tensor_tensor(out=A, in0=MOD[:, l, s + 8:s + 16], scalar=1.0,
                                                       in1=t["PAR"][:, c:c + 8], op0=ALU.add, op1=ALU.mult),
                      self.mod_tok), A, MOD[:, l, s:s + 8]

        for q in range(4):
            drain(self.ada(0, q))
        for l in range(DEPTH):
            self.l = l
            w = I["w_in"][l]
            tok, A, B = mods(l, 0)
            prev = self.last if l else None
            self.x_norm(A, B, tok)
            tabs = [self.load(t["cos1"][:, :], T["cos1"], prev), self.load(t["sin1"][:, :], T["sin1"], prev)]
            self.dec_tok = self.load(t["decay"][:, :], T["decay"], prev)
            self.wa_tok = [self.load(t["WA"][0:16, 0:256], I["w_gla_a2"][l], self.glr_used),
                           self.load(t["WA"][16:17, 0:256], I["b_gla_a"][l].rearrange("(o c) -> o c", o=1), self.glr_used)]
            self.rq_tok, self.rk_tok, self.rv_tok = [None] * 4, [None] * 4, []
            used = [None, None]
            i = 0
            for h in range(4):
                for dst, c0, toks in ((t["rq"], 0, self.rq_tok), (t["rk"], 512, self.rk_tok)):
                    def take(out, tok, i=i, dst=dst, toks=toks, h=h):
                        b, toks[h] = self.rope_pieces(out, dst[:, h, :], t["rT"][:, i % 2, :], t["cos1"][:, :],
                                                      t["sin1"][:, :], 64, 1.0, tok, tabs, used[i % 2])
                        used[i % 2] = toks[h]
                        return b
                    i += 1
                    drain(self.project(w, c0 + 128 * h, take))
            for c in range(2):
                def keep(out, tok, u, c=c):
                    k = ac(lambda e: e.activation(t["rv"][:, 2 * u:2 * u + 2, c * 256:c * 256 + 256],
                                                  out[:, :].rearrange("p (t c) -> p t c", t=2), ACT.Copy), tok)
                    self.rv_tok.append(k)
                    return k
                drain(self.project_rows(w, 1024 + 256 * c, keep))
            rest = [q for q in range(4, 12)] if l == 0 else []
            self.big_order = ["b0", "b1"]
            weave(self.ret_attention(), self.fox_inputs(w), 2)
            drain(self.fox_norm())
            self.big_order = ["b0", "b1", "b2"]

            def fill3(w=w, rest=rest):
                yield from self.gla_inputs(w)
                for q in rest[0:2]:
                    yield from self.ada(0, q)
            weave(self.fox_attention(), fill3(), 2)
            weave(self.gla_attention(), self.gated(w, 1536, t["RO"], lambda: self.ro_tok, t["ErH"], t["ErL"]), 1)
            self.er_tok = self.gated_tok
            drain(self.gated(w, 3088, t["GO"], lambda: self.go_tok, t["EgH"], t["EgL"]))
            self.eg_tok = self.gated_tok
            self.big_order = ["b0", "b1", "b2", "o", "s0", "s1"]
            ada = [(0, q) for q in rest[2:]]

            def fill6():
                for a in ada:
                    yield from self.ada(*a)
            weave(self.mixing(l), fill6(), 1)
            self.mod_all = self.mod_tok
            pe.wait(self.mod_tok)
            ve.wait(self.mod_tok)
            drain(self.out_proj(I["w_o"][l], 8, t["MH"], t["ML"], self.mix_tok, t["MOD"][:, l, 16:24]))
            self.x_sums(KD - 1)
            tok, A, B = mods(l, 1)
            self.x_norm(A, B, tok)
            c = self.pcol(l, "w_conv")
            cb = self.pcol(l, "b_conv")
            conv = (lambda j, f, c=c: t["PAR"][:, c + 22 * j + f:c + 22 * j + f + 1],
                    lambda f, cb=cb: t["PAR"][:, cb + f:cb + f + 1])

            def fill_next(l=l):
                if l + 1 < DEPTH:
                    for q in range(12):
                        yield from self.ada(l + 1, q)
            weave(self.ffn_up(I["w_up"][l], 0, I["w_up"][l], FF, conv), fill_next(), 1)
            drain(self.out_proj(I["w_down"][l], KF, t["FH"], t["FL"], self.ff_tok, t["MOD"][:, l, 40:48]))
            self.x_sums(KD - 1)
            self.big_order = ["b0", "b1", "b2"]
        self.big_order = ["b0", "b1", "b2", "o", "s0", "s1"]
        self.x_norm(t["PAR"][:, 512:520], None, self.par_tok)
        drain(self.pool_mixer())
        self.x_sums(KD - 1)
        self.x_norm(t["PAR"][:, 528:536], None, self.par_tok)
        drain(self.ffn_up(I["ffn_w_gate_2"][0], 0, I["ffn_w_up_2"][0], 0, None))
        drain(self.out_proj(I["ffn_w_down_2"][0], KF, t["FH"], t["FL"], self.ff_tok, None))
        self.x_sums(KD - 1)
        self.big_order = ["b0", "b1", "b2"]
        prev = self.last
        self.x_norm(t["PAR"][:, 520:528], None, self.par_tok)
        self.tab_tok = [self.load(t["cos2"][:, :], T["cos2"], prev), self.load(t["sin2"][:, :], T["sin2"], prev)]
        drain(self.attn_inputs())
        drain(self.attn_heads())
        self.attn_merge()
        self.big_order = ["b0", "b1", "b2", "o", "s0", "s1"]
        drain(self.out_proj(I["attn_w_out_2"][0], 8, t["YH"], t["YL"], self.y_tok, None))
        self.x_sums(KD - 1)
        self.x_norm(t["PAR"][:, 536:544], None, self.par_tok)
        drain(self.ffn_up(I["ffn_w_gate_2"][1], 0, I["ffn_w_up_2"][1], 0, None))
        drain(self.out_proj(I["ffn_w_down_2"][1], KF, t["FH"], t["FL"], self.ff_tok, None))
        self.x_sums(KD - 1)
        self.finish()


def places(nc):
    with ExitStack() as ctx:
        base = (nc.sbuf_base + 63) // 64 * 64
        TB = S * 4
        ctx.enter_context(nc.sbuf_tensor("arena", [128, (nc.sbuf_usable_end - base) // 4 - 64], F32))
        at = [base]
        t = {}

        def fixed(name, shape, dt=F32):
            n = int(np.prod(shape[1:])) * 4
            t[name] = nc.alloc_sbuf_tensor_at(name, shape, dt, offset=at[0])
            at[0] += (n + 31) // 32 * 32

        fixed("X", [128, 8, S])
        fixed("HH", [128, 8, S], F32R)
        fixed("HL", [128, 8, S], F32R)
        raw = nc.alloc_sbuf_tensor_at("raw", [128, NSLOT, 1024], F32, offset=at[0])
        fixed("lo", [128, NSLOT, 1024], F32R)
        fixed("hi", [128, NSLOT, 1024], F32R)
        for name, n in (("ident", 128), ("center", 128), ("causal", 128), ("tail", 128), ("window", 256), ("dil", 128),
                        ("chunk", 2), ("CT", 64), ("sel", 512), ("PAR", 640), ("ones", 2), ("eps", 2),
                        ("CA", 8), ("RS", 16), ("RS2", 32), ("GQ", 2), ("BF", 2), ("foxM", 16), ("foxR", 16),
                        ("AD", 16), ("aM", 64), ("aNM", 64), ("aDEN", 64), ("aR", 64), ("aL", 64)):
            fixed(name, [128, n])
        fixed("WA", [128, 256])
        t["one"], t["aLT"] = t["ones"], t["aNM"]
        fixed("MOD", [128, 2, 48])
        fixed("NA", [128, 4, 8])
        fixed("aG", [128, 9, 4])
        fixed("AA", [128, S])
        big = at[0]
        assert big + 49 * TB <= nc.sbuf_usable_end, big + 49 * TB - nc.sbuf_usable_end

        def area(name, tile, shape, dt=F32):
            t[name] = nc.alloc_sbuf_tensor_at(name, shape, dt, offset=big + int(tile * TB))
            assert big + int(tile * TB) + int(np.prod(shape[1:])) * 4 <= big + 49 * TB, name

        area("SQ", 44, [128, 2, S])
        area("NT", 46, [128, 3, S])
        area("XS", 0, [128, 4, D])
        area("PST", 20, [128, 5, 128])
        area("rq", 0, [128, 4, S])
        area("rk", 4, [128, 4, S])
        area("rv", 8, [128, 4, S])
        area("fq", 12, [128, 4, S])
        area("fk", 16, [128, 4, S])
        area("fv", 20, [128, 4, S])
        area("RO", 24, [128, 4, S])
        area("EfH", 28, [128, 4, S], F32R)
        area("EfL", 32, [128, 4, S], F32R)
        area("cos1", 36, [128, S])
        area("sin1", 37, [128, S])
        area("decay", 38, [128, 4 * S])
        area("rT", 28, [128, 2, S])
        area("retP", 42, [128, 2, S])
        area("retO", 44, [128, 2, S])
        area("retS", 30, [128, 2, S])
        area("foxS", 32, [128, 2, S])
        area("GLR", 46, [128, S])
        area("FFR", 47, [128, S])
        area("FFT", 48, [128, S])
        area("foxP", 37, [128, 2, S])
        area("foxT", 39, [128, 2, S])
        area("foxD", 41, [128, 2, 128])
        area("gk", 0, [128, 4, 256])
        area("gv", 2, [128, 4, S])
        area("gq", 6, [128, 2, S])
        area("SA", 8, [128, 2, 8, 128])
        area("GO", 20, [128, 4, S])
        area("ErH", 12, [128, 4, S], F32R)
        area("ErL", 16, [128, 4, S], F32R)
        area("EgH", 0, [128, 4, S], F32R)
        area("EgL", 4, [128, 4, S], F32R)
        area("LA", 37, [128, 2, S])
        area("TA", 39, [128, 2, S])
        area("ED", 41, [128, 2, S])
        area("glaS", 43, [128, 2, S])
        area("GT", 47, [128, 2, S])
        area("MH", 36, [128, 8, S], F32R)
        area("ML", 20, [128, 8, S], F32R)
        area("SG", 8, [128, 2, S])
        area("MX", 10, [128, 2, S])
        area("FH", 0, [128, KF, S], F32R)
        area("FL", KF, [128, KF, S], F32R)
        area("CB", 44, [128, 2, S])
        area("PH", 0, [128, 8, S], F32R)
        area("PL", 8, [128, 8, S], F32R)
        area("ZH", 16, [128, 8, S], F32R)
        area("ZL", 24, [128, 8, S], F32R)
        area("U", 32, [128, 2, S])
        area("W1", 34, [128, 2, S])
        area("W2", 36, [128, 2, S])
        area("aq", 0, [128, 8, S])
        area("ak", 8, [128, 8, S])
        area("av", 16, [128, 4, D])
        area("MO", 24, [128, 8, S])
        area("cos2", 32, [128, S])
        area("sin2", 33, [128, S])
        area("aT", 34, [128, 2, S])
        area("aS", 36, [128, 4, 256])
        area("aP", 38, [128, 4, 256])
        area("aPT", 40, [128, 4, 256])
        area("aD", 42, [128, 4, 128])
        area("ALP", 32, [128, 3, S])
        area("aTM", 35, [128, 2, S])
        area("aE", 37, [128, 3, S])
        area("YH", 0, [128, 8, S], F32R)
        area("YL", 8, [128, 8, S], F32R)
        area("OT", 0, [128, 4, D])

        bank = {b: ctx.enter_context(nc.psum_tensor(b, [128, S], F32))
                for b in ("b0", "b1", "b2", "s0", "s1", "t0", "t1", "o")}
        return ctx.pop_all(), t, raw, bank


def build(nc, I, T, out):
    stack, t, raw, bank = places(nc)
    with stack as ctx:
        mem = {"raw": raw, "hi": t["hi"], "lo": t["lo"], "t": t, "bank": bank, "tables": T}

        def sem(name):
            return ctx.enter_context(nc.semaphore(name))

        sems = (sem("s_pe"), sem("s_ve"), sem("s_ac"), sem("s_po"), [sem(f"s_ring{i}") for i in range(NSLOT + 2)],
                [sem(f"s_misc{i}") for i in range(16)], [sem(f"s_out{i}") for i in range(4)])
        draft = Program(nc, I, out, sems, mem, None)
        draft.run()
        p = Program(nc, I, out, sems, mem, draft.descs)
        p.run()
        block = ctx.enter_context(nc.Block())

        @block.sync
        def _(e):
            p.sp.emit(e)

        @block.tensor
        def _(e):
            p.pe.emit(e)

        @block.vector
        def _(e):
            p.ve.emit(e)

        @block.scalar
        def _(e):
            p.ac.emit(e)

        @block.gpsimd
        def _(e):
            p.po.emit(e)


_INS = ['x', 'c', 'norm1_g', 'norm2_g', 'w_ada', 'b_ada', 'w_in', 'w_gla_a2', 'b_gla_a', 'b_fox_f', 'ret_norm_g',
        'gla_norm_g', 'q_norm_g', 'k_norm_g', 'w_br', 'w_mg', 'b_mg', 'w_o', 'w_up', 'w_conv', 'b_conv', 'w_down',
        'norm_mix_2', 'norm_ffn_2', 'norm_final_2', 'pool_w_in_2', 'pool_w_group_2', 'pool_scale_2', 'pool_w_out_2',
        'attn_w_qkv_2', 'attn_w_out_2', 'ffn_w_gate_2', 'ffn_w_up_2', 'ffn_w_down_2']
_OUTS = [((1, 512, 1024), 'float32')]


def kernel(**inputs):
    import numpy as _np
    import concourse.bacc as _bacc
    from concourse import mybir as _mybir
    from concourse.bass_utils import run_bass_kernel_spmd as _run

    nc = _bacc.Bacc("TRN2", target_bir_lowering=False, num_devices=1)
    arrays, ins, tabs = {}, {}, {}
    for name in _INS:
        a = _np.ascontiguousarray(inputs[name])
        arrays[f"in_{name}_dram"] = a
        ins[name] = nc.dram_tensor(f"in_{name}_dram", a.shape, _mybir.dt.from_np(a.dtype), kind="ExternalInput").ap()
    for name, a in tables().items():
        arrays[f"tab_{name}_dram"] = a
        tabs[name] = nc.dram_tensor(f"tab_{name}_dram", a.shape, _mybir.dt.from_np(a.dtype), kind="ExternalInput").ap()
    shape, dtype = _OUTS[0]
    out = nc.dram_tensor("out_0_dram", shape, _mybir.dt.from_np(_np.dtype(dtype)), kind="ExternalOutput").ap()
    build(nc, ins, tabs, out)
    r = _run(nc, [arrays], core_ids=[0])
    return r.results[0]["out_0_dram"]
```

```python
from contextlib import ExitStack

import concourse.bass as bass
import numpy as np
from concourse import mybir

F32 = mybir.dt.float32
F32R = mybir.dt.float32r
ALU = mybir.AluOpType
ACT = mybir.ActivationFunctionType
AXX = mybir.AxisListType.X

S = 512
D = 1024
KD = D // 128
FF = 2816
KF = FF // 128
DEPTH = 2
EPS = 1e-6
NSLOT = 6
AHEAD = 3
NEG = -1e30
COL_A = [("b_ada", 48), ("b_mg", 24), ("norm1_g", 8), ("norm2_g", 8), ("ret_norm_g", 4), ("gla_norm_g", 1),
         ("q_norm_g", 1), ("k_norm_g", 1), ("b_conv", 22)]


CON = [("ident", 128), ("center", 128), ("causal", 128), ("tail", 128), ("window", 256), ("dil", 128), ("chunk", 2),
       ("CT", 64), ("sel", 512)]
CON_W = sum(n for _, n in CON)


def tables():
    i = np.arange(128)
    out = {}
    out["ident"] = np.eye(128)
    out["center"] = np.eye(128) - 1.0 / 128
    out["causal"] = np.where(i[:, None] >= i[None, :], 0.0, NEG)
    out["tail"] = ((i[:, None] // 64 == i[None, :] // 64) & (i[:, None] > i[None, :])) * 1.0
    out["chunk"] = (i[:, None] // 64 == np.arange(2)[None, :]) * 1.0
    kj = np.arange(256)
    dist = 128 + i[:, None] - kj[None, :]
    out["window"] = np.where((dist >= 0) & (dist <= 128), 0.0, NEG)
    out["dil"] = np.where((i[:, None] >= i[None, :]) & ((i[:, None] - i[None, :]) % 4 == 0), 0.0, NEG)
    out["sel"] = np.concatenate([np.zeros((96, 512)), np.repeat(np.eye(4), 128, axis=1), np.zeros((28, 512))])
    t = np.arange(S, dtype=np.float64)
    f = 10000.0 ** (-np.arange(64) / 64.0)
    ang = f[:, None] * t[None, :]
    out["cos1"] = np.concatenate([np.cos(ang), np.cos(ang)])
    out["sin1"] = np.concatenate([np.sin(ang), -np.sin(ang)])
    f = 10000.0 ** (-np.arange(32) / 32.0)
    ang = f[:, None] * t[None, :]
    out["cos2"] = np.concatenate([np.cos(ang)] * 4)
    out["sin2"] = np.concatenate([np.sin(ang), -np.sin(ang)] * 2)
    lg = np.log1p(-np.exp2(-5.0 - np.arange(4)))
    q = np.arange(S)[None, :]
    j = i[:, None]
    live = (q // 64) >= (j // 64)
    dec = [np.where(live, np.exp(np.abs(q - j) * g), 0.0) * 128 ** -0.5 for g in lg]
    out["decay"] = np.concatenate(dec, axis=1)
    cnt = [np.broadcast_to(1.0 / np.minimum(np.arange(16) + 1, w), (128, 16)) for w in (2, 4, 8, 16)]
    out["CT"] = np.concatenate(cnt, axis=1)
    out["con"] = np.concatenate([out.pop(name) for name, _ in CON], axis=1)
    return {k: np.ascontiguousarray(v, dtype=np.float32) for k, v in out.items()}


BUSY = "busy"


class Lane:

    def __init__(self, sem):
        self.sem, self.queue, self.count, self.seen = sem, [], 0, {}

    def wait(self, *toks):
        for tok in toks:
            if tok is None:
                continue
            if isinstance(tok, list) or isinstance(tok[0], tuple) or tok[0] is None:
                self.wait(*tok)
                continue
            sem, value = tok
            if self.seen.get(id(sem), 0) < value:
                self.seen[id(sem)] = value
                self.queue.append(lambda e, s=sem, v=value: e.wait_ge(s, v))

    def go(self, fn, *toks):
        self.wait(*toks)
        self.queue.append(fn)

    def __call__(self, fn, *toks):
        self.wait(*toks)
        self.count += 1
        self.queue.append(lambda e, s=self.sem: fn(e).then_inc(s, 1))
        return (self.sem, self.count)

    def emit(self, e):
        for f in self.queue:
            f(e)


class Flow:

    def __init__(self, lane, sem):
        self.lane, self.sem, self.count = lane, sem, 0

    def __call__(self, out, in_, *toks):
        self.lane.wait((self.sem, self.count) if self.count else None, *toks)
        self.count += 16
        self.lane.queue.append(lambda e, s=self.sem: e.dma_start(out, in_).then_inc(s, 16))
        return (self.sem, self.count)


def bc(col, n):
    return col.to_broadcast([col.shape[0], n])


def drain(gen):
    for _ in gen:
        pass


def weave(main, fill, per=1, whole=True):
    for step in main:
        for _ in range(per if step is not BUSY else 0):
            next(fill, None)
    if whole:
        drain(fill)


class Program:
    def __init__(self, nc, I, out, sems, mem, plan):
        self.nc, self.I, self.out, self.mem, self.plan = nc, I, out, mem, plan
        (s_pe, s_ve, s_ac, s_po, s_ring, s_misc, s_out) = sems
        self.pe, self.ve, self.ac, self.po = Lane(s_pe), Lane(s_ve), Lane(s_ac), Lane(s_po)
        self.sp = Lane(None)
        self.ring_flow = [Flow(self.sp, s) for s in s_ring]
        self.misc = [Flow(self.sp, s) for s in s_misc]
        self.mi = 0
        self.out_flow = [Flow(self.sp, s) for s in s_out]
        self.descs = []
        self.n_dma = 0
        self.n_split = 0
        self.dma_tok, self.split_tok, self.done_tok = {}, {}, {}
        self.free = {b: None for b in mem["bank"]}
        self.big_order = ["b0", "b1", "b2"]
        self.big_i = 0
        self.HT = [None] * KD
        self.t = mem["t"]

    def load(self, out, in_, *toks):
        f = self.misc[self.mi % len(self.misc)]
        self.mi += 1
        return f(out, in_, *toks)

    def need(self, desc, pair=False):
        n = len(self.descs)
        if pair and n % NSLOT == NSLOT - 1:
            self.descs.append(None)
            n += 1
        self.descs.append(desc)
        self.pump(n)
        return n

    def pump(self, n):
        plan = self.plan if self.plan is not None else self.descs
        def freed(m):
            m -= NSLOT
            if m >= 0 and plan[m] is None:
                m -= NSLOT
            return (True, None) if m < 0 else (m in self.done_tok, self.done_tok.get(m))

        while self.n_dma < len(plan) and self.n_dma <= n + NSLOT - 1:
            m = self.n_dma
            known, free = freed(m)
            if not known:
                break
            if plan[m] is not None:
                s = m % NSLOT
                for sub, (dst, src) in enumerate(plan[m][1]):
                    f = self.ring_flow[s if sub == 0 else NSLOT + sub - 1]
                    tok = f(dst(self.mem["raw"][:, s, :]), src, free)
                    self.dma_tok.setdefault(m, []).append(tok)
            self.n_dma += 1
        while self.n_split < self.n_dma and self.n_split <= n + AHEAD:
            m = self.n_split
            if plan[m] is not None and plan[m][0]:
                s = m % NSLOT
                w = plan[m][2]
                raw, hi, lo = (self.mem[x][:, s, 0:w] for x in ("raw", "hi", "lo"))
                th = self.ac(lambda e, o=hi, i=raw: e.activation(o, i, ACT.Copy), self.dma_tok[m], freed(m)[1])
                self.split_tok[m] = self.po(
                    lambda e, o=lo, i=raw, h=hi: e.tensor_tensor(o, i, h.bitcast(F32), ALU.subtract), th)
            elif plan[m] is not None:
                self.split_tok[m] = self.dma_tok[m]
            self.n_split += 1
        assert n in self.split_tok

    def weight(self, ap, r0, kt, c0, w, pair=False):
        src = ap[r0:r0 + kt * 128, c0:c0 + w].rearrange("(k p) c -> p k c", p=128)
        return self.need((True, [(lambda r, kt=kt, w=w: r[:, 0:kt * w].rearrange("p (k c) -> p k c", k=kt), src)],
                          kt * w), pair)

    def views(self, n, kt, w):
        s = n % NSLOT
        return tuple(self.mem[x][:, s, 0:kt * w].rearrange("p (k c) -> p k c", k=kt) for x in ("hi", "lo"))

    def pair_views(self, n):
        s = n % NSLOT
        return tuple(self.mem[x][:, s:s + 2, :].rearrange("p h (k c) -> p h k c", k=8) for x in ("hi", "lo"))

    def bank(self):
        b = self.big_order[self.big_i % len(self.big_order)]
        self.big_i += 1
        before, self.free[b] = self.free[b], BUSY
        assert before is not BUSY
        return b, before

    def dot(self, out, terms, start=True, stop=True, toks=()):
        tok = None
        total = len(terms)
        for k, (wh, wl, xh, xl, t) in enumerate(terms):
            self.pe.wait(t, list(toks) if k == 0 else None)
            for a, (w, x) in enumerate(((wh, xh), (wh, xl), (wl, xh))):
                first = start and k == 0 and a == 0
                last = stop and k == total - 1 and a == 2
                f = lambda e, w=w, x=x, fi=first, la=last: e.matmul(out, w, x, start=fi, stop=la)
                if k == total - 1 and a == 2:
                    tok = self.pe(f)
                else:
                    self.pe.go(f)
            if k % 4 == 3 and k != total - 1:
                yield None
        self.last = tok
        yield None
        return tok

    def project(self, ap, c0, then):
        n = self.weight(ap, 0, 8, c0, 128)
        hi, lo = self.views(n, 8, 128)
        yield from self.tile_of(n, hi, lo, then)

    def projects(self, jobs, group=3):
        HH, HL = self.t["HH"], self.t["HL"]
        first = []
        for ap, c0, then in jobs[:group]:
            n = self.weight(ap, 0, 8, c0, 128)
            b, fr = self.bank()
            first.append((n, *self.views(n, 8, 128), self.mem["bank"][b], b, fr, then))
        for hf in range(2):
            c = slice(256 * hf, 256 * hf + 256)
            for k in range(8):
                if hf == 0 and k in (3, 5):
                    next(self.norm)
                for n, hi, lo, out, b, fr, then in first:
                    self.pe.wait(self.H2[hf][k], (self.split_tok[n], fr) if k == 0 else None)
                    for a, (w, x) in enumerate(((hi, HH), (hi, HL), (lo, HH))):
                        f = lambda e, out=out, w=w, x=x, k=k, a=a, c=c: e.matmul(
                            out[:, c], w[:, k, :], x[:, k, c], start=(k == 0 and a == 0), stop=(k == 7 and a == 2))
                        tok = self.pe(f) if k == 7 and a == 2 else self.pe.go(f)
                    if hf == 1 and k == 7:
                        self.done_tok[n] = tok
                        self.free[b] = then(out, tok)
        self.HT = self.H2[1]
        yield None
        for job in jobs[group:]:
            yield from self.project(*job)

    def tile_of(self, n, hi, lo, then):
        b, fr = self.bank()
        out = self.mem["bank"][b]
        HH, HL = self.t["HH"], self.t["HL"]
        terms = [(hi[:, k, :], lo[:, k, :], HH[:, k, :], HL[:, k, :], self.HT[k]) for k in range(8)]
        tok = yield from self.dot(out[:, :], terms, toks=(self.split_tok[n], fr))
        self.done_tok[n] = tok
        self.free[b] = then(out, tok)

    def project_rows(self, ap, c0, then, rows=None):
        na = self.weight(ap, 0, 8, c0, 128, pair=True)
        nb = self.weight(ap, 0, 8, c0 + 128, 128)
        assert nb == na + 1 and na % NSLOT != NSLOT - 1
        hi, lo = self.pair_views(na)
        HH, HL = self.t["HH"], self.t["HL"]
        for u in range(2):
            b, fr = self.bank()
            out = self.mem["bank"][b]
            for t in (2 * u, 2 * u + 1):
                pick = slice(t * 128, t * 128 + 128) if rows is None else rows(t)
                terms = [(HH[:, k, pick], HL[:, k, pick], hi[:, :, k, :], lo[:, :, k, :], self.HT[k])
                         for k in range(8)]
                o = out[:, (t % 2) * 256:(t % 2) * 256 + 256]
                tok = yield from self.dot(o, terms, toks=(self.split_tok[na], self.split_tok[nb], fr))
            self.free[b] = then(out, tok, u)
        self.done_tok[na] = self.done_tok[nb] = tok

    def project_rows_half(self, ap, c0, then, rows=None):
        n = self.weight(ap, 0, 8, c0, 128)
        hi, lo = self.views(n, 8, 128)
        HH, HL = self.t["HH"], self.t["HL"]
        b, fr = self.bank()
        out = self.mem["bank"][b]
        for t in range(4):
            pick = slice(t * 128, t * 128 + 128) if rows is None else rows(t)
            terms = [(HH[:, k, pick], HL[:, k, pick], hi[:, k, :], lo[:, k, :], self.HT[k]) for k in range(8)]
            tok = yield from self.dot(out[:, t * 128:t * 128 + 128], terms, toks=(self.split_tok[n], fr))
        self.done_tok[n] = tok
        self.free[b] = then(out, tok)

    def colsq(self, sq, st, col, tok, start=True, stop=True, check=False):
        ones = self.t["ones"]
        for t in range(4):
            f = lambda e, t=t: e.matmul(st[:, col + t:col + t + 1], sq[:, t * 128:t * 128 + 128], ones[:, 0:1],
                                        start=start if not check else (start and t == 0), stop=stop,
                                        skip_group_check=check)
            if t == 3:
                return self.pe(f, tok)
            self.pe.go(f, tok)

    def rstd(self, st, col, n, width, tok, out):
        a = self.ac(lambda e: e.activation(out, st[:, col:col + n], ACT.Sqrt, bias=self.t["eps"][:, 0:1],
                                           scale=1.0 / width), tok)
        return self.ve(lambda e: e.reciprocal(out, out), a), a

    def spread(self, cols, bank, tok, n=4):
        out = self.mem["bank"][bank]
        ident = self.t["ident"]
        self.pe.wait(tok, self.free[bank])
        for t in range(n):
            f = lambda e, t=t: e.transpose(out[:, t * 128:t * 128 + 128], bc(cols[:, t:t + 1], 128), ident[:, :])
            if t == n - 1:
                return self.pe(f)
            self.pe.go(f)

    def x_update(self, d, bank, tok, gate, c):
        X = self.t["X"]
        out = self.mem["bank"][bank]
        if gate is None:
            a = self.ve(lambda e: e.tensor_tensor(X[:, d, c], out[:, c], X[:, d, c], ALU.add), tok)
        else:
            a = self.ve(lambda e: e.scalar_tensor_tensor(out=X[:, d, c], in0=out[:, c], scalar=gate, in1=X[:, d, c],
                                                         op0=ALU.mult, op1=ALU.add), tok)
        self.free[bank] = a
        self.square(d, a, c)

    def square(self, d, tok, c):
        X, SQ, SS = (self.t[k] for k in ("X", "SQ", "SS"))
        if self.late is not None:
            self.late()
            self.late = None
        i = d % 2
        if d == 0:
            self.ss_tok = self.ac(lambda e: e.activation(SS[:, c], X[:, d, c], ACT.Square), tok, self.ss_used)
            return
        q = self.ac(lambda e: e.activation(SQ[:, i, c], X[:, d, c], ACT.Square), tok, self.sq_used[i])
        if d == KD - 1:
            self.sq_tok = q
            return

        def late():
            self.ss_tok = self.sq_used[i] = self.ve(
                lambda e: e.tensor_tensor(SS[:, c], SS[:, c], SQ[:, i, c], ALU.add), q, self.ss_tok)
        self.late = late

    def sums(self, hf):
        SQ, SS, RS, ones = (self.t[k] for k in ("SQ", "SS", "RS", "ones"))
        b = ("t1", "s1")[hf]
        st = self.mem["bank"][b]
        assert self.late is None
        self.pe.wait(self.ss_tok, self.sq_tok, self.free[b])
        for t in range(2):
            c = slice(256 * hf + 128 * t, 256 * hf + 128 * t + 128)
            self.pe.go(lambda e, t=t, c=c: e.matmul(st[:, t:t + 1], SS[:, c], ones[:, 0:1], start=True, stop=False))
            p = self.pe(lambda e, t=t, c=c: e.matmul(st[:, t:t + 1], SQ[:, 1, c], ones[:, 0:1], start=False, stop=True))
        self.ss_used = self.sq_used[1] = p
        r, self.free[b] = self.rstd(st, 0, 2, D, p, RS[:, 2 * hf:2 * hf + 2])
        return r

    def x_norm(self, A, B, at):
        X, HH, HL, NT, RS = (self.t[k] for k in ("X", "HH", "HL", "NT", "RS"))
        for hf in range(2):
            r = self.sums(hf)
            yield None
            b = ("t0", "s0")[hf]
            sp = self.spread(RS[:, 2 * hf:2 * hf + 2], b, r, 2)
            row = self.mem["bank"][b]
            c = slice(256 * hf, 256 * hf + 256)
            toks, out = {}, [None] * KD

            def scale(k, c=c, row=row, sp=sp, toks=toks, b=b):
                i = k % 4
                v = self.ve(lambda e: e.scalar_tensor_tensor(out=NT[:, i, :], in0=X[:, k, c], scalar=A[:, k:k + 1],
                                                             in1=row[:, 0:256], op0=ALU.mult, op1=ALU.mult),
                            sp, at, self.nt_used[i])
                if B is None:
                    toks[k] = self.ac(lambda e: e.activation(HH[:, k, c], NT[:, i, :], ACT.Copy), v)
                else:
                    toks[k] = self.ac(lambda e: e.activation(HH[:, k, c], NT[:, i, :], ACT.Identity,
                                                             bias=B[:, k:k + 1]), v, at)
                self.free[b] = v

            def rest(k, c=c, toks=toks, out=out):
                i = k % 4
                if B is None:
                    l = self.ve(lambda e: e.tensor_tensor(HL[:, k, c], NT[:, i, :], HH[:, k, c].bitcast(F32),
                                                          ALU.subtract), toks[k])
                else:
                    l = self.ve(lambda e: e.scalar_tensor_tensor(out=HL[:, k, c], in0=NT[:, i, :],
                                                                 scalar=B[:, k:k + 1], in1=HH[:, k, c].bitcast(F32),
                                                                 op0=ALU.add, op1=ALU.subtract), toks[k])
                out[k] = self.nt_used[i] = l

            for k in range(KD + 1):
                if k < KD:
                    scale(k)
                if k:
                    rest(k - 1)
            self.H2[hf] = out
            yield None

    def ada(self, l, q, late=3):
        w = self.I["w_ada"][l]
        AA, MOD, CA, ones, PAR = (self.t[k] for k in ("AA", "MOD", "CA", "ones", "PAR"))
        v = None
        for g in range(4):
            src = w[g * 256:(g + 1) * 256, q * 512:(q + 1) * 512].rearrange("(k p) c -> p k c", p=128)
            n = self.need((False, [(lambda r: r.rearrange("p (k c) -> p k c", k=2), src)], 1024))
            raw = self.mem["raw"][:, n % NSLOT, :]
            for k in range(2):
                kk = 2 * g + k
                if kk == 0:
                    v = self.ve(lambda e, r=raw: e.tensor_scalar(AA[:, :], r[:, 0:512], CA[:, 0:1], None, ALU.mult),
                                self.split_tok[n], self.ca_tok, self.aa_used)
                else:
                    v = self.ve(lambda e, r=raw, k=k, kk=kk: e.scalar_tensor_tensor(
                        out=AA[:, :], in0=r[:, k * 512:k * 512 + 512], scalar=CA[:, kk:kk + 1], in1=AA[:, :],
                        op0=ALU.mult, op1=ALU.add), self.split_tok[n], v)
            self.done_tok[n] = v
            yield None
        for _ in range(late):
            yield None
        b, fr = self.bank()
        out = self.mem["bank"][b]
        self.pe.wait(v, fr)
        for j in range(4):
            f = lambda e, j=j: e.matmul(out[:, j:j + 1], AA[:, j * 128:j * 128 + 128], ones[:, 0:1], start=True,
                                        stop=True)
            p = self.pe(f)
        self.aa_used = p
        c = self.pcol(l, "b_ada")
        self.free[b] = self.mod_tok = self.ve(
            lambda e: e.tensor_tensor(MOD[:, l, 4 * q:4 * q + 4], out[:, 0:4], PAR[:, c + 4 * q:c + 4 * q + 4],
                                      ALU.add), p, self.par_tok)
        yield None

    def ada_row(self, l, q):
        w = self.I["w_ada"][l]
        AA, MOD, CA, ones, PAR = (self.t[k] for k in ("AA", "MOD", "CA", "ones", "PAR"))
        b, fr = self.bank()
        out = self.mem["bank"][b]
        self.pe.wait(self.ca_tok, fr)
        for g in range(4):
            src = w[g * 256:(g + 1) * 256, q * 512:(q + 1) * 512].rearrange("(k p) c -> p k c", p=128)
            n = self.need((False, [(lambda r: r.rearrange("p (k c) -> p k c", k=2), src)], 1024))
            raw = self.mem["raw"][:, n % NSLOT, :]
            for k in range(2):
                kk = 2 * g + k
                p = self.pe(lambda e, raw=raw, k=k, kk=kk: e.matmul(
                    out[0:1, :], CA[:, kk:kk + 1], raw[:, k * 512:k * 512 + 512], start=(kk == 0), stop=(kk == 7)),
                    self.split_tok[n])
            self.done_tok[n] = p
            yield None
        self.free[b] = a = self.ac(lambda e: e.activation(AA[0:1, :], out[0:1, :], ACT.Copy), p, self.aa_used)
        yield None
        b, fr = self.bank()
        col = self.mem["bank"][b]
        self.pe.wait(a, fr)
        for j in range(4):
            p = self.pe(lambda e, j=j: e.matmul(col[:, j:j + 1], AA[0:1, j * 128:j * 128 + 128], ones[0:1, 0:1],
                                                start=True, stop=True))
        self.aa_used = p
        c = self.pcol(l, "b_ada")
        self.free[b] = self.mod_tok = self.ve(
            lambda e: e.tensor_tensor(MOD[:, l, 4 * q:4 * q + 4], col[:, 0:4], PAR[:, c + 4 * q:c + 4 * q + 4],
                                      ALU.add), p, self.par_tok)
        yield None

    def pcol(self, l, name):
        c = l * 256
        for key, n in COL_A:
            if key == name:
                return c
            c += n
        assert name == "w_conv"
        return l * 256 + 128

    def rope_pieces(self, out, dst, tmp, cos, sin, half, scale, tok, tt, used):
        a = self.ve(lambda e: e.scalar_tensor_tensor(out=dst, in0=out[:, :], scalar=scale, in1=cos, op0=ALU.mult,
                                                     op1=ALU.mult), tok, tt, used)
        for p in range(0, 128, 2 * half):
            for d, s in ((p, p + half), (p + half, p)):
                b = self.ve(lambda e, d=d, s=s: e.scalar_tensor_tensor(
                    out=tmp[d:d + half, :], in0=out[s:s + half, :], scalar=scale, in1=sin[s:s + half, :],
                    op0=ALU.mult, op1=ALU.mult), used)
        return b, self.ve(lambda e: e.tensor_tensor(dst, dst, tmp, ALU.add), a, b)

    def ret_attention(self):
        q, k, v, O, dec = (self.t[x] for x in ("rq", "rk", "rv", "RO", "decay"))
        PT, OS, SQ, RS, PAR = (self.t[x] for x in ("retP", "retO", "retS", "RS", "PAR"))
        bank, free, pe, ve, ac = self.mem["bank"], self.free, self.pe, self.ve, self.ac
        steps = [(h, j) for h in range(4) for j in range(4)]
        st = {}
        used = [None] * 4

        def score(n):
            h, j = steps[n]
            b = f"s{n % 2}"
            w = S - 128 * j
            p = pe(lambda e: e.matmul(bank[b][:, 0:w], k[:, h, j * 128:j * 128 + 128], q[:, h, j * 128:S], start=True,
                                      stop=True), self.rk_tok[h], self.rq_tok[h], free[b])
            free[b] = st[n] = ve(lambda e: e.tensor_tensor(PT[:, n % 4, 0:w], bank[b][:, 0:w],
                                                           dec[:, h * S:h * S + w], ALU.mult), p, used[n % 4],
                                 self.dec_tok)

        def value(n):
            h, j = steps[n]
            w = S - 128 * j
            f = lambda e: e.matmul(bank["o"][:, j * 128:S], v[:, j, h * 128:h * 128 + 128], PT[:, n % 4, 0:w],
                                   start=(j == 0), stop=(j == 3))
            used[n % 4] = pe(f, st[n], self.rv_tok, free["o"] if j == 0 else None)
            if j == 3:
                free["o"] = st["o", h] = ac(lambda e: e.activation(OS[:, h % 2, :], bank["o"][:, :], ACT.Copy),
                                            used[n % 4], st.get(("xc", h - 2)))

        def center(h):
            st["xc", h] = pe(lambda e: e.matmul(bank["t0"][:, :], self.t["center"][:, :], OS[:, h % 2, :], start=True,
                                                stop=True), st["o", h], free["t0"])
            a = ac(lambda e: e.activation(SQ[:, h % 2, :], bank["t0"][:, :], ACT.Square), st["xc", h],
                   st.get(("sq", h - 2)))
            free["t0"] = ve(lambda e: e.tensor_copy(O[:, h, :], bank["t0"][:, :]), a)
            st["s", h] = a

        def sums(h):
            st["sq", h] = self.colsq(SQ[:, h % 2, :], bank["t1"], 4 * h, [st["s", h], free["t1"]])

        for n in range(len(steps) + 8):
            if n < len(steps):
                score(n)
            if 2 <= n <= len(steps) + 1:
                value(n - 2)
            if n >= 6 and (n - 6) % 4 == 0 and (n - 6) // 4 < 4:
                center((n - 6) // 4)
            if n >= 7 and (n - 7) % 4 == 0 and (n - 7) // 4 < 4:
                sums((n - 7) // 4)
            yield None
        r, a = self.rstd(bank["t1"], 0, 16, 128, st["sq", 3], RS[:, 0:16])
        free["t1"] = a
        yield None
        c = self.pcol(self.l, "ret_norm_g")
        self.ro_tok = [None] * 4
        for h in range(4):
            b = f"t{h % 2}"
            s = self.spread(RS[:, 4 * h:4 * h + 4], b, r)
            free[b] = self.ro_tok[h] = ve(lambda e, h=h, b=b: e.scalar_tensor_tensor(
                out=O[:, h, :], in0=O[:, h, :], scalar=PAR[:, c + h:c + h + 1], in1=bank[b][:, :], op0=ALU.mult,
                op1=ALU.mult), s)
            yield None

    def fox_inputs(self, w):
        bank, pe, ve, ac = self.mem["bank"], self.pe, self.ve, self.ac
        q, k, v, SQ, RS2 = (self.t[x] for x in ("fq", "fk", "fv", "foxS", "RS2"))
        GLR, FFR, FFT, bf = (self.t[x] for x in ("GLR", "FFR", "FFT", "BF"))
        st = bank["b2"]
        sq_used = [None, None]
        prev = []
        l = self.l

        srcs = []
        for (d0, c0, n) in ((0, 3072, 96), (96, 5136, 4), (100, 3168, 28)):
            src = w[:, c0:c0 + n].rearrange("(k p) c -> p k c", p=128)
            srcs.append((lambda r, d0=d0, n=n: r.rearrange("p (k c) -> p k c", k=8)[:, :, d0:d0 + n], src))
        n = self.need((True, srcs, 1024))
        hi, lo = self.views(n, 8, 128)

        def small(out, tok):
            m = self.po(lambda e: e.memset(GLR[0:32, :], 1.0), self.glr_used, self.HT)
            m = self.po(lambda e: e.memset(FFT[:, :], 0.0), self.ffr_used)
            g = ve(lambda e: e.tensor_copy(GLR[0:16, :], out[0:16, :]), tok, m)
            self.glr_tok = g
            z = slice(96, 100)
            f = ve(lambda e: e.tensor_scalar(FFR[z, :], out[z, :], bf[z, l:l + 1], None, ALU.add), g,
                   self.par_tok, self.ffr_used)
            a = ac(lambda e: e.activation(FFT[z, :], FFR[z, :], ACT.Abs), f)
            a = ac(lambda e: e.activation(FFT[z, :], FFT[z, :], ACT.Exp, scale=-1.0), a)
            a = ac(lambda e: e.activation(FFT[z, :], FFT[z, :], ACT.Ln, bias=self.t["one"][z, 0:1]), a)
            b = ve(lambda e: e.scalar_tensor_tensor(out=FFT[z, :], in0=FFR[z, :], scalar=0.0, in1=FFT[z, :],
                                                    op0=ALU.min, op1=ALU.subtract), a)
            b = ve(lambda e: e.tensor_tensor_scan(FFR[z, :], bc(self.t["one"][z, 0:1], S), FFT[z, :], 0.0,
                                                  ALU.mult, ALU.add), b)
            self.cum_tok = ve(lambda e: e.tensor_scalar(FFT[z, :], FFR[z, :], -1.0, None, ALU.mult), b)
            return f

        yield from self.tile_of(n, hi, lo, small)

        for i, (dst, c0) in enumerate([(q, 3600 + 128 * h) for h in range(4)] + [(k, 4112 + 128 * h) for h in range(4)]):
            h = i % 4

            def take(out, tok, i=i, h=h, dst=dst):
                a = ac(lambda e: e.activation(SQ[:, i % 2, :], out[:, :], ACT.Square), tok, sq_used[i % 2])
                b = ve(lambda e: e.tensor_copy(dst[:, h, :], out[:, :]), a)
                prev.append((i, a, b))
                return b

            yield from self.project(w, c0, take)
            if i >= 1:
                j, a, b = prev[i - 1]
                sq_used[j % 2] = self.colsq(SQ[:, j % 2, :], st, 4 * j, [a, self.free["b2"]])
        self.fv_tok = []
        for c in range(2):
            def keep(out, tok, u, c=c):
                t = ac(lambda e: e.activation(v[:, 2 * u:2 * u + 2, c * 256:c * 256 + 256],
                                              out[:, :].rearrange("p (t c) -> p t c", t=2), ACT.Copy), tok)
                self.fv_tok.append(t)
                return t
            yield from self.project_rows(w, 4624 + 256 * c, keep)
            if c == 0:
                j, a, b = prev[7]
                p = self.colsq(SQ[:, j % 2, :], st, 4 * j, a)
                r, a = self.rstd(st, 0, 32, 128, p, RS2[:, 0:32])
                self.free["b2"] = a
                self.foxr = r
        yield None

    def fox_norm(self):
        bank, ve = self.mem["bank"], self.ve
        RS2, PAR, GQ = (self.t[x] for x in ("RS2", "PAR", "GQ"))
        cq, ck = self.pcol(self.l, "q_norm_g"), self.pcol(self.l, "k_norm_g")
        g = ve(lambda e: e.tensor_scalar(GQ[:, 0:1], PAR[:, cq:cq + 1], 128 ** -0.5, None, ALU.mult), self.par_tok)
        self.fq_tok, self.fk_tok = [None] * 4, [None] * 4
        for h in range(4):
            for i, dst, toks, col in ((h, self.t["fq"], self.fq_tok, GQ[:, 0:1]),
                                      (4 + h, self.t["fk"], self.fk_tok, PAR[:, ck:ck + 1])):
                b = ("t0", "t1", "s0", "s1")[2 * h % 4 + i // 4]
                s = self.spread(RS2[:, 4 * i:4 * i + 4], b, self.foxr)
                toks[h] = self.free[b] = ve(lambda e, dst=dst, col=col, b=b, h=h: e.scalar_tensor_tensor(
                    out=dst[:, h, :], in0=dst[:, h, :], scalar=col, in1=bank[b][:, :], op0=ALU.mult, op1=ALU.mult),
                    s, g)
            yield None

    def fox_attention(self):
        q, k, v, EH, EL = (self.t[x] for x in ("fq", "fk", "fv", "EfH", "EfL"))
        P, PT, CB, M, R = (self.t[x] for x in ("foxP", "foxT", "foxC", "foxM", "foxR"))
        ncum, sel, ident = self.t["FFT"], self.t["sel"], self.t["ident"]
        bank, free, pe, ve, ac = self.mem["bank"], self.free, self.pe, self.ve, self.ac
        steps = [(h, i) for h in range(4) for i in range(4)]
        st = {}
        self.ef_tok = [None] * 4

        def bias(h):
            p = pe(lambda e: e.matmul(bank["o"][:, :], sel[:, h * 128:h * 128 + 128], ncum[:, :], start=True,
                                      stop=True), self.cum_tok, free["o"])
            free["o"] = st["c", h] = ac(lambda e: e.activation(CB[:, h % 2, :], bank["o"][:, :], ACT.Copy), p,
                                        st.get(("m", 4 * (h - 2) + 3)))

        def score(n):
            h, i = steps[n]
            b = f"s{n % 2}"
            w = 128 * (i + 1)
            o = bank[b]
            pe.go(lambda e: e.matmul(o[:, 0:w], q[:, h, i * 128:w], k[:, h, 0:w], start=True, stop=False),
                  self.fq_tok[h], self.fk_tok[h], free[b])
            p = pe(lambda e: e.matmul(o[:, i * 128:w], ident[:, :], self.t["causal"][:, :], start=False, stop=True))
            free[b] = st["m", n] = m = ve(lambda e: e.tensor_tensor_reduce(
                P[:, n % 3, 0:w], o[:, 0:w], CB[:, h % 2, 0:w], 1.0, -3e38, ALU.add, ALU.max, M[:, n:n + 1]), p,
                st["c", h], st.get(("t", n - 3)))
            m = ve(lambda e: e.tensor_scalar(M[:, n:n + 1], M[:, n:n + 1], -1.0, None, ALU.mult), m)
            st["x", n] = ac(lambda e: e.activation(P[:, n % 3, 0:w], P[:, n % 3, 0:w], ACT.Exp, bias=M[:, n:n + 1],
                                                   accum_out=R[:, n:n + 1]), m)

        def scale(n):
            w = 128 * (steps[n][1] + 1)
            r = ve(lambda e: e.reciprocal(R[:, n:n + 1], R[:, n:n + 1]), st["x", n])
            st["s", n] = ve(lambda e: e.tensor_scalar(P[:, n % 3, 0:w], P[:, n % 3, 0:w], R[:, n:n + 1], None,
                                                      ALU.mult), r)

        def turn(n):
            h, i = steps[n]
            b = f"t{n % 2}"
            pe.wait(st["s", n], free[b])
            for j in range(i + 1):
                f = lambda e, j=j: e.transpose(bank[b][:, j * 128:j * 128 + 128], P[:, n % 3, j * 128:j * 128 + 128],
                                               ident[:, :])
                p = pe(f) if j == i else pe.go(f)
            st["t", n] = p
            w = 128 * (i + 1)
            free[b] = st["p", n] = ac(lambda e: e.activation(PT[:, n % 3, 0:w], bank[b][:, 0:w], ACT.Copy), p,
                                      st.get(("v", n - 3)))

        def value(n):
            h, i = steps[n]
            pe.wait(st["p", n], self.fv_tok, free["o"] if i == 0 else None)
            for j in range(i + 1):
                f = lambda e, j=j: e.matmul(bank["o"][:, i * 128:i * 128 + 128], v[:, j, h * 128:h * 128 + 128],
                                            PT[:, n % 3, j * 128:j * 128 + 128], start=(j == 0), stop=(j == i))
                p = pe(f) if j == i else pe.go(f)
            st["v", n] = p
            if i == 3:
                a = ac(lambda e: e.activation(EH[:, h, :], bank["o"][:, :], ACT.Copy), p)
                free["o"] = self.ef_tok[h] = ve(lambda e: e.tensor_tensor(
                    EL[:, h, :], bank["o"][:, :], EH[:, h, :].bitcast(F32), ALU.subtract), a)
                if h + 2 < 4:
                    bias(h + 2)

        N = len(steps)
        bias(0)
        bias(1)
        for n in range(N + 3):
            if n < N:
                score(n)
            if 1 <= n <= N:
                scale(n - 1)
            if 2 <= n <= N + 1:
                turn(n - 2)
            if n >= 3:
                value(n - 3)
            yield None
        self.ffr_used = st["v", N - 1]

    def gla_inputs(self, w):
        gk, gv, gq = (self.t[x] for x in ("gk", "gv", "gq"))
        self.gk_tok, self.gv_tok, self.gq_tok = [], [], [None, None]

        def keep_k(out, tok, u):
            t = self.ac(lambda e: e.activation(gk[:, 2 * u:2 * u + 2, :], out[:, :].rearrange("p (t c) -> p t c", t=2),
                                               ACT.Copy), tok)
            self.gk_tok.append(t)
            return t

        yield from self.project_rows(w, 2304, keep_k)
        for c in range(2):
            def keep_v(out, tok, u, c=c):
                t = self.ac(lambda e: e.activation(gv[:, 2 * u:2 * u + 2, c * 256:c * 256 + 256],
                                                   out[:, :].rearrange("p (t c) -> p t c", t=2), ACT.Copy), tok)
                self.gv_tok.append(t)
                return t
            yield from self.project_rows(w, 2560 + 256 * c, keep_v)
        for c in range(2):
            def keep_q(out, tok, c=c):
                self.gq_tok[c] = self.ac(lambda e: e.activation(gq[:, c, :], out[:, :], ACT.Copy, scale=64 ** -0.5),
                                         tok)
                return self.gq_tok[c]
            yield from self.project(w, 2048 + 128 * c, keep_q)

    def gla_attention(self):
        gk, gv, gq, GO = (self.t[x] for x in ("gk", "gv", "gq", "GO"))
        LA, TA, ED, AD, SA, SQ, RS, GLR, WA, PAR = (self.t[x] for x in (
            "LA", "TA", "ED", "AD", "SA", "glaS", "RS", "GLR", "WA", "PAR"))
        bank, free, pe, ve, ac = self.mem["bank"], self.free, self.pe, self.ve, self.ac
        st = {}
        for u in range(2):
            o = bank[f"s{u}"]
            pe.wait(self.glr_tok, self.wa_tok, free[f"s{u}"])
            for t in (2 * u, 2 * u + 1):
                f = lambda e, t=t, o=o: e.matmul(o[:, (t % 2) * 256:(t % 2) * 256 + 256],
                                                 GLR[0:17, t * 128:t * 128 + 128], WA[0:17, 0:256], start=True, stop=True)
                st["z", u] = pe(f)
        self.glr_used = st["z", 1]
        yield None
        for u in range(2):
            st["a", u] = ac(lambda e, u=u: e.activation(TA[:, u, :], bank[f"s{u}"][:, :], ACT.Abs), st["z", u])
        for u in range(2):
            st["a", u] = ac(lambda e, u=u: e.activation(TA[:, u, :], TA[:, u, :], ACT.Exp, scale=-1.0), st["a", u])
        for u in range(2):
            st["a", u] = ac(lambda e, u=u: e.activation(TA[:, u, :], TA[:, u, :], ACT.Ln,
                                                        bias=self.t["one"][:, 0:1]), st["a", u])
            free[f"s{u}"] = st["l", u] = ve(lambda e, u=u: e.scalar_tensor_tensor(
                out=LA[:, u, :], in0=bank[f"s{u}"][:, :], scalar=0.0, in1=TA[:, u, :], op0=ALU.min,
                op1=ALU.subtract), st["a", u])
        yield None
        yield None
        for u in range(2):
            pe.wait(st["l", u], free[f"t{u}"])
            for t in range(2):
                f = lambda e, t=t, u=u: e.matmul(bank[f"t{u}"][:, t * 256:t * 256 + 256], self.t["tail"][:, :],
                                                 LA[:, u, t * 256:t * 256 + 256], start=True, stop=True)
                p = pe(f)
            free[f"t{u}"] = a = ac(lambda e, u=u: e.activation(ED[:, u, :], bank[f"t{u}"][:, :], ACT.Exp,
                                                               scale=1.0 / 16), p)
            st["k", u] = ve(lambda e, u=u: e.tensor_tensor(ED[:, u, :], ED[:, u, :],
                                                           gk[:, 2 * u:2 * u + 2, :].rearrange("p t c -> p (t c)"),
                                                           ALU.mult), a, self.gk_tok)
        pe.wait(free["s0"])
        for f2 in range(2):
            for t in range(4):
                f = lambda e, f2=f2, t=t: e.matmul(
                    bank["s0"][:, f2 * 8 + 2 * t:f2 * 8 + 2 * t + 2],
                    LA[:, t // 2, (t % 2) * 256 + f2 * 128:(t % 2) * 256 + f2 * 128 + 128],
                    self.t["chunk"][:, :], start=True, stop=True)
                p = pe(f)
        free["s0"] = st["ad"] = ac(lambda e: e.activation(AD[:, 0:16], bank["s0"][:, 0:16], ACT.Exp, scale=1.0 / 16), p)
        yield None
        yield None
        for p2 in range(2):
            pe.wait(st["k", 0], st["k", 1], self.gv_tok, free["t0"], free["t1"])
            for n in range(8):
                for hh in range(2):
                    c0, t = 64 * (n % 2), n // 2
                    h = 2 * p2 + hh
                    f = lambda e, c0=c0, t=t, h=h, hh=hh, n=n: e.matmul(
                        bank[f"t{n % 2}"][64 * hh:64 * hh + 64, (n // 2) * 128:(n // 2) * 128 + 128],
                        ED[c0:c0 + 64, t // 2, (t % 2) * 256 + h * 64:(t % 2) * 256 + h * 64 + 64],
                        gv[c0:c0 + 64, t, h * 128:h * 128 + 128], start=True, stop=True)
                    p = pe(f)
            for n in range(8):
                kv = bank[f"t{n % 2}"][:, (n // 2) * 128:(n // 2) * 128 + 128]
                if n == 0:
                    s = ve(lambda e, kv=kv, p2=p2: e.tensor_copy(SA[:, p2, 0, :], kv), p)
                else:
                    s = ve(lambda e, kv=kv, n=n, p2=p2: e.scalar_tensor_tensor(
                        out=SA[:, p2, n, :], in0=SA[:, p2, n - 1, :], scalar=AD[:, p2 * 8 + n:p2 * 8 + n + 1],
                        in1=kv, op0=ALU.mult, op1=ALU.add), s, p, st["ad"])
            free["t0"] = free["t1"] = s
            yield None
            st["S", p2] = s
        yield None
        for p2 in range(2):
            for hh in range(2):
                h = 2 * p2 + hh
                b = f"s{hh}"
                pe.wait(st["S", p2], self.gq_tok[p2], free[b])
                for n in range(8):
                    f = lambda e, n=n, b=b, p2=p2, hh=hh: e.matmul(
                        bank[b][:, n * 64:n * 64 + 64], SA[64 * hh:64 * hh + 64, p2, n, :],
                        gq[64 * hh:64 * hh + 64, p2, n * 64:n * 64 + 64], start=True, stop=True)
                    p = pe(f)
                a = ac(lambda e, b=b, hh=hh: e.activation(SQ[:, hh, :], bank[b][:, :], ACT.Square), p,
                       st.get(("sq", h - 2)))
                free[b] = ve(lambda e, b=b, h=h: e.tensor_copy(GO[:, h, :], bank[b][:, :]), a)
                st["s", h] = a
                yield None
                if h >= 1:
                    st["sq", h - 1] = self.colsq(SQ[:, (h - 1) % 2, :], bank["t1"], 4 * (h - 1),
                                                 [st["s", h - 1], free["t1"]])
        st["sq", 3] = self.colsq(SQ[:, 1, :], bank["t1"], 12, st["s", 3])
        r, a = self.rstd(bank["t1"], 0, 16, 128, st["sq", 3], RS[:, 0:16])
        free["t1"] = a
        yield None
        c = self.pcol(self.l, "gla_norm_g")
        self.go_tok = [None] * 4
        for h in range(4):
            b = f"t{h % 2}"
            s = self.spread(RS[:, 4 * h:4 * h + 4], b, r)
            free[b] = self.go_tok[h] = ve(lambda e, h=h, b=b: e.scalar_tensor_tensor(
                out=GO[:, h, :], in0=GO[:, h, :], scalar=PAR[:, c:c + 1], in1=bank[b][:, :], op0=ALU.mult,
                op1=ALU.mult), s)
            yield None

    def gated(self, w, c0, O, toks, EH, EL):
        G = self.t["GT"]
        ve, ac = self.ve, self.ac
        out_tok = [None] * 4
        for h in range(4):
            def take(out, tok, h=h):
                b = self.gt_i % 4
                self.gt_i += 1
                a = ac(lambda e: e.activation(G[:, b, :], out[:, :], ACT.Silu), tok, self.gt_used[b])
                m = ve(lambda e: e.tensor_tensor(G[:, b, :], G[:, b, :], O[:, h, :], ALU.mult), a, toks()[h])
                x = ac(lambda e: e.activation(EH[:, h, :], G[:, b, :], ACT.Copy), m)
                self.gt_used[b] = out_tok[h] = ve(lambda e: e.tensor_tensor(
                    EL[:, h, :], G[:, b, :], EH[:, h, :].bitcast(F32), ALU.subtract), x)
                return a
            yield from self.project(w, c0 + 128 * h, take)
        self.gated_tok = out_tok

    def mixing(self, l):
        wmg, wbr = self.I["w_mg"][l], self.I["w_br"][l]
        E = {n: (self.t[f"E{x}H"], self.t[f"E{x}L"], tk) for n, x, tk in ((0, "r", self.er_tok), (1, "g", self.eg_tok),
                                                                          (2, "f", self.ef_tok))}
        MH, ML, SG, MX, PAR = (self.t[x] for x in ("MH", "ML", "SG", "MX", "PAR"))
        ve, ac = self.ve, self.ac
        c = self.pcol(l, "b_mg")
        self.mix_tok = [None] * 8
        sg_used = [None] * 2
        sg_tok = [None] * 2
        mx_tok = [None] * 2
        for dp in range(4):
            for n in (0, 2, 1):
                for u in range(2):
                    d = 2 * dp + u

                    def gate(out, tok, u=u, d=d, n=n):
                        j = c + 8 * n + d
                        sg_tok[u] = ac(lambda e: e.activation(SG[:, u, :], out[:, :], ACT.Sigmoid,
                                                              bias=PAR[:, j:j + 1]), tok, sg_used[u])
                        return sg_tok[u]

                    yield from self.project(wmg, n * 1024 + d * 128, gate)
                m = self.weight(wbr[n], 0, 4, dp * 256, 256)
                hi, lo = self.views(m, 4, 256)
                H_, L_, tk = E[n]
                for u in range(2):
                    d = 2 * dp + u
                    b, fr = self.bank()
                    out = self.mem["bank"][b]
                    terms = [(hi[:, k, u * 128:u * 128 + 128], lo[:, k, u * 128:u * 128 + 128], H_[:, k, :], L_[:, k, :], tk[k])
                             for k in range(4)]
                    tok = yield from self.dot(out[:, :], terms, toks=(self.split_tok[m], fr))
                    if n == 0:
                        v = ve(lambda e, u=u, out=out: e.tensor_tensor(MX[:, u, :], out[:, :], SG[:, u, :], ALU.mult),
                               tok, sg_tok[u], mx_tok[u])
                        self.free[b] = sg_used[u] = v
                    else:
                        v = ve(lambda e, u=u, out=out: e.tensor_tensor(SG[:, u, :], out[:, :], SG[:, u, :], ALU.mult),
                               tok, sg_tok[u])
                        self.free[b] = v
                        v = ve(lambda e, u=u: e.tensor_tensor(MX[:, u, :], MX[:, u, :], SG[:, u, :], ALU.add), v,
                               mx_tok[u])
                        sg_used[u] = v
                    mx_tok[u] = v
                self.done_tok[m] = tok
            for u in range(2):
                d = 2 * dp + u
                a = ac(lambda e, u=u, d=d: e.activation(MH[:, d, :], MX[:, u, :], ACT.Copy), mx_tok[u])
                mx_tok[u] = self.mix_tok[d] = ve(lambda e, u=u, d=d: e.tensor_tensor(
                    ML[:, d, :], MX[:, u, :], MH[:, d, :].bitcast(F32), ALU.subtract), a)

    def out_proj(self, ap, kt, AH, AL, toks, gate, norm):
        self.ac.go(lambda e: e.activation(self.t["RS"][:, 8:9], self.t["eps"][:, 0:1], ACT.Sqrt))
        self.norm = norm
        bank = self.mem["bank"]
        halves = 7 if kt > 8 else 5
        col = lambda d: None if gate is None else gate[:, d:d + 1]

        def entries(d):
            for k0 in range(0, kt, 8):
                kn = min(8, kt - k0)
                n = self.weight(ap, k0 * 128, kn, d * 128, 128)
                yield (n, k0, kn, *self.views(n, kn, 128))

        def terms(k0, kn, hi, lo, c):
            return [(hi[:, k, :], lo[:, k, :], AH[:, k0 + k, c], AL[:, k0 + k, c], toks[k0 + k]) for k in range(kn)]

        whole = slice(0, S)
        for d in range(halves):
            b, fr = self.bank()
            for n, k0, kn, hi, lo in entries(d):
                self.done_tok[n] = tok = yield from self.dot(
                    bank[b][:, :], terms(k0, kn, hi, lo, whole), start=(k0 == 0), stop=(k0 + kn == kt),
                    toks=(self.split_tok[n], fr))
            self.x_update(d, b, tok, col(d), whole)
        held = {d: list(entries(d)) for d in range(halves, KD)}
        steps = 2
        for hf in range(2):
            c = slice(256 * hf, 256 * hf + 256)
            for d in held:
                b, fr = self.bank()
                for n, k0, kn, hi, lo in held[d]:
                    for _ in self.dot(bank[b][:, c], terms(k0, kn, hi, lo, c), start=(k0 == 0), stop=(k0 + kn == kt),
                                      toks=(self.split_tok[n], fr)):
                        if hf == 1 and steps:
                            next(norm)
                            steps -= 1
                        yield BUSY
                    tok = self.last
                    if hf == 1:
                        self.done_tok[n] = tok
                self.x_update(d, b, tok, col(d), c)

    def ffn_up(self, wu, cu, wg, cg, conv):
        AH, AL, CB, PAR = (self.t[x] for x in ("FH", "FL", "CB", "PAR"))
        ve, ac = self.ve, self.ac
        self.ff_tok = [None] * KF
        used = [None, None]
        hold = {}
        jobs = []
        for f in range(KF):
            def up(out, tok, f=f, i=f % 2):
                if conv is None:
                    hold[f] = ac(lambda e: e.activation(CB[:, i, :], out[:, :], ACT.Silu), tok, used[i])
                    return hold[f]
                wc, bcol = conv
                a = ac(lambda e: e.activation(CB[:, i, :], out[:, :], ACT.Identity, scale=wc(2, f), bias=bcol(f)), tok,
                       used[i], self.par_tok)
                v = ve(lambda e: e.scalar_tensor_tensor(out=CB[:, i, 1:S], in0=out[:, 0:S - 1], scalar=wc(1, f),
                                                        in1=CB[:, i, 1:S], op0=ALU.mult, op1=ALU.add), a)
                v = ve(lambda e: e.scalar_tensor_tensor(out=CB[:, i, 2:S], in0=out[:, 0:S - 2], scalar=wc(0, f),
                                                        in1=CB[:, i, 2:S], op0=ALU.mult, op1=ALU.add), v)
                hold[f] = ac(lambda e: e.activation(CB[:, i, :], CB[:, i, :], ACT.Silu), v)
                return v

            def gate(out, tok, f=f, i=f % 2):
                v = ve(lambda e: e.tensor_tensor(CB[:, i, :], CB[:, i, :], out[:, :], ALU.mult), tok, hold[f])
                a = ac(lambda e: e.activation(AH[:, f, :], CB[:, i, :], ACT.Copy), v)
                used[i] = self.ff_tok[f] = ve(lambda e: e.tensor_tensor(
                    AL[:, f, :], CB[:, i, :], AH[:, f, :].bitcast(F32), ALU.subtract), a)
                return v

            jobs += [(wu, cu + f * 128, up), (wg, cg + f * 128, gate)]
        yield from self.projects(jobs)

    def pool_mixer(self, norm):
        I, t = self.I, self.t
        bank, free, pe, ve, ac = self.mem["bank"], self.free, self.pe, self.ve, self.ac
        U, W1, W2, PH, PL, ZH, ZL, CT, PAR = (t[x] for x in ("U", "W1", "W2", "PH", "PL", "ZH", "ZL", "CT", "PAR"))
        p_tok = [None] * 8
        jobs = []
        for g in range(4):
            for c in range(2):
                d = 2 * g + c
                i = d % 2

                def take(out, tok, g=g, d=d, i=i):
                    u = ac(lambda e: e.activation(U[:, i, :], out[:, :], ACT.Copy), tok,
                           p_tok[d - 2] if d >= 2 else None)
                    src, v = U[:, i, :], u
                    for s in range(g + 1):
                        k = 1 << s
                        dst = (W1 if s % 2 == 0 else W2)[:, i, :]
                        a = ve(lambda e, dst=dst, src=src, k=k: e.tensor_copy(dst[:, 0:k], src[:, 0:k]), v)
                        v = ve(lambda e, dst=dst, src=src, k=k: e.tensor_tensor(dst[:, k:S], src[:, k:S],
                                                                                src[:, 0:S - k], ALU.add), v)
                        v = [a, v]
                        src = dst
                    w = 2 << g
                    oth = (W1 if g % 2 == 1 else W2)[:, i, :]
                    a = ve(lambda e: e.tensor_tensor(oth[:, 0:16], src[:, 0:16], CT[:, g * 16:g * 16 + 16], ALU.mult), v)
                    b = ve(lambda e: e.tensor_scalar(oth[:, 16:S], src[:, 16:S], 1.0 / w, None, ALU.mult))
                    b = ve(lambda e: e.tensor_tensor(oth[:, :], oth[:, :], U[:, i, :], ALU.subtract), a, b)
                    h = ac(lambda e: e.activation(PH[:, d, :], oth[:, :], ACT.Copy), b)
                    p_tok[d] = ve(lambda e: e.tensor_tensor(PL[:, d, :], oth[:, :], PH[:, d, :].bitcast(F32),
                                                            ALU.subtract), h)
                    return u

                jobs.append((I["pool_w_in_2"][0], d * 128, take))
        yield from self.projects(jobs)
        z_tok = [None] * 8
        c0 = 512 + 40
        for g in range(4):
            n = self.weight(I["pool_w_group_2"][0, g], 0, 2, 0, 256)
            hi, lo = self.views(n, 2, 256)
            for c in range(2):
                d = 2 * g + c
                b, fr = self.bank()
                out = bank[b]
                terms = [(hi[:, k, c * 128:c * 128 + 128], lo[:, k, c * 128:c * 128 + 128], PH[:, 2 * g + k, :],
                          PL[:, 2 * g + k, :], p_tok[2 * g + k]) for k in range(2)]
                tok = yield from self.dot(out[:, :], terms, toks=(self.split_tok[n], fr))
                sc = PAR[:, c0 + d:c0 + d + 1]
                h = ac(lambda e, out=out, sc=sc, d=d: e.activation(ZH[:, d, :], out[:, :], ACT.Copy, scale=sc), tok)
                free[b] = z_tok[d] = ve(lambda e, out=out, sc=sc, d=d: e.scalar_tensor_tensor(
                    out=ZL[:, d, :], in0=out[:, :], scalar=sc, in1=ZH[:, d, :].bitcast(F32), op0=ALU.mult,
                    op1=ALU.subtract), h)
            self.done_tok[n] = tok
        yield from self.out_proj(I["pool_w_out_2"][0], 8, ZH, ZL, z_tok, None, norm)

    def attn_inputs(self):
        w = self.I["attn_w_qkv_2"][0]
        t = self.t
        self.aq_tok, self.ak_tok, self.av_tok = [None] * 8, [None] * 8, [None] * 8
        used = [None, None]
        i = 0
        strided = lambda r: slice(r, S, 4)
        jobs = []
        for p in range(8):
            for dst, c0, sc, toks in ((t["aq"], 0, 64 ** -0.5, self.aq_tok), (t["ak"], 1024, 1.0, self.ak_tok)):
                def take(out, tok, i=i, dst=dst, sc=sc, toks=toks, p=p):
                    b, toks[p] = self.rope_pieces(out, dst[:, p, :], t["aT"][:, i % 2, :], t["cos2"][:, :],
                                                  t["sin2"][:, :], 32, sc, tok, self.tab_tok, used[i % 2])
                    used[i % 2] = toks[p]
                    return b
                i += 1
                jobs.append((w, c0 + 128 * p, take))
        yield from self.projects(jobs[0:4])
        self.big_order = ["b1", "b2"]
        for p in range(8):
            if p >= 2:
                for job in jobs[2 * p:2 * p + 2]:
                    yield from self.project(*job)

            def keep(out, tok, p=p):
                self.av_tok[p] = self.ac(lambda e: e.activation(
                    t["av"][:, :, p * 128:p * 128 + 128], out[:, :].rearrange("p (t c) -> p t c", t=4), ACT.Copy), tok)
                return self.av_tok[p]

            yield from self.project_rows_half(w, 2048 + 128 * p, keep, None if p < 3 else strided)
            yield p

    def attn_heads(self):
        t = self.t
        q, k, v, MO = (t[x] for x in ("aq", "ak", "av", "MO"))
        P, PT, M, NM, DEN, R = (t[x] for x in ("aP", "aPT", "aM", "aNM", "aDEN", "aR"))
        bank, free, pe, ve, ac = self.mem["bank"], self.free, self.pe, self.ve, self.ac
        steps = [(h, n) for h in range(16) for n in range(4)]
        st = {}
        self.mo_tok = [None] * 8

        def group(h):
            return 0 if h < 6 else 1 if h < 11 else 2

        def cols(h, n):
            if group(h) == 0:
                lo = max(0, n - 1)
                msk = t["window"][:, :] if n else t["window"][:, 128:256]
                return slice(n * 128, n * 128 + 128), slice(lo * 128, n * 128 + 128), list(range(lo, n + 1)), msk
            msk = t["causal"] if group(h) == 1 else t["dil"]
            return slice(n, S, 4), slice(n, S, 4), [n], msk[:, :]

        def score(m):
            h, n = steps[m]
            p, r = h // 2, slice(64 * (h % 2), 64 * (h % 2) + 64)
            b = f"s{m % 2}"
            i = m % 6
            qs, ks, tiles, msk = cols(h, n)
            w = 128 * len(tiles)
            pt = pe(lambda e: e.matmul(bank[b][:, 0:w], q[r, p, qs], k[r, p, ks], start=True, stop=True),
                    self.aq_tok[p], self.ak_tok[p], free[b])
            a = ve(lambda e: e.tensor_tensor_reduce(P[:, i, 0:w], bank[b][:, 0:w], msk, 1.0, -3e38, ALU.add, ALU.max,
                                                    M[:, m:m + 1]), pt, st.get(("t", m - 6)))
            free[b] = a
            a = ve(lambda e: e.tensor_scalar(NM[:, m:m + 1], M[:, m:m + 1], -1.0, None, ALU.mult), a)
            st["x", m] = ac(lambda e: e.activation(P[:, i, 0:w], P[:, i, 0:w], ACT.Exp, bias=NM[:, m:m + 1],
                                                   accum_out=DEN[:, m:m + 1]), a)

        def scale(m):
            i = m % 6
            w = 128 * len(cols(*steps[m])[2])
            d = ve(lambda e: e.reciprocal(R[:, m:m + 1], DEN[:, m:m + 1]), st["x", m])
            st["s", m] = ve(lambda e: e.tensor_scalar(P[:, i, 0:w], P[:, i, 0:w], R[:, m:m + 1], None, ALU.mult), d)
            self.lse_in = st["s", m]

        def turn(m):
            h, n = steps[m]
            b = f"t{m % 2}"
            i = m % 6
            nt = len(cols(h, n)[2])
            pe.wait(st["s", m], free[b])
            for j in range(nt):
                f = lambda e, j=j: e.transpose(bank[b][:, j * 128:j * 128 + 128], P[:, i, j * 128:j * 128 + 128],
                                               t["ident"][:, :])
                p = pe(f) if j == nt - 1 else pe.go(f)
            st["t", m] = p
            free[b] = st["p", m] = ac(lambda e: e.activation(PT[:, i, 0:128 * nt], bank[b][:, 0:128 * nt], ACT.Copy), p,
                                      st.get(("v", m - 6)))

        def value(m):
            h, n = steps[m]
            p, r = h // 2, slice(64 * (h % 2), 64 * (h % 2) + 64)
            i = m % 6
            ob = "o" if p % 2 == 0 else "b0"
            tiles = cols(h, n)[2]
            pe.wait(st["p", m], self.av_tok[p], free[ob] if n == 0 and h % 2 == 0 else None)
            for j, kt in enumerate(tiles):
                f = lambda e, j=j, kt=kt: e.matmul(bank[ob][r, n * 128:n * 128 + 128], v[:, kt, h * 64:h * 64 + 64],
                                                   PT[:, i, j * 128:j * 128 + 128], start=(j == 0),
                                                   stop=(j == len(tiles) - 1))
                pt = pe(f) if j == len(tiles) - 1 else pe.go(f)
            st["v", m] = pt
            if n == 3 and h % 2 == 1:
                src = bank[ob][:, :]
                if group(h) == 0:
                    f = lambda e: e.activation(MO[:, p, :], src, ACT.Copy)
                else:
                    f = lambda e: e.activation(MO[:, p, :].rearrange("p (l r) -> p r l", r=4),
                                               src.rearrange("p (r l) -> p r l", r=4), ACT.Copy)
                free[ob] = self.mo_tok[p] = ac(f, pt)

        N = len(steps)
        for m in range(N + 5):
            if m < N:
                score(m)
            if 1 <= m <= N:
                scale(m - 1)
            if 3 <= m < N + 3:
                turn(m - 3)
            if m >= 5:
                value(m - 5)
            yield None

    def attn_merge(self):
        t = self.t
        bank, free, pe, ve, ac = self.mem["bank"], self.free, self.pe, self.ve, self.ac
        M, DEN, L, GM, LT, AL, TM, MO = (t[x] for x in ("aM", "aDEN", "aL", "aG", "aLT", "ALP", "aTM", "MO"))
        a = ac(lambda e: e.activation(L[:, 0:64], DEN[:, 0:64], ACT.Ln), self.lse_in)
        l = ve(lambda e: e.tensor_tensor(L[:, 0:64], L[:, 0:64], M[:, 0:64], ALU.add), a)
        heads = ((0, 6), (6, 11), (11, 16))
        tok = []
        for g, (h0, h1) in enumerate(heads):
            nh = h1 - h0
            x = L[:, 4 * h0:4 * h1].rearrange("p (h n) -> p n h", n=4)
            m = ve(lambda e, g=g, x=x: e.tensor_reduce(GM[:, g, :], x, AXX, ALU.max), l)
            for h in range(h0, h1):
                s = ve(lambda e, h=h, g=g: e.tensor_tensor(LT[:, 4 * h:4 * h + 4], L[:, 4 * h:4 * h + 4], GM[:, g, :],
                                                           ALU.subtract), m, l)
            tok.append((m, s))
        a = ac(lambda e: e.activation(LT[:, 0:64], LT[:, 0:64], ACT.Exp), tok[2][1])
        for g, (h0, h1) in enumerate(heads):
            x = LT[:, 4 * h0:4 * h1].rearrange("p (h n) -> p n h", n=4)
            s = ve(lambda e, g=g, x=x: e.tensor_reduce(GM[:, 3 + g, :], x, AXX, ALU.add), a)
        a = ac(lambda e: e.activation(GM[:, 6:9, :], GM[:, 3:6, :], ACT.Ln, scale=1.0), s)
        for g, (h0, h1) in enumerate(heads):
            s = ve(lambda e, g=g, n=h1 - h0: e.scalar_tensor_tensor(
                out=GM[:, 6 + g, :], in0=GM[:, g, :], scalar=-float(np.log(n)), in1=GM[:, 6 + g, :], op0=ALU.add,
                op1=ALU.add), a)
        for g in range(3):
            b = ("s0", "s1", "t0")[g]
            p = self.spread(GM[:, 6 + g, :], b, s)
            src = bank[b][:, :]
            if g == 0:
                f = lambda e, src=src: e.tensor_copy(AL[:, 0, :], src)
            else:
                f = lambda e, src=src, g=g: e.tensor_copy(AL[:, g, :].rearrange("p (l r) -> p r l", r=4),
                                                          src.rearrange("p (r l) -> p r l", r=4))
            free[b] = c = ve(f, p)
        m = ve(lambda e: e.tensor_tensor(TM[:, 0, :], AL[:, 0, :], AL[:, 1, :], ALU.max), c)
        m = ve(lambda e: e.tensor_tensor(TM[:, 0, :], TM[:, 0, :], AL[:, 2, :], ALU.max), m)
        for g in range(3):
            m2 = ve(lambda e, g=g: e.tensor_tensor(AL[:, g, :], AL[:, g, :], TM[:, 0, :], ALU.subtract), m)
        E3 = t["aE"]
        for g in range(3):
            x = ac(lambda e, g=g: e.activation(E3[:, g, :], AL[:, g, :], ACT.Exp), m2)
        s = ve(lambda e: e.tensor_tensor(TM[:, 0, :], E3[:, 0, :], E3[:, 1, :], ALU.add), x)
        s = ve(lambda e: e.tensor_tensor(TM[:, 0, :], TM[:, 0, :], E3[:, 2, :], ALU.add), s)
        a = ac(lambda e: e.activation(TM[:, 1, :], TM[:, 0, :], ACT.Ln), s)
        for g in range(3):
            s = ve(lambda e, g=g: e.tensor_tensor(AL[:, g, :], AL[:, g, :], TM[:, 1, :], ALU.subtract), a)
        for g in range(3):
            a = ac(lambda e, g=g: e.activation(AL[:, g, :], AL[:, g, :], ACT.Exp), s)
        G = (0, 0, 0, 1, 1, None, 2, 2)
        YH, YL = t["YH"], t["YL"]
        self.y_tok = [None] * 8
        for p in range(8):
            parts = [(slice(0, 128), G[p])] if G[p] is not None else [(slice(0, 64), 1), (slice(64, 128), 2)]
            for r, g in parts:
                v = ve(lambda e, r=r, g=g, p=p: e.scalar_tensor_tensor(
                    out=MO[r, p, :], in0=MO[r, p, :], scalar=3.0, in1=AL[r, g, :], op0=ALU.mult, op1=ALU.mult), a,
                    self.mo_tok[p])
            h = ac(lambda e, p=p: e.activation(YH[:, p, :], MO[:, p, :], ACT.Copy), v)
            self.y_tok[p] = ve(lambda e, p=p: e.tensor_tensor(YL[:, p, :], MO[:, p, :], YH[:, p, :].bitcast(F32),
                                                              ALU.subtract), h)

    def finish(self):
        t = self.t
        bank, free, pe, ve, ac = self.mem["bank"], self.free, self.pe, self.ve, self.ac
        X, RS, OT, PAR = (t[x] for x in ("X", "RS", "OT", "PAR"))
        c0 = 512 + 32
        outs = []
        i = 0

        def store(tt):
            nonlocal i
            toks = []
            for u in range(2):
                b = ("o", "b0", "b1", "b2")[i % 4]
                pe.wait(free[b])
                for k in range(4 * u, 4 * u + 4):
                    f = lambda e, k=k, b=b: e.transpose(bank[b][:, (k % 4) * 128:(k % 4) * 128 + 128],
                                                        X[:, k, tt * 128:tt * 128 + 128], t["ident"][:, :])
                    p = pe(f, x[tt // 2][k])
                if i % 2:
                    free[b] = ac(lambda e, b=b, u=u: e.activation(OT[:, tt, u * 512:u * 512 + 512], bank[b][:, :],
                                                                  ACT.Copy), p)
                else:
                    free[b] = ve(lambda e, b=b, u=u: e.tensor_copy(OT[:, tt, u * 512:u * 512 + 512], bank[b][:, :]), p)
                toks.append(free[b])
                i += 1
            outs.append(self.out_flow[tt](self.out[0, tt * 128:tt * 128 + 128, :], OT[:, tt, :], toks))

        def scale(hf, r):
            b = ("t0", "s0")[hf]
            sp = self.spread(RS[:, 2 * hf:2 * hf + 2], b, r, 2)
            c = slice(256 * hf, 256 * hf + 256)
            return [ve(lambda e, k=k: e.scalar_tensor_tensor(
                out=X[:, k, c], in0=X[:, k, c], scalar=PAR[:, c0 + k:c0 + k + 1], in1=bank[b][:, 0:256],
                op0=ALU.mult, op1=ALU.mult), sp) for k in range(KD)]

        x = []
        r = self.sums(0)
        yield None
        x.append(scale(0, r))
        yield None
        store(0)
        r = self.sums(1)
        store(1)
        x.append(scale(1, r))
        store(2)
        store(3)
        self.sp.wait(*outs)

    def run(self):
        I, t = self.I, self.t
        pe, ve, ac, po = self.pe, self.ve, self.ac, self.po
        bank, free = self.mem["bank"], self.free
        self.sq_used, self.nt_used, self.ss_used, self.late = [None] * 2, [None] * 4, None, None
        self.H2 = [None, None]
        self.gt_i, self.gt_used = 0, [None] * 4
        self.glr_used = self.ffr_used = self.aa_used = None
        T = self.mem["tables"]

        one = po(lambda e: e.memset(t["ones"][:, :], 1.0))
        one = po(lambda e: e.memset(t["eps"][:, :], EPS))
        for lane in (pe, ve, ac):
            lane.wait(one)
        XS, PST = t["XS"], t["PST"]
        par = [self.load(PST[:, :, :], I["params"].rearrange("j r c -> r j c"))]
        for l in range(DEPTH):
            par.append(self.load(t["BF"][96:100, l:l + 1], I["b_fox_f"][l].rearrange("(h o) -> h o", o=1)))
        con = self.load(t["CON"][:, :], T["con"])
        rows = (117, 66, 117, 66, 56)
        for j, n in ((4, 56), (0, 117), (1, 66), (2, 117), (3, 66)):
            b = ("s0", "s1")[j % 2]
            p = pe(lambda e, j=j, n=n, b=b: e.transpose(bank[b][:, 0:n], PST[0:n, j, :], t["ident"][0:n, 0:n]), free[b],
                   par, con)
            free[b] = self.par_tok = ve(lambda e, j=j, n=n, b=b: e.tensor_copy(t["PAR"][:, j * 128:j * 128 + n],
                                                                               bank[b][:, 0:n]), p, con)
            if j == 4:
                self.ca_tok = ac(lambda e: e.activation(t["CA"][:, :], t["PAR"][:, 512 + 48:512 + 56], ACT.Silu),
                                 self.par_tok)

        def mods(l, which):
            c = self.pcol(l, "norm1_g" if which == 0 else "norm2_g")
            A = t["NA"][:, 2 * l + which, :]
            MOD = t["MOD"]
            s = 24 * which
            return ve(lambda e: e.scalar_tensor_tensor(out=A, in0=MOD[:, l, s + 8:s + 16], scalar=1.0,
                                                       in1=t["PAR"][:, c:c + 8], op0=ALU.add, op1=ALU.mult),
                      self.mod_tok), A, MOD[:, l, s:s + 8]

        def turn_x(ks):
            for k in ks:
                b = ("s0", "s1", "o", "t0")[k % 4]
                pe.wait(free[b])
                for tt in range(4):
                    p = pe(lambda e, k=k, tt=tt, b=b: e.transpose(
                        bank[b][:, tt * 128:tt * 128 + 128], XS[:, tt, k * 128:k * 128 + 128], t["ident"][:, :]),
                        x_in[tt])
                free[b] = ac(lambda e, k=k, b=b: e.activation(t["X"][:, k, :], bank[b][:, :], ACT.Copy), p)
                self.square(k, free[b], slice(0, S))

        rows = [self.ada_row(0, q) for q in range(4)]
        next(rows[0])
        x_in = [self.load(XS[:, tt, :], I["x"][0, tt * 128:tt * 128 + 128, :]) for tt in range(4)]
        for q in range(4):
            for _ in range(5 if q else 4):
                next(rows[q])
            if q in (1, 2):
                turn_x(range(4 * q - 4, 4 * q))
            drain(rows[q])
        ac.go(lambda e: e.activation(t["RS"][:, 8:9], t["eps"][:, 0:1], ACT.Sqrt))
        tok, A, B = mods(0, 0)
        self.norm = self.x_norm(A, B, tok)
        next(self.norm)
        next(self.norm)
        for l in range(DEPTH):
            self.l = l
            w = I["w_in"][l]
            prev = self.last if l else None
            tabs = [self.load(t["cos1"][:, :], T["cos1"], prev), self.load(t["sin1"][:, :], T["sin1"], prev)]
            self.dec_tok = self.load(t["decay"][:, :], T["decay"], prev)
            self.wa_tok = [self.load(t["WA"][0:16, 0:256], I["w_gla_a2"][l], self.glr_used),
                           self.load(t["WA"][16:17, 0:256], I["b_gla_a"][l].rearrange("(o c) -> o c", o=1), self.glr_used)]
            self.rq_tok, self.rk_tok, self.rv_tok = [None] * 4, [None] * 4, []
            used = [None, None]
            i = 0
            jobs = []
            for h in range(4):
                for dst, c0, toks in ((t["rq"], 0, self.rq_tok), (t["rk"], 512, self.rk_tok)):
                    def take(out, tok, i=i, dst=dst, toks=toks, h=h):
                        b, toks[h] = self.rope_pieces(out, dst[:, h, :], t["rT"][:, i % 2, :], t["cos1"][:, :],
                                                      t["sin1"][:, :], 64, 1.0, tok, tabs, used[i % 2])
                        used[i % 2] = toks[h]
                        return b
                    i += 1
                    jobs.append((w, c0 + 128 * h, take))
            drain(self.projects(jobs))
            for c in range(2):
                def keep(out, tok, u, c=c):
                    k = ac(lambda e: e.activation(t["rv"][:, 2 * u:2 * u + 2, c * 256:c * 256 + 256],
                                                  out[:, :].rearrange("p (t c) -> p t c", t=2), ACT.Copy), tok)
                    self.rv_tok.append(k)
                    return k
                drain(self.project_rows(w, 1024 + 256 * c, keep))
            rest = [q for q in range(4, 12)] if l == 0 else []
            self.big_order = ["b0", "b1"]
            weave(self.ret_attention(), self.fox_inputs(w), 1)
            self.big_order = ["b0", "b1", "b2"]
            fill = self.gla_inputs(w)
            weave(self.fox_norm(), fill, 2, False)
            weave(self.fox_attention(), fill, 1, False)
            drain(fill)
            weave(self.gla_attention(), self.gated(w, 1536, t["RO"], lambda: self.ro_tok, t["ErH"], t["ErL"]), 1)
            self.er_tok = self.gated_tok
            late_ada = (self.ada(0, q) for q in rest[0:2])
            weave(self.gated(w, 3088, t["GO"], lambda: self.go_tok, t["EgH"], t["EgL"]),
                  (y for g in late_ada for y in g), 2)
            self.eg_tok = self.gated_tok
            self.big_order = ["b0", "b1", "b2", "o"]
            ada = [(0, q) for q in rest[2:6]]

            def fill6():
                for a in ada:
                    yield from self.ada(*a)
            weave(self.mixing(l), fill6(), 1)
            self.mod_all = self.mod_tok
            pe.wait(self.mod_tok)
            ve.wait(self.mod_tok)
            tok, A, B = mods(l, 1)
            drain(self.out_proj(I["w_o"][l], 8, t["MH"], t["ML"], self.mix_tok, t["MOD"][:, l, 16:24],
                                self.x_norm(A, B, tok)))
            c = self.pcol(l, "w_conv")
            cb = self.pcol(l, "b_conv")
            conv = (lambda j, f, c=c: t["PAR"][:, c + 22 * j + f:c + 22 * j + f + 1],
                    lambda f, cb=cb: t["PAR"][:, cb + f:cb + f + 1])

            def fill_next(l=l, rest=rest):
                for q in rest[6:]:
                    yield from self.ada(l, q)
                if l + 1 < DEPTH:
                    for q in range(12):
                        yield from self.ada(l + 1, q)
            fill = fill_next()
            weave(self.ffn_up(I["w_up"][l], 0, I["w_up"][l], FF, conv), fill, 1, False)
            if l + 1 < DEPTH:
                tok, A, B = mods(l + 1, 0)
                norm = self.x_norm(A, B, tok)
            else:
                norm = self.x_norm(t["PAR"][:, 512:520], None, self.par_tok)
            weave(self.out_proj(I["w_down"][l], KF, t["FH"], t["FL"], self.ff_tok, t["MOD"][:, l, 40:48], norm), fill)
            ve.wait(self.mod_tok)
            self.big_order = ["b0", "b1", "b2"]
        self.big_order = ["b0", "b1", "b2", "o"]
        drain(self.pool_mixer(self.x_norm(t["PAR"][:, 528:536], None, self.par_tok)))
        drain(self.ffn_up(I["ffn_w_gate_2"][0], 0, I["ffn_w_up_2"][0], 0, None))
        drain(self.out_proj(I["ffn_w_down_2"][0], KF, t["FH"], t["FL"], self.ff_tok, None,
                            self.x_norm(t["PAR"][:, 520:528], None, self.par_tok)))
        prev = self.last
        self.tab_tok = [self.load(t["cos2"][:, :], T["cos2"], prev), self.load(t["sin2"][:, :], T["sin2"], prev)]
        heads = self.attn_heads()
        ready = 0
        for piece in self.attn_inputs():
            if piece is not None:
                ready += 8
            if ready:
                ready -= 1
                next(heads)
        drain(heads)
        self.attn_merge()
        self.big_order = ["b0", "b1", "b2", "o"]
        drain(self.out_proj(I["attn_w_out_2"][0], 8, t["YH"], t["YL"], self.y_tok, None,
                            self.x_norm(t["PAR"][:, 536:544], None, self.par_tok)))
        drain(self.ffn_up(I["ffn_w_gate_2"][1], 0, I["ffn_w_up_2"][1], 0, None))
        last = self.finish()
        drain(self.out_proj(I["ffn_w_down_2"][1], KF, t["FH"], t["FL"], self.ff_tok, None, last))
        drain(last)


def places(nc):
    with ExitStack() as ctx:
        base = (nc.sbuf_base + 63) // 64 * 64
        TB = S * 4
        ctx.enter_context(nc.sbuf_tensor("arena", [128, (nc.sbuf_usable_end - base) // 4 - 64], F32))
        at = [base]
        t = {}

        def fixed(name, shape, dt=F32):
            n = int(np.prod(shape[1:])) * 4
            t[name] = nc.alloc_sbuf_tensor_at(name, shape, dt, offset=at[0])
            at[0] += (n + 31) // 32 * 32

        fixed("X", [128, 8, S])
        t["OT"] = nc.alloc_sbuf_tensor_at("OT", [128, 4, D], F32, offset=at[0])
        fixed("HH", [128, 8, S], F32R)
        fixed("HL", [128, 8, S], F32R)
        raw = nc.alloc_sbuf_tensor_at("raw", [128, NSLOT, 1024], F32, offset=at[0])
        fixed("lo", [128, NSLOT, 1024], F32R)
        fixed("hi", [128, NSLOT, 1024], F32R)
        fixed("CON", [128, CON_W])
        c = 0
        for name, n in CON:
            t[name] = t["CON"][:, c:c + n]
            c += n
        for name, n in (("PAR", 640), ("ones", 2), ("eps", 2),
                        ("CA", 8), ("RS", 16), ("RS2", 32), ("GQ", 2), ("BF", 2), ("foxM", 16), ("foxR", 16),
                        ("AD", 16), ("aM", 64), ("aNM", 64), ("aDEN", 64), ("aR", 64), ("aL", 64)):
            fixed(name, [128, n])
        fixed("WA", [128, 256])
        t["one"], t["aLT"] = t["ones"], t["aNM"]
        fixed("MOD", [128, 2, 48])
        fixed("NA", [128, 4, 8])
        fixed("aG", [128, 9, 4])
        fixed("AA", [128, S])
        big = at[0]
        assert big + 49 * TB <= nc.sbuf_usable_end, big + 49 * TB - nc.sbuf_usable_end

        def area(name, tile, shape, dt=F32):
            t[name] = nc.alloc_sbuf_tensor_at(name, shape, dt, offset=big + int(tile * TB))
            assert big + int(tile * TB) + int(np.prod(shape[1:])) * 4 <= big + 49 * TB, name

        area("SQ", 44, [128, 2, S])
        area("NT", 46, [128, 4, 256])
        area("SS", 48, [128, S])
        area("XS", 0, [128, 4, D])
        area("PST", 20, [128, 5, 128])
        area("rq", 0, [128, 4, S])
        area("rk", 4, [128, 4, S])
        area("rv", 8, [128, 4, S])
        area("fq", 12, [128, 4, S])
        area("fk", 16, [128, 4, S])
        area("fv", 20, [128, 4, S])
        area("RO", 24, [128, 4, S])
        area("EfH", 28, [128, 4, S], F32R)
        area("EfL", 32, [128, 4, S], F32R)
        area("cos1", 36, [128, S])
        area("sin1", 37, [128, S])
        area("decay", 38, [128, 4 * S])
        area("rT", 28, [128, 2, S])
        area("retP", 42, [128, 4, S])
        area("retO", 34, [128, 2, S])
        area("retS", 30, [128, 2, S])
        area("foxS", 32, [128, 2, S])
        area("GLR", 46, [128, S])
        area("FFR", 47, [128, S])
        area("FFT", 48, [128, S])
        area("foxP", 37, [128, 3, S])
        area("foxT", 40, [128, 3, S])
        area("foxC", 43, [128, 2, S])
        area("gk", 0, [128, 4, 256])
        area("gv", 2, [128, 4, S])
        area("gq", 6, [128, 2, S])
        area("SA", 8, [128, 2, 8, 128])
        area("GO", 20, [128, 4, S])
        area("ErH", 12, [128, 4, S], F32R)
        area("ErL", 16, [128, 4, S], F32R)
        area("EgH", 0, [128, 4, S], F32R)
        area("EgL", 4, [128, 4, S], F32R)
        area("LA", 37, [128, 2, S])
        area("TA", 39, [128, 2, S])
        area("ED", 41, [128, 2, S])
        area("glaS", 43, [128, 2, S])
        area("GT", 45, [128, 4, S])
        area("MH", 36, [128, 8, S], F32R)
        area("ML", 20, [128, 8, S], F32R)
        area("SG", 8, [128, 2, S])
        area("MX", 10, [128, 2, S])
        area("FH", 0, [128, KF, S], F32R)
        area("FL", KF, [128, KF, S], F32R)
        area("CB", 44, [128, 2, S])
        area("PH", 0, [128, 8, S], F32R)
        area("PL", 8, [128, 8, S], F32R)
        area("ZH", 16, [128, 8, S], F32R)
        area("ZL", 24, [128, 8, S], F32R)
        area("U", 32, [128, 2, S])
        area("W1", 34, [128, 2, S])
        area("W2", 36, [128, 2, S])
        area("aq", 0, [128, 8, S])
        area("ak", 8, [128, 8, S])
        area("av", 16, [128, 4, D])
        area("MO", 24, [128, 8, S])
        area("cos2", 32, [128, S])
        area("sin2", 33, [128, S])
        area("aT", 34, [128, 2, S])
        area("aP", 36, [128, 6, 256])
        area("aPT", 39, [128, 6, 256])
        area("ALP", 32, [128, 3, S])
        area("aTM", 35, [128, 2, S])
        area("aE", 37, [128, 3, S])
        area("YH", 0, [128, 8, S], F32R)
        area("YL", 8, [128, 8, S], F32R)

        bank = {b: ctx.enter_context(nc.psum_tensor(b, [128, S], F32))
                for b in ("b0", "b1", "b2", "s0", "s1", "t0", "t1", "o")}
        return ctx.pop_all(), t, raw, bank


def build(nc, I, T, out):
    stack, t, raw, bank = places(nc)
    with stack as ctx:
        mem = {"raw": raw, "hi": t["hi"], "lo": t["lo"], "t": t, "bank": bank, "tables": T}

        def sem(name):
            return ctx.enter_context(nc.semaphore(name))

        sems = (sem("s_pe"), sem("s_ve"), sem("s_ac"), sem("s_po"), [sem(f"s_ring{i}") for i in range(NSLOT + 2)],
                [sem(f"s_misc{i}") for i in range(16)], [sem(f"s_out{i}") for i in range(4)])
        draft = Program(nc, I, out, sems, mem, None)
        draft.run()
        p = Program(nc, I, out, sems, mem, draft.descs)
        p.run()
        block = ctx.enter_context(nc.Block())

        @block.sync
        def _(e):
            p.sp.emit(e)

        @block.tensor
        def _(e):
            p.pe.emit(e)

        @block.vector
        def _(e):
            p.ve.emit(e)

        @block.scalar
        def _(e):
            p.ac.emit(e)

        @block.gpsimd
        def _(e):
            p.po.emit(e)


_INS = ['x', 'w_ada', 'w_in', 'w_gla_a2', 'b_gla_a', 'b_fox_f', 'w_br', 'w_mg', 'w_o', 'w_up', 'w_down', 'pool_w_in_2',
        'pool_w_group_2', 'pool_w_out_2', 'attn_w_qkv_2', 'attn_w_out_2', 'ffn_w_gate_2', 'ffn_w_up_2', 'ffn_w_down_2']
_OUTS = [((1, 512, 1024), 'float32')]


def kernel(**inputs):
    import numpy as _np
    import concourse.bacc as _bacc
    from concourse import mybir as _mybir
    from concourse.bass_utils import run_bass_kernel_spmd as _run

    nc = _bacc.Bacc("TRN2", target_bir_lowering=False, num_devices=1)
    arrays, ins, tabs = {}, {}, {}
    for name in _INS:
        a = _np.ascontiguousarray(inputs[name])
        arrays[f"in_{name}_dram"] = a
        ins[name] = nc.dram_tensor(f"in_{name}_dram", a.shape, _mybir.dt.from_np(a.dtype), kind="ExternalInput").ap()
    rows = _np.zeros((5, 128, 128), _np.float32)
    parts = [(2 * l, [inputs[name][l] for name, _ in COL_A]) for l in range(DEPTH)]
    parts += [(2 * l + 1, [inputs["w_conv"][l]]) for l in range(DEPTH)]
    parts.append((4, [inputs[name] for name in ("norm_mix_2", "norm_ffn_2", "norm_final_2", "pool_scale_2", "c")]))
    for j, part in parts:
        flat = _np.concatenate([_np.asarray(a).reshape(-1, 128) for a in part])
        rows[j, :flat.shape[0]] = flat
    arrays["in_params_dram"] = rows
    ins["params"] = nc.dram_tensor("in_params_dram", rows.shape, _mybir.dt.float32, kind="ExternalInput").ap()
    for name, a in tables().items():
        arrays[f"tab_{name}_dram"] = a
        tabs[name] = nc.dram_tensor(f"tab_{name}_dram", a.shape, _mybir.dt.from_np(a.dtype), kind="ExternalInput").ap()
    shape, dtype = _OUTS[0]
    out = nc.dram_tensor("out_0_dram", shape, _mybir.dt.from_np(_np.dtype(dtype)), kind="ExternalOutput").ap()
    build(nc, ins, tabs, out)
    r = _run(nc, [arrays], core_ids=[0])
    return r.results[0]["out_0_dram"]
```

```python
from contextlib import ExitStack

import concourse.bass as bass
import numpy as np
from concourse import mybir

F32 = mybir.dt.float32
F32R = mybir.dt.float32r
ALU = mybir.AluOpType
ACT = mybir.ActivationFunctionType
AXX = mybir.AxisListType.X

S = 512
D = 1024
KD = D // 128
FF = 2816
KF = FF // 128
DEPTH = 2
EPS = 1e-6
NSLOT = 6
AHEAD = 4
NEG = -1e30
PACE = 2
COL_A = [("b_ada", 48), ("b_mg", 24), ("norm1_g", 8), ("norm2_g", 8), ("ret_norm_g", 4), ("gla_norm_g", 1),
         ("q_norm_g", 1), ("k_norm_g", 1), ("b_conv", 22)]


CON = [("ident", 128), ("tail", 128), ("window", 256), ("dil", 128), ("chunk", 2),
       ("CT", 64), ("sel", 512)]
CON_W = sum(n for _, n in CON)


def tables():
    i = np.arange(128)
    out = {}
    out["ident"] = np.eye(128)
    out["tail"] = ((i[:, None] // 64 == i[None, :] // 64) & (i[:, None] > i[None, :])) * 1.0
    out["chunk"] = (i[:, None] // 64 == np.arange(2)[None, :]) * 1.0
    kj = np.arange(256)
    dist = 128 + i[:, None] - kj[None, :]
    out["window"] = np.where((dist >= 0) & (dist <= 128), 0.0, NEG)
    out["dil"] = np.where((i[:, None] >= i[None, :]) & ((i[:, None] - i[None, :]) % 4 == 0), 0.0, NEG)
    out["sel"] = np.concatenate([np.zeros((96, 512)), np.repeat(np.eye(4), 128, axis=1), np.zeros((28, 512))])
    t = np.arange(S, dtype=np.float64)
    f = 10000.0 ** (-np.arange(64) / 64.0)
    ang = f[:, None] * t[None, :]
    out["cos1"] = np.concatenate([np.cos(ang), np.cos(ang)])
    out["sin1"] = np.concatenate([-np.sin(ang), np.sin(ang)])
    f = 10000.0 ** (-np.arange(32) / 32.0)
    ang = f[:, None] * t[None, :]
    out["cos2"] = np.concatenate([np.cos(ang)] * 4)
    out["sin2"] = np.concatenate([-np.sin(ang), np.sin(ang)] * 2)
    lg = np.log1p(-np.exp2(-5.0 - np.arange(4)))
    q = np.arange(S)[None, :]
    j = i[:, None]
    live = (q // 64) >= (j // 64)
    dec = [np.where(live, np.exp(np.abs(q - j) * g), 0.0) * 128 ** -0.5 for g in lg]
    out["decay"] = np.concatenate(dec, axis=1)
    cnt = [np.broadcast_to(1.0 / np.minimum(np.arange(16) + 1, w), (128, 16)) for w in (2, 4, 8, 16)]
    out["CT"] = np.concatenate(cnt, axis=1)
    out["con"] = np.concatenate([out.pop(name) for name, _ in CON], axis=1)
    return {k: np.ascontiguousarray(v, dtype=np.float32) for k, v in out.items()}


BUSY = "busy"


class Lane:

    def __init__(self, sem):
        self.sem, self.queue, self.count, self.seen = sem, [], 0, {}

    def wait(self, *toks):
        for tok in toks:
            if tok is None:
                continue
            if isinstance(tok, list) or isinstance(tok[0], tuple) or tok[0] is None:
                self.wait(*tok)
                continue
            sem, value = tok
            if self.seen.get(id(sem), 0) < value:
                self.seen[id(sem)] = value
                self.queue.append(lambda e, s=sem, v=value: e.wait_ge(s, v))

    def go(self, fn, *toks):
        self.wait(*toks)
        self.queue.append(fn)

    def __call__(self, fn, *toks):
        self.wait(*toks)
        self.count += 1
        self.queue.append(lambda e, s=self.sem: fn(e).then_inc(s, 1))
        return (self.sem, self.count)

    def emit(self, e):
        for f in self.queue:
            f(e)


class Flow:

    def __init__(self, lane, sem):
        self.lane, self.sem, self.count = lane, sem, 0

    def __call__(self, out, in_, *toks):
        self.lane.wait((self.sem, self.count) if self.count else None, *toks)
        self.count += 16
        self.lane.queue.append(lambda e, s=self.sem: e.dma_start(out, in_).then_inc(s, 16))
        return (self.sem, self.count)


def bc(col, n):
    return col.to_broadcast([col.shape[0], n])


def drain(gen):
    for _ in gen:
        pass


def beside(main, other, most):
    for step in main:
        if most:
            most -= 1
            next(other, None)
        yield step


def weave(main, fill, per=1, whole=True):
    for step in main:
        for _ in range(per if step is not BUSY else 0):
            next(fill, None)
    if whole:
        drain(fill)


class Program:
    def __init__(self, nc, I, out, sems, mem, plan):
        self.nc, self.I, self.out, self.mem, self.plan = nc, I, out, mem, plan
        (s_pe, s_ve, s_ac, s_po, s_ring, s_misc, s_out) = sems
        self.pe, self.ve, self.ac, self.po = Lane(s_pe), Lane(s_ve), Lane(s_ac), Lane(s_po)
        self.sp = Lane(None)
        self.ring_flow = [Flow(self.sp, s) for s in s_ring]
        self.misc = [Flow(self.sp, s) for s in s_misc]
        self.mi = 0
        self.out_flow = [Flow(self.sp, s) for s in s_out]
        self.descs = []
        self.n_dma = 0
        self.n_split = 0
        self.ahead = AHEAD
        self.dma_tok, self.split_tok, self.done_tok = {}, {}, {}
        self.free = {b: None for b in mem["bank"]}
        self.big_order = ["b0", "b1", "b2"]
        self.big_i = 0
        self.HT = [None] * KD
        self.t = mem["t"]

    def load(self, out, in_, *toks):
        f = self.misc[self.mi % len(self.misc)]
        self.mi += 1
        return f(out, in_, *toks)

    def need(self, desc, pair=False):
        n = len(self.descs)
        if pair and n % NSLOT == NSLOT - 1:
            self.descs.append(None)
            n += 1
        self.descs.append(desc)
        self.pump(n)
        return n

    def pump(self, n):
        plan = self.plan if self.plan is not None else self.descs
        def freed(m):
            m -= NSLOT
            if m >= 0 and plan[m] is None:
                m -= NSLOT
            return (True, None) if m < 0 else (m in self.done_tok, self.done_tok.get(m))

        while self.n_dma < len(plan) and self.n_dma <= n + NSLOT - 1:
            m = self.n_dma
            known, free = freed(m)
            if not known:
                break
            if plan[m] is not None:
                s = m % NSLOT
                for sub, (dst, src) in enumerate(plan[m][1]):
                    f = self.ring_flow[s if sub == 0 else NSLOT + sub - 1]
                    tok = f(dst(self.mem["raw"][:, s, :]), src, free)
                    self.dma_tok.setdefault(m, []).append(tok)
            self.n_dma += 1
        while self.n_split < self.n_dma and self.n_split <= n + self.ahead:
            m = self.n_split
            if plan[m] is not None and plan[m][0]:
                s = m % NSLOT
                w = plan[m][2]
                raw, hi, lo = (self.mem[x][:, s, 0:w] for x in ("raw", "hi", "lo"))
                th = self.ac(lambda e, o=hi, i=raw: e.activation(o, i, ACT.Copy), self.dma_tok[m], freed(m)[1])
                self.split_tok[m] = self.po(
                    lambda e, o=lo, i=raw, h=hi: e.tensor_tensor(o, i, h.bitcast(F32), ALU.subtract), th)
            elif plan[m] is not None:
                self.split_tok[m] = self.dma_tok[m]
            self.n_split += 1
        assert n in self.split_tok

    def weight(self, ap, r0, kt, c0, w, pair=False):
        src = ap[r0:r0 + kt * 128, c0:c0 + w].rearrange("(k p) c -> p k c", p=128)
        return self.need((True, [(lambda r, kt=kt, w=w: r[:, 0:kt * w].rearrange("p (k c) -> p k c", k=kt), src)],
                          kt * w), pair)

    def views(self, n, kt, w):
        s = n % NSLOT
        return tuple(self.mem[x][:, s, 0:kt * w].rearrange("p (k c) -> p k c", k=kt) for x in ("hi", "lo"))

    def pair_views(self, n):
        s = n % NSLOT
        return tuple(self.mem[x][:, s:s + 2, :].rearrange("p h (k c) -> p h k c", k=8) for x in ("hi", "lo"))

    def bank(self):
        b = self.big_order[self.big_i % len(self.big_order)]
        self.big_i += 1
        before, self.free[b] = self.free[b], BUSY
        assert before is not BUSY
        return b, before

    def dot(self, out, terms, start=True, stop=True, toks=()):
        tok = None
        total = len(terms)
        for k, (wh, wl, xh, xl, t) in enumerate(terms):
            self.pe.wait(t, list(toks) if k == 0 else None)
            for a, (w, x) in enumerate(((wh, xh), (wh, xl), (wl, xh))):
                first = start and k == 0 and a == 0
                last = stop and k == total - 1 and a == 2
                f = lambda e, w=w, x=x, fi=first, la=last: e.matmul(out, w, x, start=fi, stop=la)
                if k == total - 1 and a == 2:
                    tok = self.pe(f)
                else:
                    self.pe.go(f)
            if k % 4 == 3 and k != total - 1:
                yield None
        self.last = tok
        yield None
        return tok

    def project(self, ap, c0, then):
        n = self.weight(ap, 0, 8, c0, 128)
        hi, lo = self.views(n, 8, 128)
        yield from self.tile_of(n, hi, lo, then)

    def projects(self, jobs, group=3):
        HH, HL = self.t["HH"], self.t["HL"]
        first = []
        self.ahead = 0
        for ap, c0, then in jobs[:group]:
            n = self.weight(ap, 0, 8, c0, 128)
            b, fr = self.bank()
            first.append((n, *self.views(n, 8, 128), self.mem["bank"][b], b, fr, then))
        for hf in range(2):
            c = slice(256 * hf, 256 * hf + 256)
            for k in range(8):
                if hf == 0 and k in ((0, 3, 5) if self.half_left else (3, 5)):
                    next(self.norm)
                    if k == 5:
                        self.ahead = AHEAD
                        self.pump(first[-1][0])
                for n, hi, lo, out, b, fr, then in first:
                    self.pe.wait(self.H2[hf][k], (self.split_tok[n], fr) if k == 0 else None)
                    for a, (w, x) in enumerate(((hi, HH), (hi, HL), (lo, HH))):
                        f = lambda e, out=out, w=w, x=x, k=k, a=a, c=c: e.matmul(
                            out[:, c], w[:, k, :], x[:, k, c], start=(k == 0 and a == 0), stop=(k == 7 and a == 2))
                        tok = self.pe(f) if k == 7 and a == 2 else self.pe.go(f)
                    if hf == 1 and k == 7:
                        self.done_tok[n] = tok
                        self.free[b] = then(out, tok)
        self.HT = self.H2[1]
        yield BUSY
        for i, job in enumerate(jobs[group:]):
            for _ in self.project(*job):
                yield BUSY if i < 2 else None

    def tile_of(self, n, hi, lo, then):
        b, fr = self.bank()
        out = self.mem["bank"][b]
        HH, HL = self.t["HH"], self.t["HL"]
        terms = [(hi[:, k, :], lo[:, k, :], HH[:, k, :], HL[:, k, :], self.HT[k]) for k in range(8)]
        tok = yield from self.dot(out[:, :], terms, toks=(self.split_tok[n], fr))
        self.done_tok[n] = tok
        self.free[b] = then(out, tok)

    def project_rows(self, ap, c0, then, rows=None):
        na = self.weight(ap, 0, 8, c0, 128, pair=True)
        nb = self.weight(ap, 0, 8, c0 + 128, 128)
        assert nb == na + 1 and na % NSLOT != NSLOT - 1
        hi, lo = self.pair_views(na)
        HH, HL = self.t["HH"], self.t["HL"]
        for u in range(2):
            b, fr = self.bank()
            out = self.mem["bank"][b]
            for t in (2 * u, 2 * u + 1):
                pick = slice(t * 128, t * 128 + 128) if rows is None else rows(t)
                terms = [(HH[:, k, pick], HL[:, k, pick], hi[:, :, k, :], lo[:, :, k, :], self.HT[k])
                         for k in range(8)]
                o = out[:, (t % 2) * 256:(t % 2) * 256 + 256]
                tok = yield from self.dot(o, terms, toks=(self.split_tok[na], self.split_tok[nb], fr))
            self.free[b] = then(out, tok, u)
        self.done_tok[na] = self.done_tok[nb] = tok

    def colsq(self, sq, st, col, tok):
        ones = self.t["ones"]
        for t in range(4):
            f = lambda e, t=t: e.matmul(st[:, col + t:col + t + 1], sq[:, t * 128:t * 128 + 128], ones[:, 0:1],
                                        start=True, stop=True)
            if t == 3:
                return self.pe(f, tok)
            self.pe.go(f, tok)

    def rstd(self, st, col, n, width, tok, out):
        a = self.ac(lambda e: e.activation(out, st[:, col:col + n], ACT.Sqrt, bias=self.t["eps"][:, 0:1],
                                           scale=1.0 / width), tok)
        return self.ve(lambda e: e.reciprocal(out, out), a), a

    def spread(self, cols, bank, tok, n=4):
        out = self.mem["bank"][bank]
        ident = self.t["ident"]
        self.pe.wait(tok, self.free[bank])
        for t in range(n):
            f = lambda e, t=t: e.transpose(out[:, t * 128:t * 128 + 128], bc(cols[:, t:t + 1], 128), ident[:, :])
            if t == n - 1:
                return self.pe(f)
            self.pe.go(f)

    def x_update(self, d, bank, tok, gate, c):
        X = self.t["X"]
        out = self.mem["bank"][bank]
        if gate is None:
            a = self.ve(lambda e: e.tensor_tensor(X[:, d, c], out[:, c], X[:, d, c], ALU.add), tok)
        else:
            a = self.ve(lambda e: e.scalar_tensor_tensor(out=X[:, d, c], in0=out[:, c], scalar=gate, in1=X[:, d, c],
                                                         op0=ALU.mult, op1=ALU.add), tok)
        self.free[bank] = a
        self.square(d, a, c)

    def square(self, d, tok, c):
        X, SQ, SS = (self.t[k] for k in ("X", "SQ", "SS"))
        if self.late is not None:
            self.late()
            self.late = None
        i = d % 2
        if d == 0:
            self.ss_tok = self.ac(lambda e: e.activation(SS[:, c], X[:, d, c], ACT.Square), tok, self.ss_used)
            return
        q = self.ac(lambda e: e.activation(SQ[:, i, c], X[:, d, c], ACT.Square), tok, self.sq_used[i])
        if d == KD - 1:
            self.sq_tok = q
            return

        def late():
            self.ss_tok = self.sq_used[i] = self.ve(
                lambda e: e.tensor_tensor(SS[:, c], SS[:, c], SQ[:, i, c], ALU.add), q, self.ss_tok)
        self.late = late

    def sums(self, hf):
        SQ, SS, RS, ones = (self.t[k] for k in ("SQ", "SS", "RS", "ones"))
        b = ("t1", "s1")[hf]
        st = self.mem["bank"][b]
        assert self.late is None
        self.pe.wait(self.ss_tok, self.sq_tok, self.free[b])
        for t in range(2):
            c = slice(256 * hf + 128 * t, 256 * hf + 128 * t + 128)
            self.pe.go(lambda e, t=t, c=c: e.matmul(st[:, t:t + 1], SS[:, c], ones[:, 0:1], start=True, stop=False))
            p = self.pe(lambda e, t=t, c=c: e.matmul(st[:, t:t + 1], SQ[:, 1, c], ones[:, 0:1], start=False, stop=True))
        self.ss_used = self.sq_used[1] = p
        r, self.free[b] = self.rstd(st, 0, 2, D, p, RS[:, 2 * hf:2 * hf + 2])
        return r

    def x_norm(self, A, B, at):
        X, HH, HL, NT, RS = (self.t[k] for k in ("X", "HH", "HL", "NT", "RS"))
        for hf in range(2):
            r = self.sums(hf)
            yield None
            b = ("t0", "s0")[hf]
            sp = self.spread(RS[:, 2 * hf:2 * hf + 2], b, r, 2)
            row = self.mem["bank"][b]
            c = slice(256 * hf, 256 * hf + 256)
            toks, out = {}, [None] * KD

            def scale(k, c=c, row=row, sp=sp, toks=toks, b=b):
                i = k % 4
                v = self.ve(lambda e: e.scalar_tensor_tensor(out=NT[:, i, :], in0=X[:, k, c], scalar=A[:, k:k + 1],
                                                             in1=row[:, 0:256], op0=ALU.mult, op1=ALU.mult),
                            sp, at, self.nt_used[i])
                if B is None:
                    toks[k] = self.ac(lambda e: e.activation(HH[:, k, c], NT[:, i, :], ACT.Copy), v)
                else:
                    toks[k] = self.ac(lambda e: e.activation(HH[:, k, c], NT[:, i, :], ACT.Identity,
                                                             bias=B[:, k:k + 1]), v, at)
                self.free[b] = v

            def rest(k, c=c, toks=toks, out=out):
                i = k % 4
                if B is None:
                    l = self.ve(lambda e: e.tensor_tensor(HL[:, k, c], NT[:, i, :], HH[:, k, c].bitcast(F32),
                                                          ALU.subtract), toks[k])
                else:
                    l = self.ve(lambda e: e.scalar_tensor_tensor(out=HL[:, k, c], in0=NT[:, i, :],
                                                                 scalar=B[:, k:k + 1], in1=HH[:, k, c].bitcast(F32),
                                                                 op0=ALU.add, op1=ALU.subtract), toks[k])
                out[k] = self.nt_used[i] = l

            self.H2[hf] = out
            for k in range(KD + 1):
                if k < KD:
                    scale(k)
                if k:
                    rest(k - 1)
                if hf == 0 and k == 3:
                    yield None
            yield None

    def ada(self, l, q):
        w = self.I["w_ada"][l]
        AA, MOD, CA, ones, PAR = (self.t[k] for k in ("AA", "MOD", "CA", "ones", "PAR"))
        v = None
        for g in range(4):
            src = w[g * 256:(g + 1) * 256, q * 512:(q + 1) * 512].rearrange("(k p) c -> p k c", p=128)
            n = self.need((False, [(lambda r: r.rearrange("p (k c) -> p k c", k=2), src)], 1024))
            raw = self.mem["raw"][:, n % NSLOT, :]
            for k in range(2):
                kk = 2 * g + k
                if kk == 0:
                    v = self.ve(lambda e, r=raw: e.tensor_scalar(AA[:, :], r[:, 0:512], CA[:, 0:1], None, ALU.mult),
                                self.split_tok[n], self.ca_tok, self.aa_used)
                else:
                    v = self.ve(lambda e, r=raw, k=k, kk=kk: e.scalar_tensor_tensor(
                        out=AA[:, :], in0=r[:, k * 512:k * 512 + 512], scalar=CA[:, kk:kk + 1], in1=AA[:, :],
                        op0=ALU.mult, op1=ALU.add), self.split_tok[n], v)
            self.done_tok[n] = v
            yield None
            yield None
        b, fr = self.bank()
        out = self.mem["bank"][b]
        self.pe.wait(v, fr)
        for j in range(4):
            f = lambda e, j=j: e.matmul(out[:, j:j + 1], AA[:, j * 128:j * 128 + 128], ones[:, 0:1], start=True,
                                        stop=True)
            p = self.pe(f)
        self.aa_used = p
        c = self.pcol(l, "b_ada")
        self.free[b] = self.mod_tok = self.ve(
            lambda e: e.tensor_tensor(MOD[:, l, 4 * q:4 * q + 4], out[:, 0:4], PAR[:, c + 4 * q:c + 4 * q + 4],
                                      ALU.add), p, self.par_tok)

    def ada_row(self, l, q):
        w = self.I["w_ada"][l]
        AA, MOD, CA, ones, PAR = (self.t[k] for k in ("AA", "MOD", "CA", "ones", "PAR"))
        b, fr = self.bank()
        out = self.mem["bank"][b]
        self.pe.wait(self.ca_tok, fr)
        for g in range(4):
            src = w[g * 256:(g + 1) * 256, q * 512:(q + 1) * 512].rearrange("(k p) c -> p k c", p=128)
            n = self.need((False, [(lambda r: r.rearrange("p (k c) -> p k c", k=2), src)], 1024))
            raw = self.mem["raw"][:, n % NSLOT, :]
            for k in range(2):
                kk = 2 * g + k
                p = self.pe(lambda e, raw=raw, k=k, kk=kk: e.matmul(
                    out[0:1, :], CA[:, kk:kk + 1], raw[:, k * 512:k * 512 + 512], start=(kk == 0), stop=(kk == 7)),
                    self.split_tok[n])
            self.done_tok[n] = p
            yield None
        self.free[b] = a = self.ac(lambda e: e.activation(AA[0:1, :], out[0:1, :], ACT.Copy), p, self.aa_used)
        yield None
        b, fr = self.bank()
        col = self.mem["bank"][b]
        self.pe.wait(a, fr)
        for j in range(4):
            p = self.pe(lambda e, j=j: e.matmul(col[:, j:j + 1], AA[0:1, j * 128:j * 128 + 128], ones[0:1, 0:1],
                                                start=True, stop=True))
        self.aa_used = p
        c = self.pcol(l, "b_ada")
        self.free[b] = self.mod_tok = self.ve(
            lambda e: e.tensor_tensor(MOD[:, l, 4 * q:4 * q + 4], col[:, 0:4], PAR[:, c + 4 * q:c + 4 * q + 4],
                                      ALU.add), p, self.par_tok)
        yield None

    def pcol(self, l, name):
        c = l * 256
        for key, n in COL_A:
            if key == name:
                return c
            c += n
        assert name == "w_conv"
        return l * 256 + 128

    def rope_pieces(self, out, dst, tmp, cos, sin, half, scale, tok, tt, used):
        for p in range(0, 128, 2 * half):
            for d, s in ((p, p + half), (p + half, p)):
                a = self.ac(lambda e, d=d, s=s: e.activation(tmp[d:d + half, :], out[s:s + half, :], ACT.Copy,
                                                             scale=scale), tok, used)
        b = self.ve(lambda e: e.scalar_tensor_tensor(out=dst, in0=out[:, :], scalar=scale, in1=cos, op0=ALU.mult,
                                                     op1=ALU.mult), a, tt)
        c = self.ve(lambda e: e.tensor_tensor(tmp, tmp, sin, ALU.mult), a)
        return b, self.ve(lambda e: e.tensor_tensor(dst, dst, tmp, ALU.add), b, c)

    def ret_attention(self):
        q, k, v, O, dec = (self.t[x] for x in ("rq", "rk", "rv", "RO", "decay"))
        PT, SQ, RS, PAR = (self.t[x] for x in ("retP", "retS", "RS", "PAR"))
        bank, free, pe, ve, ac = self.mem["bank"], self.free, self.pe, self.ve, self.ac
        steps = [(h, j) for h in range(4) for j in range(4)]
        st = {}
        used = [None] * 4

        def score(n):
            h, j = steps[n]
            b = f"s{n % 2}"
            w = S - 128 * j
            p = pe(lambda e: e.matmul(bank[b][:, 0:w], k[:, h, j * 128:j * 128 + 128], q[:, h, j * 128:S], start=True,
                                      stop=True), self.rk_tok[h], self.rq_tok[h], free[b])
            free[b] = st[n] = ve(lambda e: e.tensor_tensor(PT[:, n % 4, 0:w], bank[b][:, 0:w],
                                                           dec[:, h * S:h * S + w], ALU.mult), p, used[n % 4],
                                 self.dec_tok)

        def value(n):
            h, j = steps[n]
            w = S - 128 * j
            ob = ("o", "t0")[h % 2]
            f = lambda e: e.matmul(bank[ob][:, j * 128:S], v[:, j, h * 128:h * 128 + 128], PT[:, n % 4, 0:w],
                                   start=(j == 0), stop=(j == 3))
            used[n % 4] = pe(f, st[n], self.rv_tok, free[ob] if j == 0 else None)
            if j == 3:
                st["s", h] = a = ac(lambda e: e.activation(SQ[:, h % 2, :], bank[ob][:, :], ACT.Square), used[n % 4],
                                    st.get(("sq", h - 2)))
                free[ob] = ve(lambda e: e.tensor_copy(O[:, h, :], bank[ob][:, :]), a)

        def sums(h):
            st["sq", h] = self.colsq(SQ[:, h % 2, :], bank["t1"], 4 * h, [st["s", h], free["t1"]])

        for n in range(len(steps) + 3):
            if n < len(steps):
                score(n)
            if 2 <= n <= len(steps) + 1:
                value(n - 2)
            if n >= 6 and (n - 6) % 4 == 0:
                sums((n - 6) // 4)
            yield None
        r, a = self.rstd(bank["t1"], 0, 16, 128, st["sq", 3], RS[:, 0:16])
        free["t1"] = a
        yield None
        c = self.pcol(self.l, "ret_norm_g")
        self.ro_tok = [None] * 4
        for h in range(4):
            b = f"t{h % 2}"
            s = self.spread(RS[:, 4 * h:4 * h + 4], b, r)
            free[b] = self.ro_tok[h] = ve(lambda e, h=h, b=b: e.scalar_tensor_tensor(
                out=O[:, h, :], in0=O[:, h, :], scalar=PAR[:, c + h:c + h + 1], in1=bank[b][:, :], op0=ALU.mult,
                op1=ALU.mult), s)
            yield None

    def fox_inputs(self, w):
        bank, pe, ve, ac = self.mem["bank"], self.pe, self.ve, self.ac
        q, k, v, SQ, RS2 = (self.t[x] for x in ("fq", "fk", "fv", "foxS", "RS2"))
        GLR, FFR, FFT, bf = (self.t[x] for x in ("GLR", "FFR", "FFT", "BF"))
        st = bank["b2"]
        sq_used = [None, None]
        prev = []
        l = self.l

        srcs = []
        for (d0, c0, n) in ((0, 3072, 96), (96, 5136, 4), (100, 3168, 28)):
            src = w[:, c0:c0 + n].rearrange("(k p) c -> p k c", p=128)
            srcs.append((lambda r, d0=d0, n=n: r.rearrange("p (k c) -> p k c", k=8)[:, :, d0:d0 + n], src))
        n = self.need((True, srcs, 1024))
        hi, lo = self.views(n, 8, 128)

        def small(out, tok):
            m = self.po(lambda e: e.memset(GLR[0:32, :], 1.0), self.glr_used, self.HT)
            m = self.po(lambda e: e.memset(FFT[:, :], 0.0), self.ffr_used)
            g = ve(lambda e: e.tensor_copy(GLR[0:16, :], out[0:16, :]), tok, m)
            self.glr_tok = g
            z = slice(96, 100)
            f = ve(lambda e: e.tensor_scalar(FFR[z, :], out[z, :], bf[z, l:l + 1], None, ALU.add), g,
                   self.par_tok, self.ffr_used)
            a = ac(lambda e: e.activation(FFT[z, :], FFR[z, :], ACT.Abs), f)
            a = ac(lambda e: e.activation(FFT[z, :], FFT[z, :], ACT.Exp, scale=-1.0), a)
            a = ac(lambda e: e.activation(FFT[z, :], FFT[z, :], ACT.Ln, bias=self.t["one"][z, 0:1]), a)
            b = ve(lambda e: e.scalar_tensor_tensor(out=FFT[z, :], in0=FFR[z, :], scalar=0.0, in1=FFT[z, :],
                                                    op0=ALU.min, op1=ALU.subtract), a)
            b = ve(lambda e: e.tensor_tensor_scan(FFR[z, :], bc(self.t["one"][z, 0:1], S), FFT[z, :], 0.0,
                                                  ALU.mult, ALU.add), b)
            self.cum_tok = ve(lambda e: e.tensor_scalar(FFT[z, :], FFR[z, :], -1.0, None, ALU.mult), b)
            return f

        yield from self.tile_of(n, hi, lo, small)

        for i, (dst, c0) in enumerate([(q, 3600 + 128 * h) for h in range(4)] + [(k, 4112 + 128 * h) for h in range(4)]):
            h = i % 4

            def take(out, tok, i=i, h=h, dst=dst):
                a = ac(lambda e: e.activation(SQ[:, i % 2, :], out[:, :], ACT.Square), tok, sq_used[i % 2])
                b = ve(lambda e: e.tensor_copy(dst[:, h, :], out[:, :]), a)
                prev.append((i, a, b))
                return b

            yield from self.project(w, c0, take)
            if i >= 1:
                j, a, b = prev[i - 1]
                sq_used[j % 2] = self.colsq(SQ[:, j % 2, :], st, 4 * j, [a, self.free["b2"]])
        self.fv_tok = []
        for c in range(2):
            def keep(out, tok, u, c=c):
                t = ac(lambda e: e.activation(v[:, 2 * u:2 * u + 2, c * 256:c * 256 + 256],
                                              out[:, :].rearrange("p (t c) -> p t c", t=2), ACT.Copy), tok)
                self.fv_tok.append(t)
                return t
            yield from self.project_rows(w, 4624 + 256 * c, keep)
            if c == 0:
                j, a, b = prev[7]
                p = self.colsq(SQ[:, j % 2, :], st, 4 * j, a)
                r, a = self.rstd(st, 0, 32, 128, p, RS2[:, 0:32])
                self.free["b2"] = a
                self.foxr = r
        yield None

    def fox_norm(self):
        bank, ve = self.mem["bank"], self.ve
        RS2, PAR, GQ = (self.t[x] for x in ("RS2", "PAR", "GQ"))
        cq, ck = self.pcol(self.l, "q_norm_g"), self.pcol(self.l, "k_norm_g")
        g = ve(lambda e: e.tensor_scalar(GQ[:, 0:1], PAR[:, cq:cq + 1], 128 ** -0.5, None, ALU.mult), self.par_tok)
        self.fq_tok, self.fk_tok = [None] * 4, [None] * 4
        for h in range(4):
            for i, dst, toks, col in ((h, self.t["fq"], self.fq_tok, GQ[:, 0:1]),
                                      (4 + h, self.t["fk"], self.fk_tok, PAR[:, ck:ck + 1])):
                b = ("t0", "t1", "s0", "s1")[2 * h % 4 + i // 4]
                s = self.spread(RS2[:, 4 * i:4 * i + 4], b, self.foxr)
                toks[h] = self.free[b] = ve(lambda e, dst=dst, col=col, b=b, h=h: e.scalar_tensor_tensor(
                    out=dst[:, h, :], in0=dst[:, h, :], scalar=col, in1=bank[b][:, :], op0=ALU.mult, op1=ALU.mult),
                    s, g)
            yield None

    def fox_attention(self):
        q, k, v, EH, EL = (self.t[x] for x in ("fq", "fk", "fv", "EfH", "EfL"))
        P, PT, M, R = (self.t[x] for x in ("foxP", "foxT", "foxM", "foxR"))
        CB = [self.t["foxC0"], self.t["foxC1"]]
        ncum, sel, ident = self.t["FFT"], self.t["sel"], self.t["ident"]
        bank, free, pe, ve, ac = self.mem["bank"], self.free, self.pe, self.ve, self.ac
        steps = [(h, i) for h in range(4) for i in range(4)]
        st = {}
        self.ef_tok = [None] * 4

        def bias(h):
            p = pe(lambda e: e.matmul(bank["o"][:, :], sel[:, h * 128:h * 128 + 128], ncum[:, :], start=True,
                                      stop=True), self.cum_tok, free["o"])
            free["o"] = st["c", h] = ac(lambda e: e.activation(CB[h % 2][:, :], bank["o"][:, :], ACT.Copy), p,
                                        st.get(("m", 4 * (h - 2) + 3)))

        def score(n):
            h, i = steps[n]
            b = f"s{n % 2}"
            w = 128 * (i + 1)
            o = bank[b]
            pe.go(lambda e: e.matmul(o[:, 0:w], q[:, h, i * 128:w], k[:, h, 0:w], start=True, stop=False),
                  self.fq_tok[h], self.fk_tok[h], free[b])
            p = pe(lambda e: e.matmul(o[:, i * 128:w], self.t["identR"][:, :], self.t["causalR"][:, :], start=False, stop=True))
            free[b] = st["m", n] = m = ve(lambda e: e.tensor_tensor_reduce(
                P[:, n % 3, 0:w], o[:, 0:w], CB[h % 2][:, 0:w], 1.0, -3e38, ALU.add, ALU.max, M[:, n:n + 1]), p,
                st["c", h], st.get(("t", n - 3)))
            m = ve(lambda e: e.tensor_scalar(M[:, n:n + 1], M[:, n:n + 1], -1.0, None, ALU.mult), m)
            st["x", n] = ac(lambda e: e.activation(P[:, n % 3, 0:w], P[:, n % 3, 0:w], ACT.Exp, bias=M[:, n:n + 1],
                                                   accum_out=R[:, n:n + 1]), m)

        def scale(n):
            w = 128 * (steps[n][1] + 1)
            r = ve(lambda e: e.reciprocal(R[:, n:n + 1], R[:, n:n + 1]), st["x", n])
            st["s", n] = ve(lambda e: e.tensor_scalar(P[:, n % 3, 0:w], P[:, n % 3, 0:w], R[:, n:n + 1], None,
                                                      ALU.mult), r)

        def turn(n):
            h, i = steps[n]
            b = f"t{n % 2}"
            pe.wait(st["s", n], free[b])
            for j in range(i + 1):
                f = lambda e, j=j: e.transpose(bank[b][:, j * 128:j * 128 + 128], P[:, n % 3, j * 128:j * 128 + 128],
                                               ident[:, :])
                p = pe(f) if j == i else pe.go(f)
            st["t", n] = p
            c0 = 1664 * (h % 2) + (384 if i == 3 else 0)
            dst = PT[:, c0:c0 + 1536].rearrange("p (j c) -> p j c", c=384)[:, 0:i + 1, 128 * (i % 3):128 * (i % 3) + 128]
            free[b] = st["p", n] = ac(lambda e: e.activation(
                dst, bank[b][:, 0:128 * (i + 1)].rearrange("p (j c) -> p j c", c=128), ACT.Copy), p,
                st.get(("v", h - 2)))

        def value(h):
            pe.wait(st["p", 4 * h + 3], self.fv_tok, free["o"])
            for j in range(4):
                c0 = 1664 * (h % 2) + 512 * j
                p = pe(lambda e, j=j, c0=c0: e.matmul(bank["o"][:, j * 128:S], v[:, j, h * 128:h * 128 + 128],
                                                      PT[:, c0:c0 + S - 128 * j], start=(j == 0), stop=(j == 3)))
            st["v", h] = p
            a = ac(lambda e: e.activation(EH[:, h, :], bank["o"][:, :], ACT.Copy), p)
            free["o"] = self.ef_tok[h] = ve(lambda e: e.tensor_tensor(
                EL[:, h, :], bank["o"][:, :], EH[:, h, :].bitcast(F32), ALU.subtract), a)

        N = len(steps)
        bias(0)
        bias(1)
        for n in range(N + 3):
            if n in (7, 11):
                bias((n + 1) // 4)
            if n < N:
                score(n)
            if 1 <= n <= N:
                scale(n - 1)
            if 2 <= n <= N + 1:
                turn(n - 2)
            if n >= 6 and n % 4 == 2:
                value((n - 6) // 4)
            yield None
        self.ffr_used = st["v", 3]

    def gla_inputs(self, w):
        gk, gv, gq = (self.t[x] for x in ("gk", "gv", "gq"))
        self.gk_tok, self.gv_tok, self.gq_tok = [], [], [None, None]

        def keep_k(out, tok, u):
            t = self.ac(lambda e: e.activation(gk[:, 2 * u:2 * u + 2, :], out[:, :].rearrange("p (t c) -> p t c", t=2),
                                               ACT.Copy), tok)
            self.gk_tok.append(t)
            return t

        yield from self.project_rows(w, 2304, keep_k)
        for c in range(2):
            def keep_v(out, tok, u, c=c):
                t = self.ac(lambda e: e.activation(gv[:, 2 * u:2 * u + 2, c * 256:c * 256 + 256],
                                                   out[:, :].rearrange("p (t c) -> p t c", t=2), ACT.Copy), tok)
                self.gv_tok.append(t)
                return t
            yield from self.project_rows(w, 2560 + 256 * c, keep_v)
        for c in range(2):
            def keep_q(out, tok, c=c):
                self.gq_tok[c] = self.ac(lambda e: e.activation(gq[:, c, :], out[:, :], ACT.Copy, scale=64 ** -0.5),
                                         tok)
                return self.gq_tok[c]
            yield from self.project(w, 2048 + 128 * c, keep_q)

    def gla_gates(self):
        LA, TA, GLR, WA = (self.t[x] for x in ("LA", "TA", "GLR", "WA"))
        bank, free, pe, ve, ac = self.mem["bank"], self.free, self.pe, self.ve, self.ac
        st = {}
        for u in range(2):
            o = bank[f"s{u}"]
            pe.wait(self.glr_tok, self.wa_tok, free[f"s{u}"])
            for t in (2 * u, 2 * u + 1):
                f = lambda e, t=t, o=o: e.matmul(o[:, (t % 2) * 256:(t % 2) * 256 + 256],
                                                 GLR[0:17, t * 128:t * 128 + 128], WA[0:17, 0:256], start=True, stop=True)
                st["z", u] = pe(f)
        self.glr_used = st["z", 1]
        yield None
        for u in range(2):
            st["a", u] = ac(lambda e, u=u: e.activation(TA[:, u, :], bank[f"s{u}"][:, :], ACT.Abs), st["z", u])
        for u in range(2):
            st["a", u] = ac(lambda e, u=u: e.activation(TA[:, u, :], TA[:, u, :], ACT.Exp, scale=-1.0), st["a", u])
        for u in range(2):
            st["a", u] = ac(lambda e, u=u: e.activation(TA[:, u, :], TA[:, u, :], ACT.Ln,
                                                        bias=self.t["one"][:, 0:1]), st["a", u])
            free[f"s{u}"] = st["l", u] = ve(lambda e, u=u: e.scalar_tensor_tensor(
                out=LA[:, u, :], in0=bank[f"s{u}"][:, :], scalar=0.0, in1=TA[:, u, :], op0=ALU.min,
                op1=ALU.subtract), st["a", u])
        yield None
        yield None
        self.la_tok = [st["l", 0], st["l", 1]]

    def gla_attention(self):
        gk, gv, gq, GO = (self.t[x] for x in ("gk", "gv", "gq", "GO"))
        LA, ED, AD, SA, SQ, RS, PAR = (self.t[x] for x in ("LA", "ED", "AD", "SA", "glaS", "RS", "PAR"))
        bank, free, pe, ve, ac = self.mem["bank"], self.free, self.pe, self.ve, self.ac
        st = {}
        yield from self.gla_gates()
        for u in range(2):
            pe.wait(self.la_tok[u], free[f"t{u}"])
            for t in range(2):
                f = lambda e, t=t, u=u: e.matmul(bank[f"t{u}"][:, t * 256:t * 256 + 256], self.t["tail"][:, :],
                                                 LA[:, u, t * 256:t * 256 + 256], start=True, stop=True)
                p = pe(f)
            free[f"t{u}"] = a = ac(lambda e, u=u: e.activation(ED[:, u, :], bank[f"t{u}"][:, :], ACT.Exp,
                                                               scale=1.0 / 16), p)
            st["k", u] = ve(lambda e, u=u: e.tensor_tensor(ED[:, u, :], ED[:, u, :],
                                                           gk[:, 2 * u:2 * u + 2, :].rearrange("p t c -> p (t c)"),
                                                           ALU.mult), a, self.gk_tok)
        pe.wait(free["s0"])
        for f2 in range(2):
            for t in range(4):
                f = lambda e, f2=f2, t=t: e.matmul(
                    bank["s0"][:, f2 * 8 + 2 * t:f2 * 8 + 2 * t + 2],
                    LA[:, t // 2, (t % 2) * 256 + f2 * 128:(t % 2) * 256 + f2 * 128 + 128],
                    self.t["chunk"][:, :], start=True, stop=True)
                p = pe(f)
        free["s0"] = st["ad"] = ac(lambda e: e.activation(AD[:, 0:16], bank["s0"][:, 0:16], ACT.Exp, scale=1.0 / 16), p)
        yield None
        yield None
        for p2 in range(2):
            kvb = ("s0", "s1", "t0", "t1")
            pe.wait(st["k", 0], st["k", 1], self.gv_tok, [free[b] for b in kvb])
            for n in range(8):
                c0, t = 64 * (n % 2), n // 2
                p = pe(lambda e, c0=c0, t=t, p2=p2, n=n: e.matmul(
                    bank[kvb[n % 2 + n // 4 * 2]][:, (n // 2 % 2) * 256:(n // 2 % 2) * 256 + 256],
                    ED[c0:c0 + 64, t // 2, (t % 2) * 256 + p2 * 128:(t % 2) * 256 + p2 * 128 + 128],
                    gv[c0:c0 + 64, t, p2 * 256:p2 * 256 + 256], start=True, stop=True))
            last = [None, None]
            for n in range(8):
                for hh in range(2):
                    r = slice(64 * hh, 64 * hh + 64)
                    c1 = (n // 2 % 2) * 256 + hh * 128
                    kv = bank[kvb[n % 2 + n // 4 * 2]][r, c1:c1 + 128]
                    if n == 0:
                        f = lambda e, kv=kv, p2=p2, r=r: e.tensor_copy(SA[r, p2, 0, :], kv)
                    else:
                        f = lambda e, kv=kv, n=n, p2=p2, r=r: e.scalar_tensor_tensor(
                            out=SA[r, p2, n, :], in0=SA[r, p2, n - 1, :], scalar=AD[r, p2 * 8 + n:p2 * 8 + n + 1],
                            in1=kv, op0=ALU.mult, op1=ALU.add)
                    s = last[hh] = ve(f, last[hh], p, st["ad"])
            for b in kvb:
                free[b] = s
            yield None
            st["S", p2] = s
        yield None
        for p2 in range(2):
            for hh in range(2):
                h = 2 * p2 + hh
                b = f"s{hh}"
                pe.wait(st["S", p2], self.gq_tok[p2], free[b])
                for n in range(8):
                    f = lambda e, n=n, b=b, p2=p2, hh=hh: e.matmul(
                        bank[b][:, n * 64:n * 64 + 64], SA[64 * hh:64 * hh + 64, p2, n, :],
                        gq[64 * hh:64 * hh + 64, p2, n * 64:n * 64 + 64], start=True, stop=True)
                    p = pe(f)
                a = ac(lambda e, b=b, hh=hh: e.activation(SQ[:, hh, :], bank[b][:, :], ACT.Square), p,
                       st.get(("sq", h - 2)))
                free[b] = ve(lambda e, b=b, h=h: e.tensor_copy(GO[:, h, :], bank[b][:, :]), a)
                st["s", h] = a
                yield None
                if h >= 1:
                    st["sq", h - 1] = self.colsq(SQ[:, (h - 1) % 2, :], bank["t1"], 4 * (h - 1),
                                                 [st["s", h - 1], free["t1"]])
        st["sq", 3] = self.colsq(SQ[:, 1, :], bank["t1"], 12, st["s", 3])
        r, a = self.rstd(bank["t1"], 0, 16, 128, st["sq", 3], RS[:, 0:16])
        free["t1"] = a
        yield None
        c = self.pcol(self.l, "gla_norm_g")
        self.go_tok = [None] * 4
        for h in range(4):
            b = f"t{h % 2}"
            s = self.spread(RS[:, 4 * h:4 * h + 4], b, r)
            free[b] = self.go_tok[h] = ve(lambda e, h=h, b=b: e.scalar_tensor_tensor(
                out=GO[:, h, :], in0=GO[:, h, :], scalar=PAR[:, c:c + 1], in1=bank[b][:, :], op0=ALU.mult,
                op1=ALU.mult), s)
            yield None

    def gated(self, w, c0, O, toks, EH, EL):
        G = self.t["GT"]
        ve, ac = self.ve, self.ac
        out_tok = [None] * 4
        for h in range(4):
            def take(out, tok, h=h):
                b = self.gt_i % 4
                self.gt_i += 1
                a = ac(lambda e: e.activation(G[:, b, :], out[:, :], ACT.Silu), tok, self.gt_used[b])
                m = ve(lambda e: e.tensor_tensor(G[:, b, :], G[:, b, :], O[:, h, :], ALU.mult), a, toks()[h])
                x = ac(lambda e: e.activation(EH[:, h, :], G[:, b, :], ACT.Copy), m)
                self.gt_used[b] = out_tok[h] = ve(lambda e: e.tensor_tensor(
                    EL[:, h, :], G[:, b, :], EH[:, h, :].bitcast(F32), ALU.subtract), x)
                return a
            yield from self.project(w, c0 + 128 * h, take)
        self.gated_tok = out_tok

    def mixing(self, l):
        wmg, wbr = self.I["w_mg"][l], self.I["w_br"][l]
        E = {n: (self.t[f"E{x}H"], self.t[f"E{x}L"], tk) for n, x, tk in ((0, "r", self.er_tok), (1, "g", self.eg_tok),
                                                                          (2, "f", self.ef_tok))}
        MH, ML, SG, MX, PAR = (self.t[x] for x in ("MH", "ML", "SG", "MX", "PAR"))
        ve, ac = self.ve, self.ac
        c = self.pcol(l, "b_mg")
        self.mix_tok = [None] * 8
        sg_used = [None] * 2
        sg_tok = [None] * 2
        mx_tok = [None] * 2
        for dp in range(4):
            for n in (0, 2, 1):
                for u in range(2):
                    d = 2 * dp + u

                    def gate(out, tok, u=u, d=d, n=n):
                        j = c + 8 * n + d
                        sg_tok[u] = ac(lambda e: e.activation(SG[:, u, :], out[:, :], ACT.Sigmoid,
                                                              bias=PAR[:, j:j + 1]), tok, sg_used[u])
                        return sg_tok[u]

                    yield from self.project(wmg, n * 1024 + d * 128, gate)
                m = self.weight(wbr[n], 0, 4, dp * 256, 256)
                hi, lo = self.views(m, 4, 256)
                H_, L_, tk = E[n]
                for u in range(2):
                    d = 2 * dp + u
                    b, fr = self.bank()
                    out = self.mem["bank"][b]
                    terms = [(hi[:, k, u * 128:u * 128 + 128], lo[:, k, u * 128:u * 128 + 128], H_[:, k, :], L_[:, k, :], tk[k])
                             for k in range(4)]
                    tok = yield from self.dot(out[:, :], terms, toks=(self.split_tok[m], fr))
                    if n == 0:
                        v = ve(lambda e, u=u, out=out: e.tensor_tensor(MX[:, u, :], out[:, :], SG[:, u, :], ALU.mult),
                               tok, sg_tok[u], mx_tok[u])
                        self.free[b] = sg_used[u] = v
                    else:
                        v = ve(lambda e, u=u, out=out: e.tensor_tensor(SG[:, u, :], out[:, :], SG[:, u, :], ALU.mult),
                               tok, sg_tok[u])
                        self.free[b] = v
                        v = ve(lambda e, u=u: e.tensor_tensor(MX[:, u, :], MX[:, u, :], SG[:, u, :], ALU.add), v,
                               mx_tok[u])
                        sg_used[u] = v
                    mx_tok[u] = v
                self.done_tok[m] = tok
            for u in range(2):
                d = 2 * dp + u
                a = ac(lambda e, u=u, d=d: e.activation(MH[:, d, :], MX[:, u, :], ACT.Copy), mx_tok[u])
                mx_tok[u] = self.mix_tok[d] = ve(lambda e, u=u, d=d: e.tensor_tensor(
                    ML[:, d, :], MX[:, u, :], MH[:, d, :].bitcast(F32), ALU.subtract), a)

    def out_proj(self, ap, kt, AH, AL, toks, gate, norm):
        self.ac.go(lambda e: e.activation(self.t["RS"][:, 8:9], self.t["eps"][:, 0:1], ACT.Sqrt))
        self.norm = norm
        bank = self.mem["bank"]
        halves = 7 if kt > 8 else 5
        col = lambda d: None if gate is None else gate[:, d:d + 1]

        def entries(d):
            for k0 in range(0, kt, 8):
                kn = min(8, kt - k0)
                n = self.weight(ap, k0 * 128, kn, d * 128, 128)
                yield (n, k0, kn, *self.views(n, kn, 128))

        def terms(k0, kn, hi, lo, c):
            return [(hi[:, k, :], lo[:, k, :], AH[:, k0 + k, c], AL[:, k0 + k, c], toks[k0 + k]) for k in range(kn)]

        whole = slice(0, S)
        start = 0
        if kt == 8:
            start = 3
            first = [(d, *next(entries(d)), *self.bank()) for d in range(start)]
            for k in range(kt):
                for d, n, k0, kn, hi, lo, b, fr in first:
                    self.pe.wait(toks[k], (self.split_tok[n], fr) if k == 0 else None)
                    for a, (w, x) in enumerate(((hi, AH), (hi, AL), (lo, AH))):
                        self.done_tok[n] = tok = self.pe(lambda e, b=b, w=w, x=x, k=k, a=a: e.matmul(
                            bank[b][:, :], w[:, k, :], x[:, k, :], start=(k == 0 and a == 0), stop=(k == 7 and a == 2)))
            for d, n, k0, kn, hi, lo, b, fr in first:
                self.x_update(d, b, self.done_tok[n], col(d), whole)
            yield None
        for d in range(start, halves):
            b, fr = self.bank()
            for n, k0, kn, hi, lo in entries(d):
                self.done_tok[n] = tok = yield from self.dot(
                    bank[b][:, :], terms(k0, kn, hi, lo, whole), start=(k0 == 0), stop=(k0 + kn == kt),
                    toks=(self.split_tok[n], fr))
            self.x_update(d, b, tok, col(d), whole)
        held = {d: list(entries(d)) for d in range(halves, KD)}
        self.half_left = kt == 8
        steps = 2 if self.half_left else 3
        for hf in range(2):
            c = slice(256 * hf, 256 * hf + 256)
            for d in held:
                b, fr = self.bank()
                for n, k0, kn, hi, lo in held[d]:
                    for _ in self.dot(bank[b][:, c], terms(k0, kn, hi, lo, c), start=(k0 == 0), stop=(k0 + kn == kt),
                                      toks=(self.split_tok[n], fr)):
                        if hf == 1 and steps:
                            next(norm)
                            steps -= 1
                        yield BUSY
                    tok = self.last
                    if hf == 1:
                        self.done_tok[n] = tok
                self.x_update(d, b, tok, col(d), c)

    def ffn_up(self, wu, cu, wg, cg, conv):
        AH, AL, CB, PAR = (self.t[x] for x in ("FH", "FL", "CB", "PAR"))
        ve, ac = self.ve, self.ac
        self.ff_tok = [None] * KF
        used = [None, None]
        hold = {}
        jobs = []
        for f in range(KF):
            def up(out, tok, f=f, i=f % 2):
                if conv is None:
                    hold[f] = ac(lambda e: e.activation(CB[:, i, :], out[:, :], ACT.Silu), tok, used[i])
                    return hold[f]
                wc, bcol = conv
                a = ac(lambda e: e.activation(CB[:, i, :], out[:, :], ACT.Identity, scale=wc(2, f), bias=bcol(f)), tok,
                       used[i], self.par_tok)
                v = ve(lambda e: e.scalar_tensor_tensor(out=CB[:, i, 1:S], in0=out[:, 0:S - 1], scalar=wc(1, f),
                                                        in1=CB[:, i, 1:S], op0=ALU.mult, op1=ALU.add), a)
                v = ve(lambda e: e.scalar_tensor_tensor(out=CB[:, i, 2:S], in0=out[:, 0:S - 2], scalar=wc(0, f),
                                                        in1=CB[:, i, 2:S], op0=ALU.mult, op1=ALU.add), v)
                hold[f] = ac(lambda e: e.activation(CB[:, i, :], CB[:, i, :], ACT.Silu), v)
                return v

            def gate(out, tok, f=f, i=f % 2):
                v = ve(lambda e: e.tensor_tensor(CB[:, i, :], CB[:, i, :], out[:, :], ALU.mult), tok, hold[f])
                a = ac(lambda e: e.activation(AH[:, f, :], CB[:, i, :], ACT.Copy), v)
                used[i] = self.ff_tok[f] = ve(lambda e: e.tensor_tensor(
                    AL[:, f, :], CB[:, i, :], AH[:, f, :].bitcast(F32), ALU.subtract), a)
                return v

            jobs += [(wu, cu + f * 128, up), (wg, cg + f * 128, gate)]
        yield from self.projects(jobs)

    def pool_mixer(self, norm):
        I, t = self.I, self.t
        bank, free, pe, ve, ac = self.mem["bank"], self.free, self.pe, self.ve, self.ac
        U, W1, W2, PH, PL, ZH, ZL, CT, PAR = (t[x] for x in ("U", "W1", "W2", "PH", "PL", "ZH", "ZL", "CT", "PAR"))
        p_tok = [None] * 8
        jobs = []
        for g in (3, 2, 1, 0):
            for c in range(2):
                d = 2 * g + c
                i = d % 2

                def take(out, tok, g=g, d=d, i=i):
                    u = ac(lambda e: e.activation(U[:, d % 4, :], out[:, :], ACT.Copy), tok,
                           p_tok[d + 4] if d < 4 else None)
                    src, v = U[:, d % 4, :], u
                    for s in range(g + 1):
                        k = 1 << s
                        dst = (W1 if s % 2 == 0 else W2)[:, i, :]
                        a = ve(lambda e, dst=dst, src=src, k=k: e.tensor_copy(dst[:, 0:k], src[:, 0:k]), v)
                        v = ve(lambda e, dst=dst, src=src, k=k: e.tensor_tensor(dst[:, k:S], src[:, k:S],
                                                                                src[:, 0:S - k], ALU.add), v)
                        v = [a, v]
                        src = dst
                    w = 2 << g
                    oth = (W1 if g % 2 == 1 else W2)[:, i, :]
                    a = ve(lambda e: e.tensor_tensor(oth[:, 0:16], src[:, 0:16], CT[:, g * 16:g * 16 + 16], ALU.mult), v)
                    b = ve(lambda e: e.scalar_tensor_tensor(out=oth[:, 16:S], in0=src[:, 16:S], scalar=1.0 / w,
                                                            in1=U[:, d % 4, 16:S], op0=ALU.mult, op1=ALU.subtract))
                    a = ve(lambda e: e.tensor_tensor(oth[:, 0:16], oth[:, 0:16], U[:, d % 4, 0:16], ALU.subtract), a)
                    h = ve(lambda e: e.tensor_copy(PH[:, d, :], oth[:, :]), a, b)
                    p_tok[d] = ve(lambda e: e.tensor_tensor(PL[:, d, :], oth[:, :], PH[:, d, :].bitcast(F32),
                                                            ALU.subtract), h)
                    return u

                jobs.append((I["pool_w_in_2"][0], d * 128, take))
        yield from self.projects(jobs)
        z_tok = [None] * 8
        c0 = 512 + 40
        for g in (3, 2, 1, 0):
            if g % 2:
                n = self.weight(I["pool_w_group_2"][0].rearrange("g r c -> (g r) c"), (g - 1) * 256, 4, 0, 256)
                hi, lo = self.views(n, 4, 256)
            for c in range(2):
                d = 2 * g + c
                b, fr = self.bank()
                out = bank[b]
                terms = [(hi[:, g % 2 * 2 + k, c * 128:c * 128 + 128], lo[:, g % 2 * 2 + k, c * 128:c * 128 + 128],
                          PH[:, 2 * g + k, :], PL[:, 2 * g + k, :], p_tok[2 * g + k]) for k in range(2)]
                tok = yield from self.dot(out[:, :], terms, toks=(self.split_tok[n], fr))
                sc = PAR[:, c0 + d:c0 + d + 1]
                h = ac(lambda e, out=out, sc=sc, d=d: e.activation(ZH[:, d, :], out[:, :], ACT.Copy, scale=sc), tok)
                free[b] = z_tok[d] = ve(lambda e, out=out, sc=sc, d=d: e.scalar_tensor_tensor(
                    out=ZL[:, d, :], in0=out[:, :], scalar=sc, in1=ZH[:, d, :].bitcast(F32), op0=ALU.mult,
                    op1=ALU.subtract), h)
            if g % 2 == 0:
                self.done_tok[n] = tok
        yield from self.out_proj(I["pool_w_out_2"][0], 8, ZH, ZL, z_tok, None, norm)

    def attn_inputs(self):
        w = self.I["attn_w_qkv_2"][0]
        t = self.t
        self.aq_tok, self.ak_tok, self.av_tok = [None] * 8, [None] * 8, [None] * 8
        used = [None, None]
        i = 0
        strided = lambda r: slice(r, S, 4)
        jobs = []
        for p in range(8):
            for dst, c0, sc, toks in ((t["aq"], 0, 64 ** -0.5, self.aq_tok), (t["ak"], 1024, 1.0, self.ak_tok)):
                def take(out, tok, i=i, dst=dst, sc=sc, toks=toks, p=p):
                    b, toks[p] = self.rope_pieces(out, dst[:, p, :], t["aT"][:, i % 2, :], t["cos2"][:, :],
                                                  t["sin2"][:, :], 32, sc, tok, self.tab_tok, used[i % 2])
                    used[i % 2] = toks[p]
                    return b
                i += 1
                jobs.append((w, c0 + 128 * p, take))
        def v_pair(p):
            def keep(out, tok, u):
                a = self.ac(lambda e: e.activation(
                    t["av"][:, 2 * u:2 * u + 2, p * 128:p * 128 + 256], out[:, :].rearrange("p (t c) -> p t c", t=2),
                    ACT.Copy), tok)
                self.av_tok[p] = self.av_tok[p + 1] = a
                return a
            yield from self.project_rows(w, 2048 + 128 * p, keep, None if p < 3 else strided)

        def v_one(p):
            T = t["aV"]
            got = []

            def keep(out, tok):
                a = self.ac(lambda e: e.activation(T[:, :], out[:, :], ACT.Copy), tok, self.v_used)
                got.append(a)
                return a
            yield from self.project(w, 2048 + 128 * p, keep)
            yield None
            b, fr = self.bank()
            out = self.mem["bank"][b]
            self.pe.wait(got[0], fr)
            for n in range(4):
                c = slice(n * 128, n * 128 + 128) if p < 3 else strided(n)
                x = self.pe(lambda e, n=n, c=c: e.transpose(out[:, n * 128:n * 128 + 128], T[:, c], t["ident"][:, :]))
            self.v_used = x
            self.free[b] = self.av_tok[p] = self.ac(lambda e: e.activation(
                t["av"][:, :, p * 128:p * 128 + 128], out[:, :].rearrange("p (t c) -> p t c", t=4), ACT.Copy), x)
            yield None

        self.v_used = None
        yield from self.projects(jobs[0:3])
        yield from self.project(*jobs[3])
        yield from self.project(*jobs[4])
        yield from v_pair(0)
        self.big_order = ["b1", "b2"]
        yield 16
        for p in range(2, 8):
            for job in jobs[max(5, 2 * p):2 * p + 2]:
                yield from self.project(*job)
            if p in (3, 5):
                yield from v_pair(p)
            elif p in (2, 7):
                yield from v_one(p)
            yield 8

    def attn_heads(self):
        t = self.t
        q, k, v, MO = (t[x] for x in ("aq", "ak", "av", "MO"))
        P, PT, M, NM, DEN, R = (t[x] for x in ("aP", "aPT", "aM", "aNM", "aDEN", "aR"))
        bank, free, pe, ve, ac = self.mem["bank"], self.free, self.pe, self.ve, self.ac
        steps = [(h, n) for h in range(16) for n in range(4)]
        st = {}
        self.mo_tok = [None] * 8

        def group(h):
            return 0 if h < 6 else 1 if h < 11 else 2

        def cols(h, n):
            if group(h) == 0:
                lo = max(0, n - 1)
                msk = t["window"][:, :] if n else t["window"][:, 128:256]
                return slice(n * 128, n * 128 + 128), slice(lo * 128, n * 128 + 128), list(range(lo, n + 1)), msk
            msk = t["causal"] if group(h) == 1 else t["dil"]
            return slice(n, S, 4), slice(n, S, 4), [n], msk[:, :]

        def score(m):
            h, n = steps[m]
            p, r = h // 2, slice(64 * (h % 2), 64 * (h % 2) + 64)
            b = f"s{m % 2}"
            i = m % 6
            qs, ks, tiles, msk = cols(h, n)
            w = 128 * len(tiles)
            pt = pe(lambda e: e.matmul(bank[b][:, 0:w], q[r, p, qs], k[r, p, ks], start=True, stop=True),
                    self.aq_tok[p], self.ak_tok[p], free[b])
            a = ve(lambda e: e.tensor_tensor_reduce(P[:, i, 0:w], bank[b][:, 0:w], msk, 1.0, -3e38, ALU.add, ALU.max,
                                                    M[:, m:m + 1]), pt, st.get(("t", m - 6)))
            free[b] = a
            a = ve(lambda e: e.tensor_scalar(NM[:, m:m + 1], M[:, m:m + 1], -1.0, None, ALU.mult), a)
            st["x", m] = ac(lambda e: e.activation(P[:, i, 0:w], P[:, i, 0:w], ACT.Exp, bias=NM[:, m:m + 1],
                                                   accum_out=DEN[:, m:m + 1]), a)

        def scale(m):
            i = m % 6
            w = 128 * len(cols(*steps[m])[2])
            d = ve(lambda e: e.reciprocal(R[:, m:m + 1], DEN[:, m:m + 1]), st["x", m])
            st["s", m] = ve(lambda e: e.tensor_scalar(P[:, i, 0:w], P[:, i, 0:w], R[:, m:m + 1], None, ALU.mult), d)
            self.lse_in = st["s", m]

        def turn(m):
            h, n = steps[m]
            b = f"t{m % 2}"
            i = m % 6
            nt = len(cols(h, n)[2])
            pe.wait(st["s", m], free[b])
            for j in range(nt):
                f = lambda e, j=j: e.transpose(bank[b][:, j * 128:j * 128 + 128], P[:, i, j * 128:j * 128 + 128],
                                               t["ident"][:, :])
                p = pe(f) if j == nt - 1 else pe.go(f)
            st["t", m] = p
            free[b] = st["p", m] = ac(lambda e: e.activation(PT[:, i, 0:128 * nt], bank[b][:, 0:128 * nt], ACT.Copy), p,
                                      st.get(("v", m - 6)))

        def value(m):
            h, n = steps[m]
            p, r = h // 2, slice(64 * (h % 2), 64 * (h % 2) + 64)
            i = m % 6
            ob = "o" if p % 2 == 0 else "b0"
            tiles = cols(h, n)[2]
            pe.wait(st["p", m], self.av_tok[p], free[ob] if n == 0 and h % 2 == 0 else None)
            for j, kt in enumerate(tiles):
                f = lambda e, j=j, kt=kt: e.matmul(bank[ob][r, n * 128:n * 128 + 128], v[:, kt, h * 64:h * 64 + 64],
                                                   PT[:, i, j * 128:j * 128 + 128], start=(j == 0),
                                                   stop=(j == len(tiles) - 1))
                pt = pe(f) if j == len(tiles) - 1 else pe.go(f)
            st["v", m] = pt
            if n == 3 and h % 2 == 1:
                src = bank[ob][:, :]
                if group(h) == 0:
                    f = lambda e: e.activation(MO[:, p, :], src, ACT.Copy)
                else:
                    f = lambda e: e.activation(MO[:, p, :].rearrange("p (l r) -> p r l", r=4),
                                               src.rearrange("p (r l) -> p r l", r=4), ACT.Copy)
                free[ob] = self.mo_tok[p] = ac(f, pt)

        N = len(steps)
        for m in range(N + 5):
            if m < N:
                score(m)
            if 1 <= m <= N:
                scale(m - 1)
            if 3 <= m < N + 3:
                turn(m - 3)
            if m >= 5:
                value(m - 5)
            yield None

    def attn_merge(self):
        t = self.t
        bank, free, pe, ve, ac = self.mem["bank"], self.free, self.pe, self.ve, self.ac
        M, DEN, W, V, LT, MO = (t[x] for x in ("aM", "aDEN", "aL", "aG", "aLT", "MO"))
        heads = ((0, 6), (6, 11), (11, 16))
        view = lambda x, h0, h1: x[:, 4 * h0:4 * h1].rearrange("p (h n) -> p n h", n=4)
        for g, (h0, h1) in enumerate(heads):
            m = ve(lambda e, g=g, h0=h0, h1=h1: e.tensor_reduce(V[:, 8 * g:8 * g + 4], view(M, h0, h1), AXX, ALU.max),
                   self.lse_in)
            for h in range(h0, h1):
                s = ve(lambda e, h=h, g=g: e.tensor_tensor(LT[:, 4 * h:4 * h + 4], M[:, 4 * h:4 * h + 4],
                                                           V[:, 8 * g:8 * g + 4], ALU.subtract), m)
        a = ac(lambda e: e.activation(LT[:, 0:64], LT[:, 0:64], ACT.Exp), s)
        l = ve(lambda e: e.tensor_tensor(LT[:, 0:64], LT[:, 0:64], DEN[:, 0:64], ALU.mult), a)
        for g, (h0, h1) in enumerate(heads):
            s = ve(lambda e, g=g, h0=h0, h1=h1: e.tensor_reduce(V[:, 8 * g + 4:8 * g + 8], view(LT, h0, h1), AXX,
                                                                ALU.add), l)
        pe.wait(s, free["t1"])
        for n in range(4):
            for r in range(4):
                p = pe(lambda e, n=n, r=r: e.matmul(bank["t1"][32 * n:32 * n + 32, r:r + 5:4], t["ident"][:, r:128:4],
                                                    V[:, n:n + 5:4], start=True, stop=True))
        free["t1"] = s = ve(lambda e: e.tensor_copy(V[:, 0:8], bank["t1"][:, 0:8]), p)
        m = ve(lambda e: e.tensor_tensor(W[:, 0:4], V[:, 0:4], V[:, 8:12], ALU.max), s)
        m = ve(lambda e: e.tensor_tensor(W[:, 0:4], W[:, 0:4], V[:, 16:20], ALU.max), m)
        al = lambda g: W[:, 4 * g + 4:4 * g + 8]
        for g in range(3):
            s = ve(lambda e, g=g: e.tensor_tensor(al(g), V[:, 8 * g:8 * g + 4], W[:, 0:4], ALU.subtract), m)
        a = ac(lambda e: e.activation(W[:, 4:16], W[:, 4:16], ACT.Exp), s)
        for g, (h0, h1) in enumerate(heads):
            s = ve(lambda e, g=g, k=1.0 / (h1 - h0): e.scalar_tensor_tensor(
                out=al(g), in0=al(g), scalar=k, in1=V[:, 8 * g + 4:8 * g + 8], op0=ALU.mult, op1=ALU.mult), a)
        s = ve(lambda e: e.tensor_tensor(W[:, 0:4], al(0), al(1), ALU.add), s)
        s = ve(lambda e: e.tensor_tensor(W[:, 0:4], W[:, 0:4], al(2), ALU.add), s)
        s = ve(lambda e: e.reciprocal(W[:, 0:4], W[:, 0:4]), s)
        for g in range(3):
            m = ve(lambda e, g=g: e.tensor_tensor(al(g), al(g), W[:, 0:4], ALU.mult), s)
        rows, row_tok = ("s0", "s1", "t0"), [None] * 3
        for g in range(3):
            row_tok[g] = self.spread(al(g), rows[g], m)
        G = (0, 0, 0, 1, 1, None, 2, 2)
        YH, YL = t["YH"], t["YL"]
        self.y_tok = [None] * 8
        for p in range(8):
            parts = [(slice(0, 128), G[p])] if G[p] is not None else [(slice(0, 64), 1), (slice(64, 128), 2)]
            for r, g in parts:
                x = MO[r, p, :].rearrange("p (l r) -> p r l", r=4)
                v = free[rows[g]] = ve(lambda e, r=r, g=g, x=x: e.scalar_tensor_tensor(
                    out=x, in0=x, scalar=3.0, in1=bank[rows[g]][r, :].rearrange("p (r l) -> p r l", r=4), op0=ALU.mult,
                    op1=ALU.mult), row_tok[g], self.mo_tok[p])
            h = ac(lambda e, p=p: e.activation(YH[:, p, :], MO[:, p, :], ACT.Copy), v)
            self.y_tok[p] = ve(lambda e, p=p: e.tensor_tensor(YL[:, p, :], MO[:, p, :], YH[:, p, :].bitcast(F32),
                                                              ALU.subtract), h)

    def finish(self):
        t = self.t
        bank, free, pe, ve, ac = self.mem["bank"], self.free, self.pe, self.ve, self.ac
        X, RS, OT, PAR = (t[x] for x in ("X", "RS", "OT", "PAR"))
        c0 = 512 + 32
        outs = []
        i = 0

        def store(tt):
            nonlocal i
            toks = []
            for u in range(2):
                b = ("o", "b0", "b1", "b2")[i % 4]
                pe.wait(free[b])
                for k in range(4 * u, 4 * u + 4):
                    f = lambda e, k=k, b=b: e.transpose(bank[b][:, (k % 4) * 128:(k % 4) * 128 + 128],
                                                        X[:, k, tt * 128:tt * 128 + 128], t["ident"][:, :])
                    p = pe(f, x[tt // 2][k])
                if i % 2:
                    free[b] = ac(lambda e, b=b, u=u: e.activation(OT[:, tt, u * 512:u * 512 + 512], bank[b][:, :],
                                                                  ACT.Copy), p)
                else:
                    free[b] = ve(lambda e, b=b, u=u: e.tensor_copy(OT[:, tt, u * 512:u * 512 + 512], bank[b][:, :]), p)
                toks.append(free[b])
                i += 1
            outs.append(self.out_flow[tt](self.out[0, tt * 128:tt * 128 + 128, :], OT[:, tt, :], toks))

        def scale(hf, r):
            b = ("t0", "s0")[hf]
            sp = self.spread(RS[:, 2 * hf:2 * hf + 2], b, r, 2)
            c = slice(256 * hf, 256 * hf + 256)
            return [ve(lambda e, k=k: e.scalar_tensor_tensor(
                out=X[:, k, c], in0=X[:, k, c], scalar=PAR[:, c0 + k:c0 + k + 1], in1=bank[b][:, 0:256],
                op0=ALU.mult, op1=ALU.mult), sp) for k in range(KD)]

        x = []
        r = self.sums(0)
        yield None
        x.append(scale(0, r))
        yield None
        yield None
        store(0)
        r = self.sums(1)
        store(1)
        x.append(scale(1, r))
        store(2)
        store(3)
        self.sp.wait(*outs)

    def run(self):
        I, t = self.I, self.t
        pe, ve, ac, po = self.pe, self.ve, self.ac, self.po
        bank, free = self.mem["bank"], self.free
        self.sq_used, self.nt_used, self.ss_used, self.late = [None] * 2, [None] * 4, None, None
        self.H2 = [None, None]
        self.gt_i, self.gt_used = 0, [None] * 4
        self.glr_used = self.ffr_used = self.aa_used = self.rvm_used = None
        T = self.mem["tables"]

        one = po(lambda e: e.memset(t["ones"][:, :], 1.0))
        one = po(lambda e: e.memset(t["eps"][:, :], EPS))
        for lane in (pe, ve, ac):
            lane.wait(one)
        XS, PST = t["XS"], t["PST"]
        par = [self.load(PST[:, :, :], I["params"].rearrange("j r c -> r j c"))]
        for l in range(DEPTH):
            par.append(self.load(t["BF"][96:100, l:l + 1], I["b_fox_f"][l].rearrange("(h o) -> h o", o=1)))
        con = self.load(t["CON"][:, :], T["con"])
        for name in ("ident", "causal"):
            r = ac(lambda e, name=name: e.activation(t[name + "R"][:, :], t[name][:, :], ACT.Copy), con)
        pe.wait(r)
        for j, n in ((4, 56), (0, 117), (1, 66), (2, 117), (3, 66)):
            b = ("s0", "s1")[j % 2]
            p = pe(lambda e, j=j, n=n, b=b: e.transpose(bank[b][:, 0:n], PST[0:n, j, :], t["ident"][0:n, 0:n]), free[b],
                   par, con)
            free[b] = self.par_tok = ve(lambda e, j=j, n=n, b=b: e.tensor_copy(t["PAR"][:, j * 128:j * 128 + n],
                                                                               bank[b][:, 0:n]), p, con)
            if j == 4:
                self.ca_tok = ac(lambda e: e.activation(t["CA"][:, :], t["PAR"][:, 512 + 48:512 + 56], ACT.Silu),
                                 self.par_tok)

        def mods(l, which):
            c = self.pcol(l, "norm1_g" if which == 0 else "norm2_g")
            A = t["NA"][:, 2 * l + which, :]
            MOD = t["MOD"]
            s = 24 * which
            return ve(lambda e: e.scalar_tensor_tensor(out=A, in0=MOD[:, l, s + 8:s + 16], scalar=1.0,
                                                       in1=t["PAR"][:, c:c + 8], op0=ALU.add, op1=ALU.mult),
                      self.mod_tok), A, MOD[:, l, s:s + 8]

        def turn_x(ks):
            for k in ks:
                b = ("s0", "s1", "o", "t0")[k % 4]
                pe.wait(free[b])
                for tt in range(4):
                    p = pe(lambda e, k=k, tt=tt, b=b: e.transpose(
                        bank[b][:, tt * 128:tt * 128 + 128], XS[:, tt, k * 128:k * 128 + 128], t["ident"][:, :]),
                        x_in[tt])
                free[b] = ac(lambda e, k=k, b=b: e.activation(t["X"][:, k, :], bank[b][:, :], ACT.Copy), p)
                self.square(k, free[b], slice(0, S))

        rows = [self.ada_row(0, q) for q in range(4)]
        next(rows[0])
        x_in = [self.load(XS[:, tt, :], I["x"][0, tt * 128:tt * 128 + 128, :]) for tt in range(4)]
        for q in range(4):
            for _ in range(5 if q else 4):
                next(rows[q])
            if q in (1, 2):
                turn_x(range(4 * q - 4, 4 * q))
            drain(rows[q])
        ac.go(lambda e: e.activation(t["RS"][:, 8:9], t["eps"][:, 0:1], ACT.Sqrt))
        tok, A, B = mods(0, 0)
        self.norm = self.x_norm(A, B, tok)
        for _ in range(3):
            next(self.norm)
        self.half_left = False
        for l in range(DEPTH):
            self.l = l
            w = I["w_in"][l]
            prev = self.last if l else None
            tabs = [self.load(t["cos1"][:, :], T["cos1"], prev), self.load(t["sin1"][:, :], T["sin1"], prev)]
            self.dec_tok = self.load(t["decay"][:, :], T["decay"], prev)
            self.wa_tok = [self.load(t["WA"][0:16, 0:256], I["w_gla_a2"][l], self.glr_used),
                           self.load(t["WA"][16:17, 0:256], I["b_gla_a"][l].rearrange("(o c) -> o c", o=1), self.glr_used)]
            self.rq_tok, self.rk_tok, self.rv_tok = [None] * 4, [None] * 4, []
            used = [None, None]
            i = 0
            jobs = []
            for h in range(4):
                for dst, c0, toks in ((t["rq"], 0, self.rq_tok), (t["rk"], 512, self.rk_tok)):
                    def take(out, tok, i=i, dst=dst, toks=toks, h=h):
                        b, toks[h] = self.rope_pieces(out, dst[:, h, :], t["rT"][:, i % 2, :], t["cos1"][:, :],
                                                      t["sin1"][:, :], 64, 1.0, tok, tabs, used[i % 2])
                        used[i % 2] = toks[h]
                        return b
                    i += 1
                    jobs.append((w, c0 + 128 * h, take))
            drain(self.projects(jobs))
            for c in range(2):
                def keep(out, tok, u, c=c):
                    N = t["RVM"][:, 8 * c + 4 * u:8 * c + 4 * u + 4]
                    m = ve(lambda e: e.tensor_reduce(N, out[:, :].rearrange("p (n c) -> p n c", c=128), AXX, ALU.add),
                           tok, self.rvm_used)
                    m = ve(lambda e: e.tensor_scalar(N, N, -1.0 / 128, None, ALU.mult), m)
                    for j in range(4):
                        d = t["rv"][:, 2 * u + j // 2, c * 256 + 128 * (j % 2):c * 256 + 128 * (j % 2) + 128]
                        k = ac(lambda e, j=j, d=d: e.activation(d, out[:, 128 * j:128 * j + 128], ACT.Identity,
                                                                bias=N[:, j:j + 1]), m)
                    self.rv_tok.append(k)
                    self.rvm_used = k
                    return k
                drain(self.project_rows(w, 1024 + 256 * c, keep))
            ada = iter(())
            if l == 0:
                ada = (y for q in range(4, 12) for y in self.ada(0, q))
            self.big_order = ["b0", "b1"]
            weave(self.ret_attention(), beside(self.fox_inputs(w), ada, 16), 1)
            self.big_order = ["b0", "b1", "b2"]
            fill = self.gla_inputs(w)

            weave(self.fox_norm(), fill, 1, False)
            weave(self.fox_attention(), fill, 1, False)
            drain(fill)
            weave(self.gla_attention(), beside(self.gated(w, 1536, t["RO"], lambda: self.ro_tok, t["ErH"], t["ErL"]), ada, 8), 1)
            self.er_tok = self.gated_tok
            drain(beside(self.gated(w, 3088, t["GO"], lambda: self.go_tok, t["EgH"], t["EgL"]), ada, 8))
            self.eg_tok = self.gated_tok
            self.big_order = ["b0", "b1", "b2", "o"]
            drain(beside(self.mixing(l), ada, 18))
            self.mod_all = self.mod_tok
            pe.wait(self.mod_tok)
            ve.wait(self.mod_tok)
            tok, A, B = mods(l, 1)
            drain(self.out_proj(I["w_o"][l], 8, t["MH"], t["ML"], self.mix_tok, t["MOD"][:, l, 16:24],
                                self.x_norm(A, B, tok)))
            c = self.pcol(l, "w_conv")
            cb = self.pcol(l, "b_conv")
            conv = (lambda j, f, c=c: t["PAR"][:, c + 22 * j + f:c + 22 * j + f + 1],
                    lambda f, cb=cb: t["PAR"][:, cb + f:cb + f + 1])

            def fill_next(l=l, ada=ada):
                yield from ada
                if l + 1 < DEPTH:
                    for q in range(12):
                        yield from self.ada(l + 1, q)
            fill = fill_next()
            weave(self.ffn_up(I["w_up"][l], 0, I["w_up"][l], FF, conv), fill, 1, False)
            if l + 1 < DEPTH:
                tok, A, B = mods(l + 1, 0)
                norm = self.x_norm(A, B, tok)
            else:
                norm = self.x_norm(t["PAR"][:, 512:520], None, self.par_tok)
            weave(self.out_proj(I["w_down"][l], KF, t["FH"], t["FL"], self.ff_tok, t["MOD"][:, l, 40:48], norm), fill)
            ve.wait(self.mod_tok)
            self.big_order = ["b0", "b1", "b2"]
        self.big_order = ["b0", "b1", "b2", "o"]
        drain(self.pool_mixer(self.x_norm(t["PAR"][:, 528:536], None, self.par_tok)))
        drain(self.ffn_up(I["ffn_w_gate_2"][0], 0, I["ffn_w_up_2"][0], 0, None))
        drain(self.out_proj(I["ffn_w_down_2"][0], KF, t["FH"], t["FL"], self.ff_tok, None,
                            self.x_norm(t["PAR"][:, 520:528], None, self.par_tok)))
        prev = self.last
        self.tab_tok = [self.load(t["cos2"][:, :], T["cos2"], prev), self.load(t["sin2"][:, :], T["sin2"], prev)]
        heads = self.attn_heads()
        ready = new = 0
        for piece in self.attn_inputs():
            for _ in range(min(ready, PACE)):
                ready -= 1
                next(heads)
            ready, new = ready + new, 0 if piece in (None, BUSY) else piece
        drain(heads)
        self.attn_merge()
        self.big_order = ["b0", "b1", "b2", "o"]
        drain(self.out_proj(I["attn_w_out_2"][0], 8, t["YH"], t["YL"], self.y_tok, None,
                            self.x_norm(t["PAR"][:, 536:544], None, self.par_tok)))
        drain(self.ffn_up(I["ffn_w_gate_2"][1], 0, I["ffn_w_up_2"][1], 0, None))
        last = self.finish()
        drain(self.out_proj(I["ffn_w_down_2"][1], KF, t["FH"], t["FL"], self.ff_tok, None, last))
        drain(last)


def places(nc):
    with ExitStack() as ctx:
        base = (nc.sbuf_base + 63) // 64 * 64
        TB = S * 4
        ctx.enter_context(nc.sbuf_tensor("arena", [128, (nc.sbuf_usable_end - base) // 4 - 64], F32))
        at = [base]
        t = {}

        def fixed(name, shape, dt=F32):
            n = int(np.prod(shape[1:])) * 4
            t[name] = nc.alloc_sbuf_tensor_at(name, shape, dt, offset=at[0])
            at[0] += (n + 31) // 32 * 32

        fixed("X", [128, 8, S])
        t["OT"] = nc.alloc_sbuf_tensor_at("OT", [128, 4, D], F32, offset=at[0])
        fixed("HH", [128, 8, S], F32R)
        fixed("HL", [128, 8, S], F32R)
        raw = nc.alloc_sbuf_tensor_at("raw", [128, NSLOT, 1024], F32, offset=at[0])
        fixed("lo", [128, NSLOT, 1024], F32R)
        fixed("hi", [128, NSLOT, 1024], F32R)
        fixed("CON", [128, CON_W])
        c = 0
        for name, n in CON:
            t[name] = t["CON"][:, c:c + n]
            c += n
        t["causal"] = t["window"][:, 128:256]
        for name, n in (("PAR", 640), ("ones", 2), ("eps", 2),
                        ("CA", 8), ("RS", 16), ("RS2", 32), ("GQ", 2), ("BF", 2), ("foxM", 16), ("foxR", 16),
                        ("AD", 16), ("RVM", 16), ("aM", 64), ("aNM", 64), ("aDEN", 64), ("aR", 64), ("aL", 64)):
            fixed(name, [128, n])
        fixed("WA", [128, 256])
        fixed("identR", [128, 128], F32R)
        fixed("causalR", [128, 128], F32R)
        t["one"], t["aLT"] = t["ones"], t["aNM"]
        fixed("MOD", [128, 2, 48])
        fixed("NA", [128, 4, 8])
        fixed("aG", [128, 24])
        fixed("AA", [128, S])
        big = at[0]
        assert big + 49 * TB <= nc.sbuf_usable_end, big + 49 * TB - nc.sbuf_usable_end

        def area(name, tile, shape, dt=F32):
            t[name] = nc.alloc_sbuf_tensor_at(name, shape, dt, offset=big + int(tile * TB))
            assert big + int(tile * TB) + int(np.prod(shape[1:])) * 4 <= big + 49 * TB, name

        area("SQ", 44, [128, 2, S])
        area("NT", 46, [128, 4, 256])
        area("SS", 48, [128, S])
        area("XS", 0, [128, 4, D])
        area("PST", 20, [128, 5, 128])
        area("rq", 0, [128, 4, S])
        area("rk", 4, [128, 4, S])
        area("rv", 8, [128, 4, S])
        area("fq", 12, [128, 4, S])
        area("fk", 16, [128, 4, S])
        area("fv", 20, [128, 4, S])
        area("RO", 24, [128, 4, S])
        area("EfH", 28, [128, 4, S], F32R)
        area("EfL", 32, [128, 4, S], F32R)
        area("cos1", 36, [128, S])
        area("sin1", 37, [128, S])
        area("decay", 38, [128, 4 * S])
        area("rT", 28, [128, 2, S])
        area("retP", 42, [128, 4, S])
        area("retS", 30, [128, 2, S])
        area("foxS", 32, [128, 2, S])
        area("GLR", 46, [128, S])
        area("FFR", 47, [128, S])
        area("FFT", 48, [128, S])
        area("foxP", 36, [128, 3, S])
        area("foxT", 39, [128, 7 * S])
        area("foxC0", 31, [128, S])
        area("foxC1", 35, [128, S])
        area("gk", 0, [128, 4, 256])
        area("gv", 2, [128, 4, S])
        area("gq", 6, [128, 2, S])
        area("SA", 8, [128, 2, 8, 128])
        area("GO", 20, [128, 4, S])
        area("ErH", 12, [128, 4, S], F32R)
        area("ErL", 16, [128, 4, S], F32R)
        area("EgH", 0, [128, 4, S], F32R)
        area("EgL", 4, [128, 4, S], F32R)
        area("LA", 8, [128, 2, S])
        area("TA", 10, [128, 2, S])
        area("ED", 41, [128, 2, S])
        area("glaS", 43, [128, 2, S])
        area("GT", 45, [128, 4, S])
        area("MH", 36, [128, 8, S], F32R)
        area("ML", 20, [128, 8, S], F32R)
        area("SG", 8, [128, 2, S])
        area("MX", 10, [128, 2, S])
        area("FH", 0, [128, KF, S], F32R)
        area("FL", KF, [128, KF, S], F32R)
        area("CB", 44, [128, 2, S])
        area("PH", 0, [128, 8, S], F32R)
        area("PL", 8, [128, 8, S], F32R)
        area("ZH", 16, [128, 8, S], F32R)
        area("ZL", 24, [128, 8, S], F32R)
        area("U", 38, [128, 4, S])
        area("W1", 34, [128, 2, S])
        area("W2", 36, [128, 2, S])
        area("aq", 0, [128, 8, S])
        area("ak", 8, [128, 8, S])
        area("av", 16, [128, 4, D])
        area("MO", 24, [128, 8, S])
        area("cos2", 32, [128, S])
        area("sin2", 33, [128, S])
        area("aT", 34, [128, 2, S])
        area("aV", 42, [128, S])
        area("aP", 36, [128, 6, 256])
        area("aPT", 39, [128, 6, 256])
        area("YH", 0, [128, 8, S], F32R)
        area("YL", 8, [128, 8, S], F32R)

        bank = {b: ctx.enter_context(nc.psum_tensor(b, [128, S], F32))
                for b in ("b0", "b1", "b2", "s0", "s1", "t0", "t1", "o")}
        return ctx.pop_all(), t, raw, bank


def build(nc, I, T, out):
    stack, t, raw, bank = places(nc)
    with stack as ctx:
        mem = {"raw": raw, "hi": t["hi"], "lo": t["lo"], "t": t, "bank": bank, "tables": T}

        def sem(name):
            return ctx.enter_context(nc.semaphore(name))

        sems = (sem("s_pe"), sem("s_ve"), sem("s_ac"), sem("s_po"), [sem(f"s_ring{i}") for i in range(NSLOT + 2)],
                [sem(f"s_misc{i}") for i in range(16)], [sem(f"s_out{i}") for i in range(4)])
        draft = Program(nc, I, out, sems, mem, None)
        draft.run()
        p = Program(nc, I, out, sems, mem, draft.descs)
        p.run()
        block = ctx.enter_context(nc.Block())

        @block.sync
        def _(e):
            p.sp.emit(e)

        @block.tensor
        def _(e):
            p.pe.emit(e)

        @block.vector
        def _(e):
            p.ve.emit(e)

        @block.scalar
        def _(e):
            p.ac.emit(e)

        @block.gpsimd
        def _(e):
            p.po.emit(e)


_INS = ['x', 'w_ada', 'w_in', 'w_gla_a2', 'b_gla_a', 'b_fox_f', 'w_br', 'w_mg', 'w_o', 'w_up', 'w_down', 'pool_w_in_2',
        'pool_w_group_2', 'pool_w_out_2', 'attn_w_qkv_2', 'attn_w_out_2', 'ffn_w_gate_2', 'ffn_w_up_2', 'ffn_w_down_2']
_OUTS = [((1, 512, 1024), 'float32')]


def kernel(**inputs):
    import numpy as _np
    import concourse.bacc as _bacc
    from concourse import mybir as _mybir
    from concourse.bass_utils import run_bass_kernel_spmd as _run

    nc = _bacc.Bacc("TRN2", target_bir_lowering=False, num_devices=1)
    arrays, ins, tabs = {}, {}, {}
    for name in _INS:
        a = _np.ascontiguousarray(inputs[name])
        arrays[f"in_{name}_dram"] = a
        ins[name] = nc.dram_tensor(f"in_{name}_dram", a.shape, _mybir.dt.from_np(a.dtype), kind="ExternalInput").ap()
    rows = _np.zeros((5, 128, 128), _np.float32)
    parts = [(2 * l, [inputs[name][l] for name, _ in COL_A]) for l in range(DEPTH)]
    parts += [(2 * l + 1, [inputs["w_conv"][l]]) for l in range(DEPTH)]
    parts.append((4, [inputs[name] for name in ("norm_mix_2", "norm_ffn_2", "norm_final_2", "pool_scale_2", "c")]))
    for j, part in parts:
        flat = _np.concatenate([_np.asarray(a).reshape(-1, 128) for a in part])
        rows[j, :flat.shape[0]] = flat
    arrays["in_params_dram"] = rows
    ins["params"] = nc.dram_tensor("in_params_dram", rows.shape, _mybir.dt.float32, kind="ExternalInput").ap()
    for name, a in tables().items():
        arrays[f"tab_{name}_dram"] = a
        tabs[name] = nc.dram_tensor(f"tab_{name}_dram", a.shape, _mybir.dt.from_np(a.dtype), kind="ExternalInput").ap()
    shape, dtype = _OUTS[0]
    out = nc.dram_tensor("out_0_dram", shape, _mybir.dt.from_np(_np.dtype(dtype)), kind="ExternalOutput").ap()
    build(nc, ins, tabs, out)
    r = _run(nc, [arrays], core_ids=[0])
    return r.results[0]["out_0_dram"]
```
